# Optimizing a Trainium2 kernel written in Bass

```python
import jax, jax.numpy as jnp
from jax import lax
import numpy as np
import math

D_MODEL = 1024
BATCH = 1
SEQ = 256
DEPTH = 2

N_BRANCH = 4
MIX_W = D_MODEL // N_BRANCH
HEAD_DIM = 64
CONV_A_K = 31
NA_HEADS = MIX_W // HEAD_DIM
NA_ROWS = 8
NA_COLS = 16
GRID_W = 64
DIL_HEADS = MIX_W // HEAD_DIM
DIL_PAIRS = ((128, 1), (512, 4), (2048, 16))
SWA_Q_HEADS = MIX_W // HEAD_DIM
SWA_KV_HEADS = SWA_Q_HEADS // 2
SWA_WINDOW = 128
Q_BLOCK = 128
ROPE_THETA = 500000.0
ROPE_DIMS = HEAD_DIM // 4
D_FF = 2816
FFN_CONV_K = 3
EPS = 1e-6
NEG_INF = -1e30

IN_SIZES = (
    N_BRANCH * D_MODEL,
    2 * MIX_W,
    3 * NA_HEADS * HEAD_DIM,
    3 * DIL_HEADS * HEAD_DIM,
    SWA_Q_HEADS * HEAD_DIM,
    2 * SWA_KV_HEADS * HEAD_DIM,
)
N_IN = sum(IN_SIZES)
IN_SPLITS = [int(s) for s in np.cumsum(IN_SIZES)[:-1]]


def _rmsnorm(x, g):
    xf = x.astype(jnp.float32)
    y = xf * lax.rsqrt(jnp.mean(jnp.square(xf), axis=-1, keepdims=True) + EPS)
    return (y * g.astype(jnp.float32)).astype(x.dtype)

def _layernorm(x, g, b):
    xf = x.astype(jnp.float32)
    mu = jnp.mean(xf, axis=-1, keepdims=True)
    var = jnp.mean(jnp.square(xf - mu), axis=-1, keepdims=True)
    y = (xf - mu) * lax.rsqrt(var + EPS)
    return (y * g.astype(jnp.float32) + b.astype(jnp.float32)).astype(x.dtype)

def _rope_tables(seq):
    pos = jnp.arange(seq, dtype=jnp.float32)
    inv = ROPE_THETA ** (-jnp.arange(0, ROPE_DIMS, 2, dtype=jnp.float32) / ROPE_DIMS)
    ang = pos[:, None] * inv[None, :]
    return jnp.cos(ang), jnp.sin(ang)

def _partial_rope(x, cos, sin):
    half = ROPE_DIMS // 2
    xf = x.astype(jnp.float32)
    x1, x2, rest = xf[..., :half], xf[..., half:ROPE_DIMS], xf[..., ROPE_DIMS:]
    c, s = cos[None, :, None, :], sin[None, :, None, :]
    out = jnp.concatenate([x1 * c - x2 * s, x2 * c + x1 * s, rest], axis=-1)
    return out.astype(x.dtype)

def _depthwise_conv(u, w, b):
    k, ch = w.shape
    p = (k - 1) // 2
    y = lax.conv_general_dilated(u, w[:, None, :].astype(u.dtype), (1,), [(p, p)],
                                 dimension_numbers=('NWC', 'WIO', 'NWC'),
                                 feature_group_count=ch)
    return y + b.astype(u.dtype)

def _conformer_conv(a_in, conv_w, conv_b, ln_g, ln_b):
    a, g = jnp.split(a_in, 2, axis=-1)
    u = a * jax.nn.sigmoid(g)
    u = _depthwise_conv(u, conv_w, conv_b)
    u = _layernorm(u, ln_g, ln_b)
    return jax.nn.silu(u)

def _neighbourhood_attn(q, k, v, rpb):
    bsz, seq, heads, dh = q.shape
    rows = seq // GRID_W
    kr = min(NA_ROWS, rows)
    kc = min(NA_COLS, GRID_W)
    qg = q.reshape(bsz, rows, GRID_W, heads, dh)
    kg = k.reshape(bsz, rows, GRID_W, heads, dh)
    vg = v.reshape(bsz, rows, GRID_W, heads, dh)
    col = np.arange(GRID_W)
    col_start = np.clip(col - kc // 2, 0, GRID_W - kc)
    col_idx = col_start[:, None] + np.arange(kc)[None, :]
    dc = col_idx - col[:, None] + (NA_COLS - 1)
    bias_c = rpb[:, :, dc].astype(jnp.float32)
    scale = dh ** -0.5

    def row_block(r):
        row_start = jnp.clip(r - kr // 2, 0, rows - kr)
        row_idx = row_start + jnp.arange(kr)
        dr = row_idx - r + (NA_ROWS - 1)
        q_r = lax.dynamic_index_in_dim(qg, r, axis=1, keepdims=False)
        k_r = jnp.take(kg, row_idx, axis=1)[:, :, col_idx]
        v_r = jnp.take(vg, row_idx, axis=1)[:, :, col_idx]
        s = jnp.einsum('bwhd,brwkhd->bhwrk', q_r, k_r).astype(jnp.float32) * scale
        bias = jnp.transpose(jnp.take(bias_c, dr, axis=1), (0, 2, 1, 3))
        s = s + bias[None]
        p = jax.nn.softmax(s.reshape(bsz, heads, GRID_W, kr * kc), axis=-1)
        p = p.reshape(bsz, heads, GRID_W, kr, kc).astype(v.dtype)
        return jnp.einsum('bhwrk,brwkhd->bwhd', p, v_r)

    out = lax.map(row_block, jnp.arange(rows))
    return jnp.transpose(out, (1, 0, 2, 3, 4)).reshape(bsz, seq, heads * dh)

def _dilated_group(q, k, v, dil, n_side):
    bsz, seq, heads, dh = q.shape
    offs = dil * np.arange(-n_side, n_side + 1)
    scale = dh ** -0.5

    def block(i):
        start = i * Q_BLOCK
        kpos = start + jnp.arange(Q_BLOCK)[:, None] + offs[None, :]
        valid = (kpos >= 0) & (kpos < seq)
        kidx = jnp.clip(kpos, 0, seq - 1)
        q_b = lax.dynamic_slice_in_dim(q, start, Q_BLOCK, axis=1)
        k_b = jnp.take(k, kidx, axis=1)
        v_b = jnp.take(v, kidx, axis=1)
        s = jnp.einsum('bqhd,bqjhd->bhqj', q_b, k_b).astype(jnp.float32) * scale
        s = jnp.where(valid[None, None], s, NEG_INF)
        m = jnp.max(s, axis=-1, keepdims=True)
        p = jnp.exp(s - m)
        l = jnp.sum(p, axis=-1)
        o = jnp.einsum('bhqj,bqjhd->bqhd', p, v_b.astype(jnp.float32))
        o = o / jnp.transpose(l, (0, 2, 1))[..., None]
        lse = jnp.transpose(m[..., 0] + jnp.log(l), (0, 2, 1))
        return o, lse

    o, lse = lax.map(block, jnp.arange(seq // Q_BLOCK))
    o = jnp.transpose(o, (1, 0, 2, 3, 4)).reshape(bsz, seq, heads, dh)
    lse = jnp.transpose(lse, (1, 0, 2, 3)).reshape(bsz, seq, heads)
    return o, lse

def _dilated_attn(q, k, v):
    bsz, seq, heads, dh = q.shape
    outs, lses = [], []
    for window, dil in DIL_PAIRS:
        o, lse = _dilated_group(q, k, v, dil, window // (2 * dil))
        outs.append(o)
        lses.append(lse)
    wts = jax.nn.softmax(jnp.stack(lses, axis=0), axis=0)
    out = jnp.sum(wts[..., None] * jnp.stack(outs, axis=0), axis=0)
    return out.reshape(bsz, seq, heads * dh).astype(q.dtype)

def _window_gqa_sink(q, k, v, sink):
    bsz, seq, hq, dh = q.shape
    hkv = k.shape[2]
    grp = hq // hkv
    pad = SWA_WINDOW
    klen = Q_BLOCK + 2 * pad
    kp = jnp.pad(k, ((0, 0), (pad, pad), (0, 0), (0, 0)))
    vp = jnp.pad(v, ((0, 0), (pad, pad), (0, 0), (0, 0)))
    qg = q.reshape(bsz, seq, hkv, grp, dh)
    sink_g = sink.astype(jnp.float32).reshape(hkv, grp)[None, :, :, None]
    scale = dh ** -0.5

    def block(i):
        start = i * Q_BLOCK
        q_b = lax.dynamic_slice_in_dim(qg, start, Q_BLOCK, axis=1)
        k_b = lax.dynamic_slice_in_dim(kp, start, klen, axis=1)
        v_b = lax.dynamic_slice_in_dim(vp, start, klen, axis=1)
        qpos = start + jnp.arange(Q_BLOCK)
        kpos = start - pad + jnp.arange(klen)
        valid = (jnp.abs(qpos[:, None] - kpos[None, :]) <= SWA_WINDOW) & (kpos >= 0)[None] & (kpos < seq)[None]
        s = jnp.einsum('bqkgd,bskd->bkgqs', q_b, k_b).astype(jnp.float32) * scale
        s = jnp.where(valid[None, None, None], s, NEG_INF)
        m = jnp.maximum(jnp.max(s, axis=-1), sink_g)
        p = jnp.exp(s - m[..., None])
        denom = jnp.sum(p, axis=-1) + jnp.exp(sink_g - m)
        o = jnp.einsum('bkgqs,bskd->bqkgd', p, v_b.astype(jnp.float32))
        o = o / jnp.transpose(denom, (0, 3, 1, 2))[..., None]
        return o.reshape(bsz, Q_BLOCK, hq * dh).astype(q.dtype)

    out = lax.map(block, jnp.arange(seq // Q_BLOCK))
    return jnp.transpose(out, (1, 0, 2, 3)).reshape(bsz, seq, hq * dh)

def _conv_ffn(h, w_up, conv_w, conv_b, w_down):
    u = _depthwise_conv(h @ w_up, conv_w, conv_b)
    gate, up = jnp.split(u, 2, axis=-1)
    return (jax.nn.silu(gate) * up) @ w_down

def first_inputs(seed: int = 0) -> dict:
    key = jax.random.key(seed)
    ks = jax.random.split(key, 24)
    f32 = jnp.float32

    def nrm(k, shape, scale):
        return jax.random.normal(k, shape, f32) * scale

    def gain(k, shape):
        return 1.0 + 0.02 * jax.random.normal(k, shape, f32)

    return {
        'x': nrm(ks[0], (BATCH, SEQ, D_MODEL), 1.0),
        'g_mix': gain(ks[1], (DEPTH, D_MODEL)),
        'w_in': nrm(ks[2], (DEPTH, D_MODEL, N_IN), D_MODEL ** -0.5),
        'gate_b': nrm(ks[3], (DEPTH, N_BRANCH, D_MODEL), 0.01),
        'a_conv_w': nrm(ks[4], (DEPTH, CONV_A_K, MIX_W), CONV_A_K ** -0.5),
        'a_conv_b': nrm(ks[5], (DEPTH, MIX_W), 0.01),
        'a_ln_g': gain(ks[6], (DEPTH, MIX_W)),
        'a_ln_b': nrm(ks[7], (DEPTH, MIX_W), 0.01),
        'na_qn': gain(ks[8], (DEPTH, HEAD_DIM)),
        'na_kn': gain(ks[9], (DEPTH, HEAD_DIM)),
        'na_rpb': nrm(ks[10], (DEPTH, NA_HEADS, 2 * NA_ROWS - 1, 2 * NA_COLS - 1), 0.1),
        'dil_qn': gain(ks[11], (DEPTH, HEAD_DIM)),
        'dil_kn': gain(ks[12], (DEPTH, HEAD_DIM)),
        'swa_qn': gain(ks[13], (DEPTH, HEAD_DIM)),
        'swa_kn': gain(ks[14], (DEPTH, HEAD_DIM)),
        'swa_sink': nrm(ks[15], (DEPTH, SWA_Q_HEADS), 1.0),
        'w_branch': nrm(ks[16], (DEPTH, N_BRANCH, MIX_W, D_MODEL), MIX_W ** -0.5),
        'w_out': nrm(ks[17], (DEPTH, D_MODEL, D_MODEL), D_MODEL ** -0.5),
        'g_ffn': gain(ks[18], (DEPTH, D_MODEL)),
        'w_up': nrm(ks[19], (DEPTH, D_MODEL, 2 * D_FF), D_MODEL ** -0.5),
        'ffn_conv_w': nrm(ks[20], (DEPTH, FFN_CONV_K, 2 * D_FF), FFN_CONV_K ** -0.5),
        'ffn_conv_b': nrm(ks[21], (DEPTH, 2 * D_FF), 0.01),
        'w_down': nrm(ks[22], (DEPTH, D_FF, D_MODEL), D_FF ** -0.5),
    }

def first_block(x, g_mix, w_in, gate_b, a_conv_w, a_conv_b, a_ln_g, a_ln_b,
              na_qn, na_kn, na_rpb, dil_qn, dil_kn, swa_qn, swa_kn, swa_sink,
              w_branch, w_out, g_ffn, w_up, ffn_conv_w, ffn_conv_b, w_down):
    bsz, seq, _ = x.shape
    cos, sin = _rope_tables(seq)
    for l in range(DEPTH):
        h = _rmsnorm(x, g_mix[l])
        proj = h @ w_in[l]
        gate_pre, a_in, na_qkv, dil_qkv, swa_q, swa_kv = jnp.split(proj, IN_SPLITS, axis=-1)

        y_a = _conformer_conv(a_in, a_conv_w[l], a_conv_b[l], a_ln_g[l], a_ln_b[l])

        bq, bk, bv = [t.reshape(bsz, seq, NA_HEADS, HEAD_DIM) for t in jnp.split(na_qkv, 3, axis=-1)]
        y_b = _neighbourhood_attn(_rmsnorm(bq, na_qn[l]), _rmsnorm(bk, na_kn[l]), bv, na_rpb[l])

        cq, ck, cv = [t.reshape(bsz, seq, DIL_HEADS, HEAD_DIM) for t in jnp.split(dil_qkv, 3, axis=-1)]
        cq = _partial_rope(_rmsnorm(cq, dil_qn[l]), cos, sin)
        ck = _partial_rope(_rmsnorm(ck, dil_kn[l]), cos, sin)
        y_c = _dilated_attn(cq, ck, cv)

        dq = swa_q.reshape(bsz, seq, SWA_Q_HEADS, HEAD_DIM)
        dk, dv = [t.reshape(bsz, seq, SWA_KV_HEADS, HEAD_DIM) for t in jnp.split(swa_kv, 2, axis=-1)]
        dq = _partial_rope(_rmsnorm(dq, swa_qn[l]), cos, sin)
        dk = _partial_rope(_rmsnorm(dk, swa_kn[l]), cos, sin)
        y_d = _window_gqa_sink(dq, dk, dv, swa_sink[l])

        ys = jnp.stack([y_a, y_b, y_c, y_d], axis=2)
        branch = jnp.einsum('bsnc,ncd->bsnd', ys, w_branch[l])
        gates = jax.nn.sigmoid(gate_pre.reshape(bsz, seq, N_BRANCH, D_MODEL) + gate_b[l])
        mixed = jnp.sum(gates * branch, axis=2)
        x = x + mixed @ w_out[l]

        x = x + _conv_ffn(_rmsnorm(x, g_ffn[l]), w_up[l], ffn_conv_w[l], ffn_conv_b[l], w_down[l])
    return x


DEPTH_2 = 1

CHUNK = 128
SSD_INNER = D_MODEL
SSD_HEADDIM = 64
SSD_HEADS = SSD_INNER // SSD_HEADDIM
SSD_GROUPS = 2
SSD_STATE = 128
SSD_CONV = 4
SSD_CONV_DIM = SSD_INNER + 2 * SSD_GROUPS * SSD_STATE
LRU_WIDTH = D_MODEL
LRU_BLOCKS = 4
LRU_BLOCK = LRU_WIDTH // LRU_BLOCKS
LRU_CONV = 4
LRU_C = 8.0
RET_HEADS = 4
RET_QK_DIM = D_MODEL // (2 * RET_HEADS)
RET_V_DIM = D_MODEL // RET_HEADS
RET_WIDTH = RET_HEADS * RET_V_DIM
ROPE_BASE = 10000.0
FFN_DIM = 3 * D_MODEL
FFN_CONV = 3
N_BRANCHES = 3
IN_SPLITS_2 = (SSD_INNER, SSD_CONV_DIM, SSD_HEADS, LRU_WIDTH, LRU_WIDTH,
             RET_HEADS * RET_QK_DIM, RET_HEADS * RET_QK_DIM, RET_WIDTH, RET_WIDTH,
             N_BRANCHES * D_MODEL)
IN_PROJ_DIM = sum(IN_SPLITS_2)


def rmsnorm(x, g):
    x32 = x.astype(jnp.float32)
    y = x32 * lax.rsqrt(jnp.mean(x32 * x32, axis=-1, keepdims=True) + EPS)
    return (y * g.astype(jnp.float32)).astype(x.dtype)

def causal_dwconv(x, w, b):
    k = w.shape[0]
    y = lax.conv_general_dilated(
        x, w[:, None, :].astype(x.dtype), window_strides=(1,), padding=[(k - 1, 0)],
        dimension_numbers=('NWC', 'WIO', 'NWC'), feature_group_count=x.shape[-1])
    return y + b

def ssd_chunked(xdt, a, bm, cm):
    b, s, h, p = xdt.shape
    g, n = bm.shape[-2:]
    r = h // g
    c, L = s // CHUNK, CHUNK
    xdt = xdt.reshape(b, c, L, g, r, p)
    a = a.reshape(b, c, L, g, r)
    bm = bm.reshape(b, c, L, g, n)
    cm = cm.reshape(b, c, L, g, n)
    a_cs = jnp.cumsum(a, axis=2)
    causal = jnp.tril(jnp.ones((L, L), dtype=bool))
    seg = a_cs[:, :, :, None] - a_cs[:, :, None]
    decay = jnp.exp(jnp.where(causal[:, :, None, None], seg, -jnp.inf))
    cb = jnp.einsum('bclgn,bcsgn->bclsg', cm, bm)
    y_diag = jnp.einsum('bclsgr,bcsgrp->bclgrp', cb[..., None] * decay, xdt)
    state_decay = jnp.exp(a_cs[:, :, -1:] - a_cs)
    chunk_states = jnp.einsum('bclgn,bclgr,bclgrp->bcgrpn', bm, state_decay, xdt)
    chunk_decay = jnp.exp(a_cs[:, :, -1])

    def step(state, inp):
        st, dec = inp
        return state * dec[..., None, None] + st, state

    init = jnp.zeros((b, g, r, p, n), dtype=jnp.float32)
    _, s_prev = lax.scan(step, init, (jnp.moveaxis(chunk_states, 1, 0), jnp.moveaxis(chunk_decay, 1, 0)))
    s_prev = jnp.moveaxis(s_prev, 0, 1)
    y_off = jnp.einsum('bclgn,bcgrpn,bclgr->bclgrp', cm, s_prev, jnp.exp(a_cs))
    return (y_diag + y_off).reshape(b, s, h, p)

def ssd_mixer(z, xbc, dt_raw, conv_w, conv_b, dt_bias, a_log, d_skip, norm_w):
    b, s, _ = z.shape
    xbc = jax.nn.silu(causal_dwconv(xbc, conv_w, conv_b))
    xs, bm, cm = jnp.split(xbc, [SSD_INNER, SSD_INNER + SSD_GROUPS * SSD_STATE], axis=-1)
    xs = xs.reshape(b, s, SSD_HEADS, SSD_HEADDIM).astype(jnp.float32)
    bm = bm.reshape(b, s, SSD_GROUPS, SSD_STATE).astype(jnp.float32)
    cm = cm.reshape(b, s, SSD_GROUPS, SSD_STATE).astype(jnp.float32)
    dt = jax.nn.softplus(dt_raw.astype(jnp.float32) + dt_bias.astype(jnp.float32))
    a = -jnp.exp(a_log.astype(jnp.float32))
    y = ssd_chunked(xs * dt[..., None], dt * a, bm, cm)
    y = y + xs * d_skip.astype(jnp.float32)[:, None]
    y = y.reshape(b, s, SSD_INNER) * jax.nn.silu(z.astype(jnp.float32))
    return rmsnorm(y, norm_w).astype(z.dtype)

def _lru_combine(left, right):
    a1, b1 = left
    a2, b2 = right
    return a1 * a2, a2 * b1 + b2

def rglru_mixer(y_gate, xb, conv_w, conv_b, w_a, b_a, w_i, b_i, lam):
    b, s, _ = xb.shape
    xb = causal_dwconv(xb, conv_w, conv_b).astype(jnp.float32)
    xblk = xb.reshape(b, s, LRU_BLOCKS, LRU_BLOCK)
    r = jax.nn.sigmoid(jnp.einsum('bski,kij->bskj', xblk, w_a).reshape(b, s, LRU_WIDTH) + b_a)
    i = jax.nn.sigmoid(jnp.einsum('bski,kij->bskj', xblk, w_i).reshape(b, s, LRU_WIDTH) + b_i)
    log_a = -LRU_C * r * jax.nn.softplus(-lam.astype(jnp.float32))
    a = jnp.exp(log_a)
    u = jnp.sqrt(-jnp.expm1(2.0 * log_a)) * (i * xb)
    _, h = lax.associative_scan(_lru_combine, (a, u), axis=1)
    return (h * jax.nn.gelu(y_gate.astype(jnp.float32))).astype(y_gate.dtype)

def rotary(x):
    s, d = x.shape[1], x.shape[-1]
    inv = 1.0 / (ROPE_BASE ** jnp.linspace(0.0, 1.0, d // 2, dtype=jnp.float32))
    ang = jnp.arange(s, dtype=jnp.float32)[:, None] * inv[None]
    cos = jnp.cos(ang)[None, :, None]
    sin = jnp.sin(ang)[None, :, None]
    x1 = x[..., 0::2]
    x2 = x[..., 1::2]
    return jnp.stack([x1 * cos - x2 * sin, x1 * sin + x2 * cos], axis=-1).reshape(x.shape)

def retention_chunked(q, k, v, log_gamma):
    b, s, h, dk = q.shape
    dv = v.shape[-1]
    c, L = s // CHUNK, CHUNK
    q = q.reshape(b, c, L, h, dk)
    k = k.reshape(b, c, L, h, dk)
    v = v.reshape(b, c, L, h, dv)
    idx = jnp.arange(L, dtype=jnp.float32)
    diff = idx[:, None] - idx[None, :]
    dmask = jnp.where(diff[None] >= 0, jnp.exp(jnp.maximum(diff, 0.0)[None] * log_gamma[:, None, None]), 0.0)
    scores = jnp.einsum('bclhd,bcshd->bchls', q, k) * dmask[None, None]
    inner = jnp.einsum('bchls,bcshe->bclhe', scores, v)
    k_decay = jnp.exp((L - 1.0 - idx)[:, None] * log_gamma[None])
    chunk_kv = jnp.einsum('bclhd,lh,bclhe->bchde', k, k_decay, v)
    chunk_decay = jnp.exp(L * log_gamma)

    def step(state, kv):
        return state * chunk_decay[:, None, None] + kv, state

    init = jnp.zeros((b, h, dk, dv), dtype=jnp.float32)
    _, s_prev = lax.scan(step, init, jnp.moveaxis(chunk_kv, 1, 0))
    s_prev = jnp.moveaxis(s_prev, 0, 1)
    q_decay = jnp.exp((idx + 1.0)[:, None] * log_gamma[None])
    cross = jnp.einsum('bclhd,lh,bchde->bclhe', q, q_decay, s_prev)
    return (inner + cross).reshape(b, s, h, dv)

def retention_mixer(q, k, v, g):
    b, s, _ = q.shape
    qh = rotary(q.reshape(b, s, RET_HEADS, RET_QK_DIM).astype(jnp.float32))
    kh = rotary(k.reshape(b, s, RET_HEADS, RET_QK_DIM).astype(jnp.float32)) * (RET_QK_DIM ** -0.5)
    vh = v.reshape(b, s, RET_HEADS, RET_V_DIM).astype(jnp.float32)
    log_gamma = jnp.log(1.0 - jnp.exp2(-5.0 - jnp.arange(RET_HEADS, dtype=jnp.float32)))
    y = retention_chunked(qh, kh, vh, log_gamma)
    y = y * lax.rsqrt(jnp.mean(y * y, axis=-1, keepdims=True) + EPS)
    y = y.reshape(b, s, RET_WIDTH) * jax.nn.silu(g.astype(jnp.float32))
    return y.astype(q.dtype)

def conv_ffn(h, w_in, conv_w, conv_b, w_out):
    a, u = jnp.split(h @ w_in, 2, axis=-1)
    a = causal_dwconv(a, conv_w, conv_b)
    return (jax.nn.gelu(a) * u) @ w_out

def second_inputs(seed: int = 0) -> dict:
    key = jax.random.key(seed)
    ks = jax.random.split(key, 24)
    f32 = jnp.float32
    nrm = lambda k, shape, scale: scale * jax.random.normal(k, shape, dtype=f32)
    x = jax.random.normal(ks[0], (BATCH, SEQ, D_MODEL), dtype=f32)
    norm_mix = 1.0 + nrm(ks[1], (DEPTH_2, D_MODEL), 0.02)
    w_in = nrm(ks[2], (DEPTH_2, D_MODEL, IN_PROJ_DIM), D_MODEL ** -0.5)
    ssd_conv_w = nrm(ks[3], (DEPTH_2, SSD_CONV, SSD_CONV_DIM), SSD_CONV ** -0.5)
    ssd_conv_b = nrm(ks[4], (DEPTH_2, SSD_CONV_DIM), 0.02)
    dt0 = jnp.exp(jax.random.uniform(ks[5], (DEPTH_2, SSD_HEADS), dtype=f32,
                                     minval=math.log(1e-3), maxval=math.log(1e-1)))
    ssd_dt_bias = dt0 + jnp.log(-jnp.expm1(-dt0))
    ssd_a_log = jnp.log(jax.random.uniform(ks[6], (DEPTH_2, SSD_HEADS), dtype=f32, minval=1.0, maxval=16.0))
    ssd_d = 1.0 + nrm(ks[7], (DEPTH_2, SSD_HEADS), 0.1)
    ssd_norm = 1.0 + nrm(ks[8], (DEPTH_2, SSD_INNER), 0.02)
    lru_conv_w = nrm(ks[9], (DEPTH_2, LRU_CONV, LRU_WIDTH), LRU_CONV ** -0.5)
    lru_conv_b = nrm(ks[10], (DEPTH_2, LRU_WIDTH), 0.02)
    lru_w_a = nrm(ks[11], (DEPTH_2, LRU_BLOCKS, LRU_BLOCK, LRU_BLOCK), LRU_BLOCK ** -0.5)
    lru_b_a = nrm(ks[12], (DEPTH_2, LRU_WIDTH), 0.02)
    lru_w_i = nrm(ks[13], (DEPTH_2, LRU_BLOCKS, LRU_BLOCK, LRU_BLOCK), LRU_BLOCK ** -0.5)
    lru_b_i = nrm(ks[14], (DEPTH_2, LRU_WIDTH), 0.02)
    a8 = jax.random.uniform(ks[15], (DEPTH_2, LRU_WIDTH), dtype=f32, minval=0.9, maxval=0.999)
    a0 = a8 ** (1.0 / LRU_C)
    lru_lambda = jnp.log(a0) - jnp.log1p(-a0)
    w_branch = nrm(ks[16], (DEPTH_2, N_BRANCHES, D_MODEL, D_MODEL), D_MODEL ** -0.5)
    w_o = nrm(ks[17], (DEPTH_2, D_MODEL, D_MODEL), D_MODEL ** -0.5)
    norm_ffn = 1.0 + nrm(ks[18], (DEPTH_2, D_MODEL), 0.02)
    ffn_w_in = nrm(ks[19], (DEPTH_2, D_MODEL, 2 * FFN_DIM), D_MODEL ** -0.5)
    ffn_conv_w = nrm(ks[20], (DEPTH_2, FFN_CONV, FFN_DIM), FFN_CONV ** -0.5)
    ffn_conv_b = nrm(ks[21], (DEPTH_2, FFN_DIM), 0.02)
    ffn_w_out = nrm(ks[22], (DEPTH_2, FFN_DIM, D_MODEL), FFN_DIM ** -0.5)
    norm_final = 1.0 + nrm(ks[23], (D_MODEL,), 0.02)
    return {'x': x, 'norm_mix': norm_mix, 'w_in': w_in,
            'ssd_conv_w': ssd_conv_w, 'ssd_conv_b': ssd_conv_b, 'ssd_dt_bias': ssd_dt_bias,
            'ssd_a_log': ssd_a_log, 'ssd_d': ssd_d, 'ssd_norm': ssd_norm,
            'lru_conv_w': lru_conv_w, 'lru_conv_b': lru_conv_b, 'lru_w_a': lru_w_a, 'lru_b_a': lru_b_a,
            'lru_w_i': lru_w_i, 'lru_b_i': lru_b_i, 'lru_lambda': lru_lambda,
            'w_branch': w_branch, 'w_o': w_o, 'norm_ffn': norm_ffn,
            'ffn_w_in': ffn_w_in, 'ffn_conv_w': ffn_conv_w, 'ffn_conv_b': ffn_conv_b,
            'ffn_w_out': ffn_w_out, 'norm_final': norm_final}

def second_block(x, norm_mix, w_in, ssd_conv_w, ssd_conv_b, ssd_dt_bias, ssd_a_log, ssd_d, ssd_norm,
              lru_conv_w, lru_conv_b, lru_w_a, lru_b_a, lru_w_i, lru_b_i, lru_lambda,
              w_branch, w_o, norm_ffn, ffn_w_in, ffn_conv_w, ffn_conv_b, ffn_w_out, norm_final):
    b, s, _ = x.shape
    offsets = np.cumsum(IN_SPLITS_2)[:-1].tolist()
    for l in range(DEPTH_2):
        h = rmsnorm(x, norm_mix[l])
        proj = h @ w_in[l]
        (z, xbc, dt_raw, lru_y, lru_x, q, k, v, ret_g, gate_pre) = jnp.split(proj, offsets, axis=-1)
        y_ssd = ssd_mixer(z, xbc, dt_raw, ssd_conv_w[l], ssd_conv_b[l], ssd_dt_bias[l],
                          ssd_a_log[l], ssd_d[l], ssd_norm[l])
        y_lru = rglru_mixer(lru_y, lru_x, lru_conv_w[l], lru_conv_b[l], lru_w_a[l], lru_b_a[l],
                            lru_w_i[l], lru_b_i[l], lru_lambda[l])
        y_ret = retention_mixer(q, k, v, ret_g)
        branches = jnp.stack([y_ssd, y_lru, y_ret], axis=2)
        branch_d = jnp.einsum('bskw,kwd->bskd', branches, w_branch[l])
        gates = jax.nn.sigmoid(gate_pre.reshape(b, s, N_BRANCHES, D_MODEL))
        merged = jnp.sum(gates * branch_d, axis=2)
        x = x + merged @ w_o[l]
        h = rmsnorm(x, norm_ffn[l])
        x = x + conv_ffn(h, ffn_w_in[l], ffn_conv_w[l], ffn_conv_b[l], ffn_w_out[l])
    return rmsnorm(x, norm_final)


def setup_inputs(seed=0):
    out = dict(first_inputs(seed))
    for name, value in second_inputs(seed + 1).items():
        if name != "x":
            out[name + "_2"] = value
    return out


def reference(
    x, g_mix, w_in, gate_b, a_conv_w, a_conv_b, a_ln_g, a_ln_b, na_qn, na_kn, na_rpb, dil_qn,
    dil_kn, swa_qn, swa_kn, swa_sink, w_branch, w_out, g_ffn, w_up, ffn_conv_w, ffn_conv_b,
    w_down, norm_mix_2, w_in_2, ssd_conv_w_2, ssd_conv_b_2, ssd_dt_bias_2, ssd_a_log_2, ssd_d_2,
    ssd_norm_2, lru_conv_w_2, lru_conv_b_2, lru_w_a_2, lru_b_a_2, lru_w_i_2, lru_b_i_2,
    lru_lambda_2, w_branch_2, w_o_2, norm_ffn_2, ffn_w_in_2, ffn_conv_w_2, ffn_conv_b_2,
    ffn_w_out_2, norm_final_2,
):
    x = first_block(
        x, g_mix, w_in, gate_b, a_conv_w, a_conv_b, a_ln_g, a_ln_b, na_qn, na_kn, na_rpb,
        dil_qn, dil_kn, swa_qn, swa_kn, swa_sink, w_branch, w_out, g_ffn, w_up, ffn_conv_w,
        ffn_conv_b, w_down,
    )
    return second_block(
        x, norm_mix_2, w_in_2, ssd_conv_w_2, ssd_conv_b_2, ssd_dt_bias_2, ssd_a_log_2, ssd_d_2,
        ssd_norm_2, lru_conv_w_2, lru_conv_b_2, lru_w_a_2, lru_b_a_2, lru_w_i_2, lru_b_i_2,
        lru_lambda_2, w_branch_2, w_o_2, norm_ffn_2, ffn_w_in_2, ffn_conv_w_2, ffn_conv_b_2,
        ffn_w_out_2, norm_final_2,
    )


_drawn_inputs = setup_inputs


def setup_inputs(seed=0):
    import zlib

    import numpy as np

    out = dict(_drawn_inputs(seed))
    spreads = {}
    factors = {'g_mix': 3.23,
     'gate_b': 8.0,
     'a_conv_b': 4.246,
     'a_ln_g': 3.628,
     'a_ln_b': 8.0,
     'na_qn': 8.0,
     'na_kn': 8.0,
     'na_rpb': 3.077,
     'dil_qn': 8.0,
     'dil_kn': 8.0,
     'swa_qn': 8.0,
     'swa_kn': 8.0,
     'swa_sink': 8.0,
     'ffn_conv_b': 4.457,
     'norm_mix_2': 3.556,
     'ssd_conv_b_2': 5.661,
     'ssd_norm_2': 29.068,
     'lru_conv_b_2': 8.386,
     'lru_b_a_2': 35.22,
     'lru_b_i_2': 50.322,
     'norm_ffn_2': 14.743,
     'ffn_conv_b_2': 21.062,
     'norm_final_2': 23.243,
     'ssd_d_2': 64.0}
    for name, (base, spread) in spreads.items():
        noise = np.random.default_rng([zlib.crc32(name.encode()), seed]).standard_normal(out[name].shape)
        drawn = base * np.exp(spread * noise) if base else spread * noise
        out[name] = __import__('jax').numpy.asarray(drawn.astype(out[name].dtype))
    for name, factor in factors.items():
        out[name] = (out[name] * factor).astype(out[name].dtype)
    return out
```

```python
from contextlib import ExitStack, contextmanager

import numpy as np
import concourse.bass as bass
from concourse import mybir

F32 = mybir.dt.float32
F32R = mybir.dt.float32r
ALU = mybir.AluOpType
ACT = mybir.ActivationFunctionType
AX = mybir.AxisListType.X

P = 128
T = 256
D = 1024
CH = D // P
DEPTH = 2
EPS = 1e-6
NEG = -1e30
RING = 4

HD = 64
NG1 = 4
QKT = 11
VT = 5
TAPS = 31
FF1 = 2816 // P
SCALE = 0.125
UNITS1 = 4 + QKT + VT + 4 * CH + 2 * CH + 3 * FF1
PAD1 = -UNITS1 % RING
SWA_TILE = 8
PIECES = [
    (0, 2, 0, 64, 2), (1, 3, 128, 64, 3),
    (4, 6, 256, 64, 4), (5, 7, 384, 64, 5),
    (8, 10, 512, 64, 6), (9, 10, 512, 64, 7)]


def columns(widths):
    at, out = 0, {}
    for name, w in widths:
        out[name] = at
        at += w
    return out, at


P1, NP1 = columns([("g_mix", CH), ("g_ffn", CH), ("gate_b", 4 * CH), ("conv_w", 2 * TAPS), ("conv_b", 2),
                   ("ln_g", 2), ("ln_b", 2), ("qk_g", QKT), ("sink", 4), ("ffn", 8 * FF1)])

SSD_T = 12
HEADS, GROUPS = 16, 2
RET_H = 4
FF2 = 3072 // P
UNITS2 = CH + SSD_T + 1 + 4 + CH + CH + CH + CH + CH + 3 * 2 * CH + CH + 3 * FF2
W15 = T + T // 2
P2, NP2 = columns([("g_mix", CH), ("g_ffn", CH), ("g_out", CH), ("ssd_conv", 5 * SSD_T), ("dt_bias", 1), ("a_log", 1),
                   ("ssd_d", CH), ("ssd_g", CH), ("lru_conv", 5 * CH), ("b_a", CH), ("b_i", CH), ("lam", CH),
                   ("ffn", 4 * FF2)])
K2, NK2 = columns([("perm", P), ("cos", T), ("sin", T), ("causal", W15), ("decay", RET_H * W15),
                   ("sel", HEADS * P), ("hot", 2 * RET_H * RET_H)])
K0, NK0 = columns([("ident", P), ("ones", P), ("ones256", P)])
K1, NK1 = columns([("hstat", QKT * 2 * QKT), ("hsel", QKT * P), ("perm", P), ("cos", T), ("sin", T),
                   ("dil", 2 * T), ("swa", 2 * T)])


STEP = {}


class Desk:

    def __init__(self, eng, name, per_trip, found):
        self.eng, self.name, self.per_trip, self.found = eng, name, per_trip, found
        self.n, self.loops, self.n_loops, self.last = {}, [], 0, None

    def value(self, sem, role, back=0):
        v = self.n.get((sem.name, role), 0) - back
        for reg, loop in self.loops:
            per = self.per_trip.get((loop, sem.name, role), 0)
            if per:
                v = reg * per + v
        return v

    def skip(self, sem, k=1, role="wait"):
        self.n[(sem.name, role)] = self.n.get((sem.name, role), 0) + k * STEP.get(sem.name, 1)

    def next(self, sem, k=1, role="wait"):
        self.skip(sem, k, role)
        return self.value(sem, role)

    def inc(self, sem, k=1):
        self.skip(sem, k, "made")
        self.last = sem
        return k * STEP.get(sem.name, 1)

    def made(self, sem, back=0):
        return self.value(sem, "made", back)

    @contextmanager
    def loop(self, trips):
        loop = (self.name, self.n_loops)
        self.n_loops += 1
        before = dict(self.n)
        with self.eng.Fori(0, trips) as i:
            self.loops.append((i, loop))
            yield i
            self.loops.pop()
        for key, n in self.n.items():
            per = n - before.get(key, 0)
            self.found[(loop, *key)] = per
            self.n[key] = before.get(key, 0) + trips * per


def program(nc, t, per_trip, found, blocks=3):
    with ExitStack() as ctx:
        def sb(name, n, dt=F32):
            return ctx.enter_context(nc.sbuf_tensor(name, [P, n], dt))

        def signal(name, step=1):
            sem = ctx.enter_context(nc.semaphore(name))
            STEP[sem.name] = step
            return sem

        raw = [sb(f"raw{s}", D) for s in range(RING)]
        w_hi = [sb(f"w_hi{s}", D, F32R) for s in range(RING)]
        w_lo = [sb(f"w_lo{s}", D, F32R) for s in range(RING)]
        h_hi, h_lo = sb("h_hi", CH * T, F32R), sb("h_lo", CH * T, F32R)
        y_hi, y_lo = sb("y_hi", 2 * CH * T, F32R), sb("y_lo", 2 * CH * T, F32R)
        f_hi, f_lo = sb("f_hi", 2 * T, F32R), sb("f_lo", 2 * T, F32R)
        zero = sb("zero", P, F32R)
        x = sb("x", CH * T)
        common = sb("common", NK0)
        A1, NA1 = columns([("gates", 4 * CH * T), ("qk", QKT * T), ("v", 2 * VT * P), ("u", 2 * (T + TAPS - 1)),
                           ("conv", 2 * T), ("sg", 2 * T), ("sc", 4 * 2 * T), ("pts", 2 * 2 * T),
                           ("consts", NK1), ("bias", 4 * 2 * T)])
        A2, NA2 = columns([("xb", CH * T), ("r", CH * T), ("i", CH * T), ("qk", CH * T), ("xbc", SSD_T * T),
                           ("xdt", 2 * D), ("cb", GROUPS * W15), ("seg", 3 * W15), ("dt", 2 * T), ("tab", 4 * HEADS),
                           ("merged", CH * T), ("consts", NK2)])
        A2R, _ = columns([("v", 2 * D), ("y", CH * T), ("p", 2 * W15)])
        arena = sb("arena", max(NA1, NA2))
        rows, rstd = sb("rows", T), sb("rstd", T)
        small = sb("small", 64)
        pre = sb("pre", 4 * T)
        mixf = sb("mixf", 2 * T)
        prm = sb("prm", max(NP1, NP2))
        psum = ctx.enter_context(nc.psum_tensor("psum", [P, 8 * 512], F32))

        def a1(name, lo, n):
            return arena[:, A1[name] + lo:A1[name] + lo + n]

        def a2(name, lo, n, parts=P, table=A2):
            lo = lo + table[name]
            return arena[0:parts, lo:lo + n] if isinstance(lo, int) else arena[0:parts, bass.ds(lo, n)]

        def ar(name, lo, n, parts=P):
            return a2(name, lo, n, parts, A2R)

        def c2(name, lo, n, parts=P):
            return a2("consts", K2[name] + lo, n, parts)

        def p2(name, lo=0, n=1, parts=P):
            lo = lo + P2[name]
            return prm[0:parts, lo:lo + n] if isinstance(lo, int) else prm[0:parts, bass.ds(lo, n)]

        def ck(name, lo, n, parts=P):
            return arena[0:parts, A1["consts"] + K1[name] + lo:A1["consts"] + K1[name] + lo + n]

        def bank(b, lo=0, n=512):
            return psum[:, b * 512 + lo:b * 512 + lo + n]

        def slot(s):
            return bank(4 + s, 0, T)

        def acc(f):
            return psum[:, f * T:(f + 1) * T]

        ident, ones, ones256 = (common[:, K0[n]:K0[n] + P] for n in ("ident", "ones", "ones256"))

        def chunk(buf, c, n=1):
            return buf[:, c * T:(c + n) * T] if isinstance(c, int) else buf[:, bass.ds(c * T, n * T)]

        raw_full = [signal(f"raw_full{s}", 16) for s in range(RING)]
        hi_ready, lo_ready = signal("hi_ready"), signal("lo_ready")
        unit_done = signal("unit_done")
        slot_free = signal("slot_free")
        loaded = signal("loaded", 16)
        params_full = signal("params_full", 16)
        bias_full = signal("bias_full", 16)
        init = signal("init")
        vec, act_own = signal("vec"), signal("act_own")
        x_ready, sq_ready, stat_ready = signal("x_ready"), signal("sq_ready"), signal("stat_ready")
        sd_ready, hf_ready = signal("sd_ready"), signal("hf_ready")
        hhi_ready, hlo_ready = signal("hhi_ready"), signal("hlo_ready")
        sg_ready, qsq_ready, qr_ready = signal("sg_ready"), signal("qsq_ready"), signal("qr_ready")
        bc_ready, qn_ready, pm_ready, rope_ready = (signal(n) for n in ("bc_ready", "qn_ready", "pm_ready", "rope_ready"))
        conv_ready, mean_ready = signal("conv_ready"), signal("mean_ready")
        s_ready, s_free, negm_ready, exp_ready = (signal(n) for n in ("s_ready", "s_free", "negm_ready", "exp_ready"))
        p_ready, pt_ready, pts_ready, o_ready = (signal(n) for n in ("p_ready", "pt_ready", "pts_ready", "o_ready"))
        yhi_ready, ylo_ready = signal("yhi_ready"), signal("ylo_ready")
        gsig_ready, mixf_ready = signal("gsig_ready"), signal("mixf_ready")
        fhi_ready, flo_ready = signal("fhi_ready"), signal("flo_ready")
        pre_ready, cg_ready, sil_ready = signal("pre_ready"), signal("cg_ready"), signal("sil_ready")
        consts2_full = signal("consts2_full", 16)
        soft_in, soft_exp, coef_ready = signal("soft_in"), signal("soft_exp"), signal("coef_ready")
        conv_done, ri_ready, at_ready, m2_ready, root_ready = (
            signal(n) for n in ("conv_done", "ri_ready", "at_ready", "m2_ready", "root_ready"))
        acs_ready, turn_ready, xt_ready, xdt_ready = (signal(n) for n in ("acs_ready", "turn_ready", "xt_ready", "xdt_ready"))
        silu_ready, cb_ready, cbm_ready, ea_ready = (signal(n) for n in ("silu_ready", "cb_ready", "cbm_ready", "ea_ready"))
        seg_bc, seg_ready, dec_ready, m_ready, yh_ready, ys_ready = (
            signal(n) for n in ("seg_bc", "seg_ready", "dec_ready", "m_ready", "yh_ready", "ys_ready"))
        qk2_ready, pm2_ready, rot_ready = signal("qk2_ready"), signal("pm2_ready"), signal("rot_ready")
        act_out, prod_ready, yhi2_ready, ylo2_ready = (signal(n) for n in ("act_out", "prod_ready", "yhi2_ready", "ylo2_ready"))
        v_ready, rs_ready, rp_ready, ry_ready, ryf_ready, rsq_ready = (
            signal(n) for n in ("v_ready", "rs_ready", "rp_ready", "ry_ready", "ryf_ready", "rsq_ready"))
        rstat_ready, rsd_ready, rrow_ready, rbc_ready, rn_ready = (
            signal(n) for n in ("rstat_ready", "rsd_ready", "rrow_ready", "rbc_ready", "rn_ready"))
        merged_ready, result_ready = signal("merged_ready"), signal("result_ready")
        stored = signal("stored", 16)

        total_units = t["units"].shape[0]
        block = ctx.enter_context(nc.Block())

        @block.sync
        def _(sp):
            d = Desk(sp, "sp", per_trip, found)
            sp.dma_start(x[:, :].rearrange("p (c t) -> p c t", c=CH),
                                t["x"].rearrange("(c p) t -> p c t", p=P)).then_inc(loaded, d.inc(loaded))
            sp.dma_start(common[:, :], t["common"]).then_inc(loaded, d.inc(loaded))
            for s in range(RING):
                sp.dma_start(raw[s][:, :], t["units"][s]).then_inc(raw_full[s], d.inc(raw_full[s]))
            sp.dma_start(arena[:, A1["consts"]:A1["consts"] + NK1], t["consts1"]).then_inc(loaded, d.inc(loaded))

            def load(index, s):
                sp.wait_ge(hi_ready, d.next(hi_ready))
                sp.wait_ge(lo_ready, d.next(lo_ready))
                sp.dma_start(raw[s][:, :], t["units"][bass.ds(index, 1)].rearrange("a p c -> p (a c)"))\
                    .then_inc(raw_full[s], d.inc(raw_full[s]))

            with d.loop((total_units - RING) // RING) as i:
                for s in range(RING):
                    load(i * RING + (RING + s), s)
            for u in range(total_units - total_units % RING, total_units):
                load(u, u % RING)
            for q in range(4):
                sp.wait_ge(result_ready, d.next(result_ready, 2))
                sp.dma_start(t["out"].rearrange("(c p) t -> p c t", p=P)[:, 2 * q:2 * q + 2, :],
                                    chunk(arena, 2 * q, 2).rearrange("p (c t) -> p c t", c=2))\
                                        .then_inc(stored, d.inc(stored))
            sp.wait_ge(stored, d.made(stored))

        @block.gpsimd
        def _(pool):
            d = Desk(pool, "pool", per_trip, found)

            def low(s):
                pool.wait_ge(raw_full[s], d.next(raw_full[s]))
                pool.wait_ge(hi_ready, d.next(hi_ready))
                pool.wait_ge(unit_done, d.next(unit_done, 1, "slot"))
                pool.tensor_tensor(w_lo[s][:, :], raw[s][:, :], w_hi[s][:, :].bitcast(F32), ALU.subtract)\
                    .then_inc(lo_ready, d.inc(lo_ready))

            with d.loop(total_units // RING) as _:
                for s in range(RING):
                    low(s)
            for s in range(total_units % RING):
                low(s)

        @block.scalar
        def _(act):
            d = Desk(act, "act", per_trip, found)
            units_hi = [0]

            def high(n=1):
                for _ in range(n):
                    if not d.loops and d.n.get((hi_ready.name, "made"), 0) >= total_units:
                        return
                    s = units_hi[0] % RING
                    units_hi[0] += 1
                    act.wait_ge(raw_full[s], d.next(raw_full[s]))
                    act.wait_ge(unit_done, d.next(unit_done, 1, "slot"))
                    act.activation(w_hi[s][:, :], raw[s][:, :], ACT.Copy).then_inc(hi_ready, d.inc(hi_ready))

            def norm(between=None):
                for q in range(4):
                    act.wait_ge(x_ready, d.next(x_ready))
                    act.activation(chunk(arena, 2 * q, 2), chunk(x, 2 * q, 2), ACT.Square)\
                        .then_inc(sq_ready, d.inc(sq_ready))
                if between:
                    between()
                act.wait_ge(stat_ready, d.next(stat_ready))
                act.activation(rows[:, :], bank(0, 0, T), ACT.Sqrt, bias=small[:, 60:61])\
                    .then_inc(sd_ready, d.inc(sd_ready))
                for q in range(4):
                    act.wait_ge(hf_ready, d.next(hf_ready))
                    act.activation(chunk(h_hi, 2 * q, 2), chunk(arena, 2 * q, 2), ACT.Copy)\
                        .then_inc(hhi_ready, d.inc(hhi_ready))

            def exps(p):
                q_tile = PIECES[p][0]
                for h in range(2):
                    sc = a1("sc", (2 * (p % 2) + h) * 512, 512)
                    act.wait_ge(negm_ready, d.next(negm_ready))
                    c = 8 * h
                    for r in range(2):
                        last = act.activation(sc[:, r * T:(r + 1) * T], sc[:, r * T:(r + 1) * T], ACT.Exp,
                                              bias=small[:, c + 2 + r:c + 3 + r], accum_out=small[:, c + 4 + r:c + 5 + r])
                        if r == 0:
                            last.then_inc(act_own, d.inc(act_own))
                    if q_tile >= SWA_TILE:
                        last.then_inc(act_own, d.inc(act_own))
                        head = q_tile - SWA_TILE + 2 * h
                        last = act.activation(small[:, c + 6:c + 8], small[:, c + 2:c + 4], ACT.Exp,
                                              bias=prm[:, P1["sink"] + head:P1["sink"] + head + 1])
                    last.then_inc(exp_ready, d.inc(exp_ready))

            def outputs(p):
                for h in range(2):
                    act.wait_ge(pt_ready, d.next(pt_ready))
                    act.activation(a1("pts", h * 512, 512), bank(h), ACT.Copy).then_inc(pts_ready, d.inc(pts_ready))
                act.wait_ge(o_ready, d.next(o_ready))
                act.activation(chunk(y_hi, PIECES[p][4]), bank(0, 0, T), ACT.Copy)\
                    .then_inc(yhi_ready, d.inc(yhi_ready))

            d.skip(unit_done, RING)
            act.wait_ge(init, d.next(init))
            high(RING - 1)
            with d.loop(DEPTH) as layer:
                act.wait_ge(x_ready, d.next(x_ready, 4, "layer"))
                act.dma_start(prm[:, :], t["params1"][bass.ds(layer, 1)].rearrange("a p c -> p (a c)"))\
                    .then_inc(params_full, d.inc(params_full))
                act.dma_start(a1("bias", 0, 4 * 2 * T), t["bias1"][bass.ds(layer, 1)].rearrange("a p c -> p (a c)"))\
                    .then_inc(bias_full, d.inc(bias_full))
                d.skip(x_ready, 4, "layer")
                norm()
                high(2)
                d.skip(unit_done, 2)
                for k in range(2):
                    high()
                    act.wait_ge(unit_done, d.next(unit_done))
                    act.activation(a1("sg", k * T, T), slot(2 + k), ACT.Sigmoid).then_inc(sg_ready, d.inc(sg_ready))
                for k in range(QKT):
                    high()
                    act.wait_ge(unit_done, d.next(unit_done))
                    act.activation(a1("gates", (8 + k) * T, T), slot(k % RING), ACT.Square)\
                        .then_inc(qsq_ready, d.inc(qsq_ready))
                for k in range(VT):
                    high()
                d.skip(unit_done, VT)
                act.wait_ge(stat_ready, d.next(stat_ready))
                act.activation(rows[0:2 * QKT, :], psum[0:2 * QKT, 0:T], ACT.Sqrt,
                                      bias=small[0:2 * QKT, 60:61]).then_inc(sd_ready, d.inc(sd_ready))
                with d.loop(3) as _:
                    high(RING)
                d.skip(unit_done, 3 * RING)
                act.wait_ge(hf_ready, d.next(hf_ready))
                act.activation(a1("sg", 0, 2 * T), a1("conv", 0, 2 * T), ACT.Square)\
                    .then_inc(sq_ready, d.inc(sq_ready))
                act.wait_ge(stat_ready, d.next(stat_ready))
                act.activation(rows[:, :], bank(1, T, T), ACT.Sqrt, bias=small[:, 60:61])\
                    .then_inc(sd_ready, d.inc(sd_ready))
                for k in range(2):
                    act.wait_ge(hf_ready, d.next(hf_ready))
                    act.activation(a1("sg", k * T, T), a1("conv", k * T, T), ACT.Silu,
                                          bias=prm[:, P1["ln_b"] + k:P1["ln_b"] + k + 1])\
                                              .then_inc(act_own, d.inc(act_own))
                act.wait_ge(d.last, d.made(d.last))
                act.activation(chunk(y_hi, 0, 2), a1("sg", 0, 2 * T), ACT.Copy)\
                    .then_inc(yhi_ready, d.inc(yhi_ready))
                for p in range(len(PIECES)):
                    more = p < len(PIECES) - 1
                    if more:
                        high()
                    exps(p)
                    if more:
                        high(3)
                        d.skip(unit_done, RING)
                    outputs(p)
                def gate_sigmoid(c):
                    act.activation(a1("gates", c * 4 * T, 4 * T), a1("gates", c * 4 * T, 4 * T), ACT.Sigmoid)\
                        .then_inc(gsig_ready, d.inc(gsig_ready))

                def feed_high(b):
                    act.wait_ge(mixf_ready, d.next(mixf_ready))
                    act.activation(chunk(f_hi, b), chunk(mixf, b), ACT.Copy).then_inc(fhi_ready, d.inc(fhi_ready))

                for c in range(3):
                    gate_sigmoid(c)
                for c in range(2):
                    high()
                    d.skip(unit_done, 1)
                    feed_high(c)
                for c in range(3, CH):
                    gate_sigmoid(c)
                with d.loop((CH - 2) // 2) as _:
                    for b in range(2):
                        high(2)
                        d.skip(unit_done, 1)
                        act.wait_ge(unit_done, d.next(unit_done))
                        feed_high(b)
                high(2)
                d.skip(unit_done, 2)
                norm()

                def ffn_act(j, b):
                    for k in range(2):
                        high()
                        act.wait_ge(unit_done, d.next(unit_done))
                        cols = P1["ffn"] + 4 * k
                        at = (lambda o: prm[:, bass.ds(j * 8 + (cols + o), 1)])
                        act.activation(pre[:, (2 * b + k) * T:(2 * b + k + 1) * T], slot(2 * b + k), ACT.Identity,
                                              scale=at(1), bias=at(3)).then_inc(pre_ready, d.inc(pre_ready))

                def ffn_gate(b):
                    act.wait_ge(cg_ready, d.next(cg_ready))
                    act.activation(pre[:, 2 * b * T:(2 * b + 1) * T], pre[:, 2 * b * T:(2 * b + 1) * T], ACT.Silu)\
                        .then_inc(sil_ready, d.inc(sil_ready))

                for j in range(2):
                    ffn_act(j, j)
                    ffn_gate(j)
                    feed_high(j)
                with d.loop((FF1 - 2) // RING) as i:
                    for jj in range(RING):
                        ffn_act(i * RING + (2 + jj), jj % 2)
                        high()
                        ffn_gate(jj % 2)
                        act.wait_ge(unit_done, d.next(unit_done))
                        feed_high(jj % 2)
                high(2 + PAD1)
                d.skip(unit_done, 2 + PAD1)

            slots = [0]

            def next_slot():
                slots[0] += 1
                return (slots[0] - 1) % RING

            def take():
                high()
                act.wait_ge(unit_done, d.next(unit_done))
                return next_slot()

            def middle_tap(dst, tap, bias):
                s = take()
                act.wait_ge(init, 1)
                act.activation(dst, slot(s), ACT.Identity, scale=tap, bias=bias)\
                    .then_inc(pre_ready, d.inc(pre_ready))

            def softplus_exp(n, parts):
                act.wait_ge(soft_in, d.next(soft_in))
                e = small[:, 16:16 + n] if n == CH else rows[0:parts, :]
                act.activation(e, e, ACT.Exp).then_inc(soft_exp, d.inc(soft_exp))

            def parts_high(buf, c, src):
                act.wait_ge(init, 1)
                act.activation(chunk(y_hi, buf * CH + c), src, ACT.Copy).then_inc(yhi2_ready, d.inc(yhi2_ready))

            act.wait_ge(x_ready, d.next(x_ready, 4, "layer"))
            act.dma_start(prm[:, 0:NP2], t["params2"]).then_inc(params_full, d.inc(params_full))
            act.dma_start(a2("consts", 0, NK2), t["consts2"]).then_inc(consts2_full, d.inc(consts2_full))
            norm(lambda: softplus_exp(CH, P))
            with d.loop(CH // RING) as i:
                for k in range(RING):
                    c = i * RING + k
                    middle_tap(a2("xb", c * T, T), p2("lru_conv", c * 5 + 3), p2("lru_conv", c * 5 + 4))
                    act.wait_ge(conv_done, d.next(conv_done))
                    parts_high(1, c, a2("xb", c * T, T))
            with d.loop(SSD_T // RING) as i:
                for k in range(RING):
                    c = i * RING + k
                    middle_tap(a2("xbc", c * T, T), p2("ssd_conv", c * 5 + 3), p2("ssd_conv", c * 5 + 4))
                    act.wait_ge(conv_done, d.next(conv_done))
                    act.activation(small[:, 57:58], small[:, 60:61], ACT.Copy)
                    act.activation(a2("xbc", c * T, T), a2("xbc", c * T, T), ACT.Silu)\
                        .then_inc(silu_ready, d.inc(silu_ready))
            high()
            d.skip(unit_done, 1)
            next_slot()
            softplus_exp(T, HEADS)
            act.activation(small[0:HEADS, 58:59], p2("a_log", 0, 1, HEADS), ACT.Exp)\
                .then_inc(ea_ready, d.inc(ea_ready))
            for b in range(4):
                high()
                act.wait_ge(unit_done, d.next(unit_done))
                for k in range(4):
                    name, bias, c = (("r", "b_a"), ("i", "b_i"))[k // 2] + (2 * b + k % 2,)
                    act.activation(a2(name, c * T, T), slot(next_slot()), ACT.Sigmoid, bias=p2(bias, c))\
                        .then_inc(ri_ready, d.inc(ri_ready))
            act.wait_ge(coef_ready, d.next(coef_ready))
            for c in range(CH):
                if c < RING:
                    high()
                    d.skip(unit_done)
                    next_slot()
                if c % 2 == 0:
                    act.wait_ge(conv_done, d.next(conv_done))
                act.wait_ge(ri_ready, d.made(ri_ready))
                act.activation(a2("xb", c * T, T), a2("r", c * T, T), ACT.Exp, scale=small[:, 24 + c:25 + c])\
                    .then_inc(act_own, d.inc(act_own))
                act.activation(a2("r", c * T, T), a2("r", c * T, T), ACT.Tanh, scale=small[:, 32 + c:33 + c])\
                    .then_inc(at_ready, d.inc(at_ready))
            act.wait_ge(m2_ready, d.next(m2_ready))
            for q in range(4):
                high()
                d.skip(unit_done)
                next_slot()
                if q:
                    act.wait_ge(m2_ready, d.next(m2_ready))
                act.activation(a2("r", 2 * q * T, 2 * T), a2("r", 2 * q * T, 2 * T), ACT.Sqrt)\
                    .then_inc(root_ready, d.inc(root_ready))

            def times_activation(func, buf):
                with d.loop(CH // RING) as i:
                    for k in range(RING):
                        c = i * RING + k
                        s = take()
                        act.activation(chunk(pre, k), slot(s), func).then_inc(act_out, d.inc(act_out))
                        if buf is not None:
                            act.wait_ge(prod_ready, d.next(prod_ready))
                            parts_high(buf, c, chunk(mixf, k % 2))

            def gated_branch():
                with d.loop(CH // RING * 2) as _:
                    for k in range(2):
                        act.activation(chunk(pre, k), slot(take()), ACT.Sigmoid).then_inc(act_out, d.inc(act_out))
                        high()
                        d.skip(unit_done)
                        next_slot()

            act.wait_ge(rot_ready, d.next(rot_ready, CH))
            times_activation(ACT.Gelu_apprx_tanh, 0)
            gated_branch()
            for h in range(HEADS + 1):
                if h < HEADS:
                    act.wait_ge(seg_ready, d.next(seg_ready))
                    seg = a2("seg", h % 3 * W15, W15)
                    act.activation(seg, seg, ACT.Exp).then_inc(dec_ready, d.inc(dec_ready))
                if h % 2 == 0 and h < HEADS:
                    high()
                    d.skip(unit_done)
                    next_slot()
            times_activation(ACT.Silu, None)
            for q in range(4):
                if q == 0:
                    act.wait_ge(prod_ready, d.next(prod_ready, CH))
                act.activation(a2("xdt", 2 * q * T, 2 * T), a2("xbc", 2 * q * T, 2 * T), ACT.Square)\
                    .then_inc(sq_ready, d.inc(sq_ready))
            for h in range(RET_H):
                act.wait_ge(ryf_ready, d.next(ryf_ready))
                act.activation(a2("seg", 0, 2 * T) if h % 2 == 0 else a2("seg", 2 * T, 2 * T),
                                      ar("y", 2 * h * T, 2 * T), ACT.Square).then_inc(rsq_ready, d.inc(rsq_ready))
                if h == 0:
                    act.wait_ge(stat_ready, d.next(stat_ready))
                    act.activation(rows[:, :], bank(0, 0, T), ACT.Sqrt, bias=small[:, 60:61])\
                        .then_inc(sd_ready, d.inc(sd_ready))
                if h == 2:
                    for q in range(4):
                        act.wait_ge(hf_ready, d.next(hf_ready))
                        act.activation(chunk(y_hi, CH + 2 * q, 2), a2("xbc", 2 * q * T, 2 * T), ACT.Copy)\
                            .then_inc(yhi2_ready, d.inc(yhi2_ready))
            act.wait_ge(rstat_ready, d.next(rstat_ready))
            act.activation(rows[0:RET_H, :], psum[0:RET_H, 3 * 512:3 * 512 + T], ACT.Sqrt, bias=small[0:RET_H, 60:61])\
                .then_inc(rsd_ready, d.inc(rsd_ready))
            gated_branch()
            times_activation(ACT.Silu, 0)
            gated_branch()
            for c in range(CH):
                if c == 0:
                    act.wait_ge(merged_ready, d.next(merged_ready))
                high()
                if c >= 2:
                    act.wait_ge(unit_done, d.next(unit_done))
                act.activation(chunk(f_hi, c % 2), a2("merged", c * T, T), ACT.Copy)\
                    .then_inc(fhi_ready, d.inc(fhi_ready))
            d.skip(unit_done, 2)
            norm()

            def ffn2(j, b):
                s = take()
                act.wait_ge(init, 1)
                act.activation(chunk(pre, b), slot(s), ACT.Identity, scale=p2("ffn", j * 4 + 2), bias=p2("ffn", j * 4 + 3))\
                    .then_inc(pre_ready, d.inc(pre_ready))
                high()
                next_slot()
                act.wait_ge(cg_ready, d.next(cg_ready))
                act.activation(chunk(pre, b), chunk(pre, b), ACT.Gelu_apprx_tanh)\
                    .then_inc(sil_ready, d.inc(sil_ready))

            for j in range(2):
                ffn2(j, j)
                d.skip(unit_done)
                feed_high(j)
            with d.loop((FF2 - 2) // RING) as i:
                for jj in range(RING):
                    ffn2(i * RING + (2 + jj), jj % 2)
                    high()
                    d.skip(unit_done)
                    act.wait_ge(unit_done, d.next(unit_done))
                    feed_high(jj % 2)
            for jj in range((FF2 - 2) % RING):
                ffn2(FF2 - (FF2 - 2) % RING + jj, jj % 2)
                if jj == 0:
                    high()
                d.skip(unit_done)
                act.wait_ge(unit_done, d.next(unit_done))
                feed_high(jj % 2)
            for q in range(4):
                act.wait_ge(x_ready, d.next(x_ready))
                act.activation(chunk(arena, 2 * q, 2), chunk(x, 2 * q, 2), ACT.Square)\
                    .then_inc(sq_ready, d.inc(sq_ready))
            act.wait_ge(stat_ready, d.next(stat_ready))
            act.activation(rows[:, :], bank(0, 0, T), ACT.Sqrt, bias=small[:, 60:61])\
                .then_inc(sd_ready, d.inc(sd_ready))

        @block.tensor
        def _(pe):
            d = Desk(pe, "pe", per_trip, found)
            n_units, n_slots = [0], [0]

            def next_slot():
                s = n_slots[0] % RING
                n_slots[0] += 1
                return s

            def mm3(out, hi, lo, r_hi, r_lo, start, stop, **kw):
                pe.matmul(out, hi, r_hi, start=start, stop=False, **kw)
                pe.matmul(out, lo, r_hi, start=False, stop=False, **kw)
                return pe.matmul(out, hi, r_lo, start=False, stop=stop, **kw)

            def blocks_of(w, k):
                return w[:, k * P:(k + 1) * P]

            def unit():
                s = n_units[0] % RING
                n_units[0] += 1
                pe.wait_ge(lo_ready, d.next(lo_ready))
                return s

            def linear_unit(src_hi, src_lo, first=None):
                s = unit()
                o = slot(next_slot())
                pe.wait_ge(slot_free, d.next(slot_free))
                for c in range(CH):
                    if first is not None and c % 2 == 0:
                        pe.wait_ge(first, d.next(first))
                    last = mm3(o, blocks_of(w_hi[s], c), blocks_of(w_lo[s], c), chunk(src_hi, c), chunk(src_lo, c),
                               c == 0, c == CH - 1)
                last.then_inc(unit_done, d.inc(unit_done))

            def value_unit():
                s = unit()
                o = slot(next_slot())
                pe.wait_ge(slot_free, d.next(slot_free))
                for half in range(2):
                    for c in range(CH):
                        lo = c * T + half * P
                        last = mm3(o[:, half * P:(half + 1) * P], h_hi[:, lo:lo + P], h_lo[:, lo:lo + P],
                                   blocks_of(w_hi[s], c), blocks_of(w_lo[s], c), c == 0, c == CH - 1)
                last.then_inc(unit_done, d.inc(unit_done))

            def zero_acc():
                for b in range(4):
                    for k in range(4):
                        pe.matmul(bank(b, k * P, P), zero[:, :], zero[:, :], start=(k == 0), stop=(k == 3), skip_group_check=True)

            def acc_unit(b, pads=0):
                s = unit()
                pe.wait_ge(flo_ready, d.next(flo_ready))
                for f in range(CH):
                    last = mm3(acc(f), blocks_of(w_hi[s], f), blocks_of(w_lo[s], f), chunk(f_hi, b), chunk(f_lo, b),
                               False, f == CH - 1, skip_group_check=True)
                d.skip(lo_ready, pads)
                n_units[0] += pads
                last.then_inc(unit_done, d.inc(unit_done, 1 + pads))

            def norm_stats():
                for q in range(4):
                    pe.wait_ge(sq_ready, d.next(sq_ready))
                    for c in (2 * q, 2 * q + 1):
                        last = pe.matmul(bank(0, 0, T), ones, chunk(arena, c), start=(c == 0), stop=(c == CH - 1))
                last.then_inc(stat_ready, d.inc(stat_ready))

            def scores(p):
                q_tile, k_tile = PIECES[p][:2]
                if p:
                    pe.wait_ge(s_free, d.next(s_free, 2))
                for h in range(2):
                    lo, hi = h * HD, (h + 1) * HD
                    for r in range(2):
                        at = A1["qk"] + q_tile * T + r * P
                        ak = A1["qk"] + k_tile * T
                        last = pe.matmul(bank(2 + h, r * T, T), arena[lo:hi, at:at + P], arena[lo:hi, ak:ak + T],
                                         start=True, stop=True)
                    last.then_inc(s_ready, d.inc(s_ready))
                if p == len(PIECES) - 1:
                    d.skip(s_free, 2)

            def attend(p):
                v0, step = PIECES[p][2:4]
                pe.wait_ge(yhi_ready, d.next(yhi_ready))
                pe.wait_ge(ylo_ready, d.next(ylo_ready))
                for h in range(2):
                    pe.wait_ge(p_ready, d.next(p_ready))
                    sc = a1("sc", (2 * (p % 2) + h) * 512, 512)
                    for kc in range(2):
                        for r in range(2):
                            last = pe.transpose(bank(h, kc * T + r * P, P), sc[:, r * T + kc * P:r * T + (kc + 1) * P], ident)
                    last.then_inc(pt_ready, d.inc(pt_ready))
                if p < len(PIECES) - 1:
                    scores(p + 1)
                for h in range(2):
                    pe.wait_ge(pts_ready, d.next(pts_ready))
                    for kc in range(2):
                        av = A1["v"] + kc * VT * P + v0 + h * step
                        last = pe.matmul(psum[h * HD:(h + 1) * HD, 0:T], arena[:, av:av + HD],
                                         a1("pts", h * 512 + kc * T, T), start=(kc == 0), stop=(kc == 1))
                last.then_inc(o_ready, d.inc(o_ready))

            pe.wait_ge(loaded, d.next(loaded, 3))
            pe.wait_ge(init, d.next(init))
            pe.sem_inc(unit_done, RING)
            with d.loop(DEPTH) as _:
                norm_stats()
                linear_unit(h_hi, h_lo, hlo_ready)
                for _ in range(3):
                    linear_unit(h_hi, h_lo)
                with d.loop(2) as _:
                    for _ in range(RING):
                        linear_unit(h_hi, h_lo)
                for _ in range(QKT - 2 * RING):
                    linear_unit(h_hi, h_lo)
                for _ in range(VT):
                    value_unit()
                pe.wait_ge(qsq_ready, d.next(qsq_ready, QKT))
                for j in range(QKT):
                    last = pe.matmul(psum[0:2 * QKT, 0:T], ck("hstat", j * 2 * QKT, 2 * QKT),
                                     a1("gates", (8 + j) * T, T), start=(j == 0), stop=(j == QKT - 1))
                last.then_inc(stat_ready, d.inc(stat_ready))
                with d.loop(2) as _:
                    for _ in range(RING):
                        linear_unit(h_hi, h_lo)
                def spread(tiles):
                    for b in range(4):
                        for j in tiles[2 * b:2 * b + 2]:
                            last = pe.matmul(bank(b, j % 2 * T, T), ck("hsel", j * P, P, 2 * QKT), rstd[0:2 * QKT, :],
                                             start=True, stop=True)
                            if j % 2 or j == QKT - 1:
                                last.then_inc(bc_ready, d.inc(bc_ready))

                def partners(tiles, b):
                    for j in tiles:
                        last = pe.matmul(bank(b, j % 2 * T, T), ck("perm", 0, P), a1("qk", j * T, T), start=True, stop=True)
                    last.then_inc(pm_ready, d.inc(pm_ready))

                pe.wait_ge(qr_ready, d.next(qr_ready))
                spread(range(8))
                for _ in range(RING):
                    linear_unit(h_hi, h_lo)
                pe.wait_ge(qn_ready, d.next(qn_ready, 8))
                spread(range(8, QKT))
                partners((4, 5), 2)
                partners((6, 7), 3)
                pe.wait_ge(qn_ready, d.next(qn_ready, QKT - 8))
                partners((8, 9), 0)
                partners((10,), 1)
                pe.wait_ge(rope_ready, d.next(rope_ready, QKT - 4))
                scores(0)
                pe.wait_ge(conv_ready, d.next(conv_ready))
                for k in range(2):
                    last = pe.matmul(bank(1, 0, T), ones256, a1("conv", k * T, T), start=(k == 0), stop=(k == 1))
                last.then_inc(mean_ready, d.inc(mean_ready))
                pe.wait_ge(sq_ready, d.next(sq_ready))
                for k in range(2):
                    last = pe.matmul(bank(1, T, T), ones256, a1("sg", k * T, T), start=(k == 0), stop=(k == 1))
                last.then_inc(stat_ready, d.inc(stat_ready))
                for p in range(len(PIECES)):
                    if p < len(PIECES) - 1:
                        for _ in range(RING):
                            linear_unit(h_hi, h_lo)
                    attend(p)
                pe.wait_ge(yhi_ready, d.next(yhi_ready))
                pe.wait_ge(ylo_ready, d.next(ylo_ready))

                def branch_unit():
                    s = unit()
                    pe.wait_ge(slot_free, d.next(slot_free, 2))
                    pair = [next_slot(), next_slot()]
                    for n in range(NG1):
                        o = bank(4 + pair[n // 2], n % 2 * T, T)
                        for c in (2 * n, 2 * n + 1):
                            last = mm3(o, blocks_of(w_hi[s], c), blocks_of(w_lo[s], c), chunk(y_hi, c), chunk(y_lo, c),
                                       c == 2 * n, c == 2 * n + 1)
                    last.then_inc(unit_done, d.inc(unit_done))

                zero_acc()
                branch_unit()
                branch_unit()
                with d.loop((CH - 2) // 2) as _:
                    for b in range(2):
                        branch_unit()
                        acc_unit(b)
                for b in range(2):
                    acc_unit(b)
                norm_stats()
                linear_unit(h_hi, h_lo, hlo_ready)
                zero_acc()
                for _ in range(3):
                    linear_unit(h_hi, h_lo)
                with d.loop((FF1 - 2) // RING) as _:
                    for jj in range(RING):
                        linear_unit(h_hi, h_lo)
                        linear_unit(h_hi, h_lo)
                        acc_unit(jj % 2)
                acc_unit(0)
                acc_unit(1, PAD1)

            pe.wait_ge(consts2_full, d.next(consts2_full))
            norm_stats()
            linear_unit(h_hi, h_lo, hlo_ready)
            for _ in range(3):
                linear_unit(h_hi, h_lo)

            def linear_units(n, src_hi=h_hi, src_lo=h_lo):
                with d.loop(n // RING) as _:
                    for _ in range(RING):
                        linear_unit(src_hi, src_lo)

            linear_units(CH - RING)
            linear_units(SSD_T)
            linear_unit(h_hi, h_lo)
            y1_hi, y1_lo = y_hi[:, CH * T:2 * CH * T], y_lo[:, CH * T:2 * CH * T]
            pe.wait_ge(ylo2_ready, d.next(ylo2_ready, CH))
            for b in range(4):
                s = unit()
                pe.wait_ge(slot_free, d.next(slot_free, RING))
                for k in range(4):
                    o = slot(next_slot())
                    for c in range(2):
                        last = mm3(o, blocks_of(w_hi[s], 2 * k + c), blocks_of(w_lo[s], 2 * k + c),
                                   chunk(y1_hi, 2 * b + c), chunk(y1_lo, 2 * b + c), c == 0, c == 1)
                last.then_inc(unit_done, d.inc(unit_done))
            for _ in range(RING):
                linear_unit(h_hi, h_lo)
            pe.wait_ge(acs_ready, d.next(acs_ready))
            for n in range(2):
                for half in range(2):
                    last = pe.transpose(bank(0, (2 * n + half) * HEADS, HEADS), a2("dt", n * T + half * P, P, HEADS), ident[0:HEADS, 0:HEADS])
            last.then_inc(turn_ready, d.inc(turn_ready))
            for c in range(CH):
                for half in range(2):
                    last = pe.transpose(bank([1, 2, 3, 0][c // 2], (c % 2 * 2 + half) * P, P), a2("xbc", c * T + half * P, P), ident)
                if c % 2:
                    last.then_inc(xt_ready, d.inc(xt_ready))
                if c == 5:
                    pe.wait_ge(xdt_ready, d.next(xdt_ready, 1))
            for _ in range(RING):
                linear_unit(h_hi, h_lo)
            pe.wait_ge(xdt_ready, d.next(xdt_ready, 2))
            for g in range(GROUPS):
                bt, ct = CH + g, CH + GROUPS + g
                pe.matmul(bank(1 + g, 0, T), a2("xbc", bt * T, P), a2("xbc", ct * T, T), start=True, stop=True)
                last = pe.matmul(bank(1 + g, T, P), a2("xbc", bt * T + P, P), a2("xbc", ct * T + P, P), start=True, stop=True)
                last.then_inc(cb_ready, d.inc(cb_ready))
            pe.wait_ge(xdt_ready, d.next(xdt_ready, 2))
            pe.wait_ge(cbm_ready, d.next(cbm_ready, 2))
            pe.wait_ge(qk2_ready, d.next(qk2_ready))
            for c in range(CH):
                last = pe.matmul(bank(c // 2, c % 2 * T, T), c2("perm", 0, P), a2("qk", c * T, T), start=True, stop=True)
                if c % 2:
                    last.then_inc(pm2_ready, d.inc(pm2_ready))

            def gated_branch(buf):
                with d.loop(CH // RING * 2) as _:
                    for _ in range(2):
                        linear_unit(h_hi, h_lo)
                        linear_unit(*((y1_hi, y1_lo) if buf else (y_hi, y_lo)))

            linear_units(CH)
            pe.wait_ge(ylo2_ready, d.next(ylo2_ready, CH))
            gated_branch(0)
            pe.wait_ge(rot_ready, d.next(rot_ready, CH))

            def segment(h):
                pe.matmul(bank(h % 2, 0, T), c2("sel", h * P, P, HEADS), a2("dt", T, T, HEADS), start=True, stop=True)\
                    .then_inc(seg_bc, d.inc(seg_bc))

            def ssd_head(h):
                m = a2("seg", h % 3 * W15, W15)
                lo = h % 2 * HD
                b = 2 + h // 2 % 2
                pe.wait_ge(m_ready, d.next(m_ready))
                if h % 2 == 0 and h >= 4:
                    pe.wait_ge(ys_ready, d.next(ys_ready))
                pe.matmul(psum[lo:lo + HD, b * 512:b * 512 + T], a2("xdt", h * HD, HD), m[:, 0:T], start=True, stop=False)
                last = pe.matmul(psum[lo:lo + HD, b * 512 + P:b * 512 + T], a2("xdt", D + h * HD, HD), m[:, T:W15], start=False, stop=True)
                last.then_inc(yh_ready, d.inc(yh_ready))

            segment(0)
            segment(1)
            for h in range(HEADS):
                if h % 2 == 0:
                    value_unit()
                ssd_head(h)
                if h + 2 < HEADS:
                    pe.wait_ge(seg_ready, d.next(seg_ready))
                    segment(h + 2)
            pe.wait_ge(seg_ready, d.next(seg_ready, 2))
            linear_units(CH)
            pe.wait_ge(ys_ready, d.next(ys_ready, 2))
            for h in range(RET_H):
                if h == 0:
                    for q in range(4):
                        pe.wait_ge(sq_ready, d.next(sq_ready))
                        for c in (2 * q, 2 * q + 1):
                            last = pe.matmul(bank(0, 0, T), ones, a2("xdt", c * T, T), start=(c == 0), stop=(c == CH - 1))
                    last.then_inc(stat_ready, d.inc(stat_ready))
                if h >= 1:
                    pe.wait_ge(rsq_ready, d.next(rsq_ready))
                kt, qt = RET_H + h, h
                pe.matmul(bank(1, 0, T), a2("qk", kt * T, P), a2("qk", qt * T, T), start=True, stop=True)
                last = pe.matmul(bank(1, T, P), a2("qk", kt * T + P, P), a2("qk", qt * T + P, P), start=True, stop=True)
                last.then_inc(rs_ready, d.inc(rs_ready))
                pe.wait_ge(rp_ready, d.next(rp_ready))
                pr = ar("p", h % 2 * W15, W15)
                for e in range(2):
                    cv = h * 2 * P + e * P
                    pe.matmul(bank(2, e * T, T), ar("v", cv, P), pr[:, 0:T], start=True, stop=False)
                    last = pe.matmul(bank(2, e * T + P, P), ar("v", D + cv, P), pr[:, T:W15], start=False, stop=True)
                last.then_inc(ry_ready, d.inc(ry_ready))
                if h >= 1:
                    for e in range(2):
                        last = pe.matmul(psum[0:RET_H, 3 * 512:3 * 512 + T], c2("hot", (h - 1) * RET_H, RET_H),
                                         a2("seg", (h - 1) % 2 * 2 * T + e * T, T), start=(h == 1 and e == 0), stop=False)
            pe.wait_ge(rsq_ready, d.next(rsq_ready))
            for e in range(2):
                last = pe.matmul(psum[0:RET_H, 3 * 512:3 * 512 + T], c2("hot", (RET_H - 1) * RET_H, RET_H),
                                 a2("seg", 2 * T + e * T, T), start=False, stop=(e == 1))
            last.then_inc(rstat_ready, d.inc(rstat_ready))
            pe.wait_ge(ylo2_ready, d.next(ylo2_ready, 4))
            gated_branch(1)
            pe.wait_ge(rrow_ready, d.next(rrow_ready))
            for h in range(RET_H):
                last = pe.matmul(bank(1 + h // 2, h % 2 * T, T), c2("sel", h * P, P, RET_H), rstd[0:RET_H, :], start=True, stop=True)
                if h % 2:
                    last.then_inc(rbc_ready, d.inc(rbc_ready))
            linear_units(CH)
            pe.wait_ge(ylo2_ready, d.next(ylo2_ready, CH))
            pe.wait_ge(rn_ready, d.next(rn_ready, RET_H))
            gated_branch(0)
            zero_acc()
            for c in range(CH):
                acc_unit(c % 2)
            norm_stats()
            linear_unit(h_hi, h_lo, hlo_ready)
            zero_acc()
            for _ in range(3):
                linear_unit(h_hi, h_lo)
            with d.loop((FF2 - 2) // RING) as _:
                for jj in range(RING):
                    linear_unit(h_hi, h_lo)
                    linear_unit(h_hi, h_lo)
                    acc_unit(jj % 2)
            for jj in range((FF2 - 2) % RING):
                linear_unit(h_hi, h_lo)
                linear_unit(h_hi, h_lo)
                acc_unit(jj % 2)
            for b in range(2):
                acc_unit(b)
            norm_stats()

        @block.vector
        def _(dve):
            d = Desk(dve, "dve", per_trip, found)




            def norm(gain):
                dve.wait_ge(sd_ready, d.next(sd_ready))
                dve.reciprocal(rstd[:, :], rows[:, :]).then_inc(vec, d.inc(vec))
                dve.wait_ge(d.last, d.made(d.last))
                for c in range(CH):
                    dve.scalar_tensor_tensor(chunk(arena, c), chunk(x, c), prm[:, gain + c:gain + c + 1], rstd[:, :], ALU.mult, ALU.mult)\
                        .then_inc(hf_ready if c % 2 else vec, d.inc(hf_ready if c % 2 else vec))
                for q in range(4):
                    dve.wait_ge(hhi_ready, d.next(hhi_ready))
                    dve.tensor_tensor(chunk(h_lo, 2 * q, 2), chunk(arena, 2 * q, 2), chunk(h_hi, 2 * q, 2).bitcast(F32), ALU.subtract)\
                        .then_inc(hlo_ready, d.inc(hlo_ready))

            def residual():
                dve.wait_ge(unit_done, d.next(unit_done))
                for q in range(4):
                    dve.tensor_tensor(chunk(x, 2 * q, 2), chunk(x, 2 * q, 2), bank(q), ALU.add)\
                        .then_inc(x_ready, d.inc(x_ready))

            def feed_low(b):
                dve.wait_ge(fhi_ready, d.next(fhi_ready))
                dve.tensor_tensor(chunk(f_lo, b), chunk(mixf, b), chunk(f_hi, b).bitcast(F32), ALU.subtract)\
                    .then_inc(flo_ready, d.inc(flo_ready))

            def conv_taps(first, n):
                with d.loop(n) as i:
                    for k in range(2):
                        dve.wait_ge(vec, d.made(vec, 1))
                        dve.scalar_tensor_tensor(a1("conv", k * T, T), arena[:, bass.ds(i + (A1["u"] + k * (T + TAPS - 1) + first), T)], prm[:, bass.ds(i + (P1["conv_w"] + k * TAPS + first), 1)], a1("conv", k * T, T), ALU.mult, ALU.add)\
                            .then_inc(vec, d.inc(vec))

            gate_tiles = [0]

            def gates(n):
                for _ in range(n):
                    g = gate_tiles[0]
                    gate_tiles[0] += 1
                    dve.wait_ge(unit_done, d.next(unit_done))
                    dve.tensor_scalar(a1("gates", g * T, T), slot(g % RING), prm[:, P1["gate_b"] + g:P1["gate_b"] + g + 1], None, ALU.add)\
                        .then_inc(slot_free, d.inc(slot_free))

            def softmax_scores(p):
                q_tile = PIECES[p][0]
                for h in range(2):
                    sc = a1("sc", (2 * (p % 2) + h) * 512, 512)
                    c = 8 * h
                    if p < 2:
                        bias = a1("bias", (2 * p + h) * 512, 512)
                    else:
                        bias = ck("dil" if p < 4 else "swa", 0, 512)
                    dve.wait_ge(s_ready, d.next(s_ready))
                    dve.scalar_tensor_tensor(sc, bank(2 + h), SCALE, bias, ALU.mult, ALU.add)\
                        .then_inc(s_free, d.inc(s_free))
                    dve.wait_ge(d.last, d.made(d.last))
                    dve.reduce_max(small[:, c:c + 2], sc.rearrange("p (r k) -> p r k", r=2), AX)\
                        .then_inc(vec, d.inc(vec))
                    dve.wait_ge(d.last, d.made(d.last))
                    if q_tile >= SWA_TILE:
                        head = q_tile - SWA_TILE + 2 * h
                        dve.tensor_scalar(small[:, c + 2:c + 4], small[:, c:c + 2], prm[:, P1["sink"] + head:P1["sink"] + head + 1], -1.0, ALU.max, ALU.mult)\
                            .then_inc(negm_ready, d.inc(negm_ready))
                    else:
                        dve.tensor_scalar(small[:, c + 2:c + 4], small[:, c:c + 2], -1.0, None, ALU.mult)\
                            .then_inc(negm_ready, d.inc(negm_ready))

            def softmax_norm(p):
                q_tile = PIECES[p][0]
                for h in range(2):
                    sc = a1("sc", (2 * (p % 2) + h) * 512, 512)
                    c = 8 * h
                    dve.wait_ge(exp_ready, d.next(exp_ready))
                    if q_tile >= SWA_TILE:
                        dve.tensor_tensor(small[:, c + 4:c + 6], small[:, c + 4:c + 6], small[:, c + 6:c + 8], ALU.add)\
                            .then_inc(vec, d.inc(vec))
                        dve.wait_ge(d.last, d.made(d.last))
                    dve.reciprocal(small[:, c + 4:c + 6], small[:, c + 4:c + 6]).then_inc(vec, d.inc(vec))
                    dve.wait_ge(d.last, d.made(d.last))
                    for r in range(2):
                        dve.tensor_scalar(sc[:, r * T:(r + 1) * T], sc[:, r * T:(r + 1) * T], small[:, c + 4 + r:c + 5 + r], None, ALU.mult)\
                            .then_inc(p_ready if r else vec, d.inc(p_ready if r else vec))

            def y_low(p):
                dve.wait_ge(yhi_ready, d.next(yhi_ready))
                cy = PIECES[p][4]
                dve.tensor_tensor(chunk(y_lo, cy), bank(0, 0, T), chunk(y_hi, cy).bitcast(F32), ALU.subtract)\
                    .then_inc(ylo_ready, d.inc(ylo_ready))

            dve.memset(zero[:, :].bitcast(F32), 0.0).then_inc(vec, d.inc(vec))
            dve.memset(a1("u", 0, 2 * (T + TAPS - 1)), 0.0).then_inc(vec, d.inc(vec))
            dve.memset(small[:, 60:61], EPS).then_inc(init, d.inc(init))
            dve.wait_ge(loaded, d.next(loaded, 3))
            dve.sem_inc(x_ready, 4)
            dve.sem_inc(slot_free, RING)
            d.skip(x_ready, 4, "made")
            d.skip(slot_free, RING, "made")
            d.skip(unit_done, RING)
            with d.loop(DEPTH) as _:
                gate_tiles[0] = 0
                dve.wait_ge(params_full, d.next(params_full))
                norm(P1["g_mix"])
                for k in range(2):
                    dve.wait_ge(sg_ready, d.next(sg_ready))
                    lo = k * (T + TAPS - 1) + TAPS // 2
                    dve.tensor_tensor(a1("u", lo, T), slot(k), a1("sg", k * T, T), ALU.mult)\
                        .then_inc(slot_free if k else vec, d.inc(slot_free if k else vec, RING if k else 1))
                d.skip(unit_done, RING)
                for j in range(QKT):
                    dve.wait_ge(unit_done, d.next(unit_done))
                    dve.wait_ge(qsq_ready, d.next(qsq_ready))
                    dve.tensor_copy(a1("qk", j * T, T), slot(j % RING)).then_inc(slot_free, d.inc(slot_free))
                for j in range(VT):
                    dve.wait_ge(unit_done, d.next(unit_done))
                    v = a1("v", 0, 2 * VT * P).rearrange("p (h c) -> p h c", h=2)[:, :, j * P:(j + 1) * P]
                    dve.tensor_copy(v, slot((QKT + j) % RING).rearrange("p (h c) -> p h c", h=2))\
                        .then_inc(slot_free, d.inc(slot_free))
                dve.wait_ge(sd_ready, d.next(sd_ready))
                dve.reciprocal(rstd[0:2 * QKT, :], rows[0:2 * QKT, :]).then_inc(qr_ready, d.inc(qr_ready))
                for k in range(2):
                    dve.tensor_scalar(a1("conv", k * T, T), a1("u", k * (T + TAPS - 1), T), prm[:, P1["conv_w"] + k * TAPS:P1["conv_w"] + k * TAPS + 1], prm[:, P1["conv_b"] + k:P1["conv_b"] + k + 1], ALU.mult, ALU.add)\
                        .then_inc(vec, d.inc(vec))
                conv_taps(1, 10)
                gates(RING)
                conv_taps(11, 10)
                gates(RING)
                def normalise(j):
                    if j % 2 == 0:
                        dve.wait_ge(bc_ready, d.next(bc_ready))
                    dve.scalar_tensor_tensor(a1("qk", j * T, T), a1("qk", j * T, T), prm[:, P1["qk_g"] + j:P1["qk_g"] + j + 1], bank(j % 8 // 2, j % 2 * T, T), ALU.mult, ALU.mult)\
                        .then_inc(qn_ready, d.inc(qn_ready))
                for j in range(8):
                    normalise(j)
                conv_taps(21, 9)
                dve.wait_ge(vec, d.made(vec, 1))
                for k in range(2):
                    dve.scalar_tensor_tensor(a1("conv", k * T, T), a1("u", k * (T + TAPS - 1) + TAPS - 1, T), prm[:, P1["conv_w"] + (k + 1) * TAPS - 1:P1["conv_w"] + (k + 1) * TAPS], a1("conv", k * T, T), ALU.mult, ALU.add)\
                        .then_inc(conv_ready if k else vec, d.inc(conv_ready if k else vec))
                    if k == 0:
                        dve.wait_ge(vec, d.made(vec, 1))
                gates(RING)
                for j in range(8, QKT):
                    normalise(j)
                for n, j in enumerate(range(4, QKT)):
                    if j % 2 == 0:
                        dve.wait_ge(pm_ready, d.next(pm_ready))
                    tmp = a1("pts", n % 2 * T, T)
                    dve.tensor_tensor(a1("qk", j * T, T), a1("qk", j * T, T), ck("cos", 0, T), ALU.mult)\
                        .then_inc(vec, d.inc(vec))
                    dve.tensor_tensor(tmp, bank([2, 3, 0, 1][n // 2], j % 2 * T, T), ck("sin", 0, T), ALU.mult)\
                        .then_inc(vec, d.inc(vec))
                    dve.wait_ge(d.last, d.made(d.last))
                    dve.tensor_tensor(a1("qk", j * T, T), a1("qk", j * T, T), tmp, ALU.add)\
                        .then_inc(rope_ready, d.inc(rope_ready))
                dve.wait_ge(bias_full, d.next(bias_full))
                softmax_scores(0)
                dve.wait_ge(mean_ready, d.next(mean_ready))
                for k in range(2):
                    dve.tensor_tensor(a1("conv", k * T, T), a1("conv", k * T, T), bank(1, 0, T), ALU.subtract)\
                        .then_inc(hf_ready if k else vec, d.inc(hf_ready if k else vec))
                dve.wait_ge(sd_ready, d.next(sd_ready))
                dve.reciprocal(rstd[:, :], rows[:, :]).then_inc(vec, d.inc(vec))
                dve.wait_ge(d.last, d.made(d.last))
                for k in range(2):
                    dve.scalar_tensor_tensor(a1("conv", k * T, T), a1("conv", k * T, T), prm[:, P1["ln_g"] + k:P1["ln_g"] + k + 1], rstd[:, :], ALU.mult, ALU.mult)\
                        .then_inc(hf_ready, d.inc(hf_ready))
                dve.wait_ge(yhi_ready, d.next(yhi_ready))
                dve.tensor_tensor(chunk(y_lo, 0, 2), a1("sg", 0, 2 * T), chunk(y_hi, 0, 2).bitcast(F32), ALU.subtract)\
                    .then_inc(ylo_ready, d.inc(ylo_ready))
                for p in range(len(PIECES)):
                    more = p < len(PIECES) - 1
                    if more:
                        gates(2)
                    softmax_norm(p)
                    if more:
                        gates(2)
                        softmax_scores(p + 1)
                    y_low(p)

                def mix(c, b):
                    dve.wait_ge(unit_done, d.next(unit_done))
                    dve.wait_ge(gsig_ready, d.next(gsig_ready))
                    prod = a1("sc", 0, 4 * T)
                    gat = arena[:, bass.ds(c * (4 * T) + A1["gates"], 4 * T)]
                    dve.tensor_tensor(prod, psum[:, (4 + 2 * b) * 512:(4 + 2 * b) * 512 + 4 * T], gat, ALU.mult)\
                        .then_inc(slot_free, d.inc(slot_free, 2))
                    dve.wait_ge(d.last, d.made(d.last))
                    half = a1("sc", 4 * T, 2 * T)
                    dve.tensor_tensor(half, prod[:, 0:2 * T], prod[:, 2 * T:4 * T], ALU.add)\
                        .then_inc(vec, d.inc(vec))
                    dve.wait_ge(d.last, d.made(d.last))
                    dve.tensor_tensor(chunk(mixf, b), half[:, 0:T], half[:, T:2 * T], ALU.add)\
                        .then_inc(mixf_ready, d.inc(mixf_ready))
                    feed_low(b)

                mix(0, 0)
                mix(1, 1)
                with d.loop((CH - 2) // 2) as i:
                    for b in range(2):
                        mix(i * 2 + (2 + b), b)
                        d.skip(unit_done, 1)
                d.skip(unit_done, 1)
                residual()
                norm(P1["g_ffn"])

                def ffn(j, b):
                    at = (lambda k, o: prm[:, bass.ds(j * 8 + (P1["ffn"] + 4 * k + o), 1)])
                    buf = [pre[:, (2 * b + k) * T:(2 * b + k + 1) * T] for k in range(2)]
                    for k in range(2):
                        dve.wait_ge(pre_ready, d.next(pre_ready))
                        dve.scalar_tensor_tensor(buf[k][:, 1:T], slot(2 * b + k)[:, 0:T - 1], at(k, 0), buf[k][:, 1:T], ALU.mult, ALU.add)\
                            .then_inc(vec, d.inc(vec))
                    for k in range(2):
                        dve.wait_ge(vec, d.made(vec, 1 - k))
                        dve.scalar_tensor_tensor(buf[k][:, 0:T - 1], slot(2 * b + k)[:, 1:T], at(k, 2), buf[k][:, 0:T - 1], ALU.mult, ALU.add)\
                            .then_inc(slot_free if k else cg_ready, d.inc(slot_free if k else cg_ready, 2 if k else 1))
                    dve.wait_ge(d.last, d.made(d.last))
                    dve.wait_ge(sil_ready, d.next(sil_ready))
                    dve.tensor_tensor(chunk(mixf, b), buf[0], buf[1], ALU.mult)\
                        .then_inc(mixf_ready, d.inc(mixf_ready))
                    feed_low(b)

                for j in range(2):
                    ffn(j, j)
                d.skip(unit_done, 4)
                with d.loop((FF1 - 2) // RING) as i:
                    for jj in range(RING):
                        ffn(i * RING + (2 + jj), jj % 2)
                        d.skip(unit_done, 3)
                d.skip(unit_done, 1)
                residual()
                d.skip(unit_done, PAD1)

            slots = [0]

            def next_slot():
                slots[0] += 1
                return (slots[0] - 1) % RING

            def take():
                dve.wait_ge(unit_done, d.next(unit_done))
                return next_slot()

            def shifted_taps(dst, s, name, c, per, taps, final):
                dve.wait_ge(pre_ready, d.next(pre_ready))
                for k in range(1, taps):
                    if k > 1:
                        dve.wait_ge(d.last, d.made(d.last))
                    dve.scalar_tensor_tensor(dst[:, k:T], slot(s)[:, 0:T - k], p2(name, c * per + (taps - 1 - k)), dst[:, k:T], ALU.mult, ALU.add)\
                        .then_inc(final if k == taps - 1 else vec, d.inc(final if k == taps - 1 else vec))

            def release(k=1):
                dve.wait_ge(slot_free, d.made(slot_free))
                dve.memset(small[:, 59:60], 0.0).then_inc(slot_free, d.inc(slot_free, k))

            def softplus(dst, src, work, parts, n):
                e, s, q = work
                dve.scalar_tensor_tensor(e, src, -1.0, src, ALU.mult, ALU.min).then_inc(soft_in, d.inc(soft_in))
                dve.tensor_scalar(src, src, 0.0, None, ALU.max).then_inc(vec, d.inc(vec))
                dve.wait_ge(soft_exp, d.next(soft_exp))
                dve.tensor_scalar(s, e, 2.0, None, ALU.add).then_inc(vec, d.inc(vec))
                dve.wait_ge(d.last, d.made(d.last))
                dve.reciprocal(s, s).then_inc(vec, d.inc(vec))
                dve.wait_ge(d.last, d.made(d.last))
                dve.tensor_tensor(s, s, e, ALU.mult).then_inc(vec, d.inc(vec))
                dve.wait_ge(d.last, d.made(d.last))
                dve.tensor_tensor(q, s, s, ALU.mult).then_inc(vec, d.inc(vec))
                dve.wait_ge(d.last, d.made(d.last))
                dve.tensor_scalar(e, q, 1.0 / 17, None, ALU.mult).then_inc(vec, d.inc(vec))
                for k in range(15, 1, -2):
                    dve.wait_ge(d.last, d.made(d.last))
                    dve.scalar_tensor_tensor(e, e, 1.0 / k, q, ALU.add, ALU.mult).then_inc(vec, d.inc(vec))
                dve.wait_ge(d.last, d.made(d.last))
                dve.scalar_tensor_tensor(e, e, 1.0, s, ALU.add, ALU.mult).then_inc(vec, d.inc(vec))
                dve.wait_ge(d.last, d.made(d.last))
                return dve.scalar_tensor_tensor(dst, e, 2.0, src, ALU.mult, ALU.add).then_inc(vec, d.inc(vec))

            def parts_low(buf, c, src, sig=None, k=1):
                dve.wait_ge(yhi2_ready, d.next(yhi2_ready))
                dve.tensor_tensor(chunk(y_lo, buf * CH + c), src, chunk(y_hi, buf * CH + c).bitcast(F32), ALU.subtract)\
                    .then_inc(sig or ylo2_ready, d.inc(sig or ylo2_ready, k))

            dve.wait_ge(params_full, d.next(params_full))
            dve.tensor_scalar(small[:, 40:48], p2("lam", 0, CH), -1.0, None, ALU.mult).then_inc(vec, d.inc(vec))
            dve.wait_ge(d.last, d.made(d.last))
            softplus(small[:, 24:32], small[:, 40:48], (small[:, 16:24], small[:, 32:40], small[:, 48:56]), P, CH)
            dve.wait_ge(d.last, d.made(d.last))
            dve.tensor_scalar(small[:, 32:40], small[:, 24:32], 8.0, None, ALU.mult).then_inc(vec, d.inc(vec))
            dve.tensor_scalar(small[:, 24:32], small[:, 24:32], -8.0, None, ALU.mult)\
                .then_inc(coef_ready, d.inc(coef_ready))
            norm(P2["g_mix"])
            with d.loop(CH // RING) as i:
                for k in range(RING):
                    c = i * RING + k
                    s = take()
                    shifted_taps(a2("xb", c * T, T), s, "lru_conv", c, 5, 4, conv_done)
                    parts_low(1, c, a2("xb", c * T, T))
                    release()
            with d.loop(SSD_T // RING) as i:
                for k in range(RING):
                    c = i * RING + k
                    s = take()
                    shifted_taps(a2("xbc", c * T, T), s, "ssd_conv", c, 5, 4, conv_done)
                    release()
            s = take()
            row = [a2("dt", 0, T, HEADS), rows[0:HEADS, :], rstd[0:HEADS, :], a2("dt", T, T, HEADS)]
            dve.tensor_scalar(row[0], slot(s)[0:HEADS, :], p2("dt_bias", 0, 1, HEADS), None, ALU.add)\
                .then_inc(slot_free, d.inc(slot_free))
            dve.wait_ge(d.last, d.made(d.last))
            softplus(row[0], row[0], (row[1], row[2], row[3]), HEADS, T)
            dve.wait_ge(d.last, d.made(d.last))
            dve.memset(row[1], 1.0).then_inc(vec, d.inc(vec))
            dve.wait_ge(d.last, d.made(d.last))
            dve.wait_ge(ea_ready, d.next(ea_ready))
            dve.tensor_scalar(row[2], row[0], small[0:HEADS, 58:59], -1.0, ALU.mult, ALU.mult)\
                .then_inc(vec, d.inc(vec))
            dve.wait_ge(d.last, d.made(d.last))
            dve.tensor_tensor_scan(row[3], row[1], row[2], 0.0, ALU.mult, ALU.add)\
                .then_inc(acs_ready, d.inc(acs_ready))
            for b in range(4):
                dve.wait_ge(ri_ready, d.next(ri_ready, 4))
                d.skip(unit_done)
                for _ in range(4):
                    next_slot()
                dve.tensor_tensor(a2("i", 2 * b * T, 2 * T), a2("i", 2 * b * T, 2 * T), a2("xb", 2 * b * T, 2 * T), ALU.mult)\
                    .then_inc(conv_done, d.inc(conv_done))
                release(4)
            for c in range(CH):
                if c < RING:
                    s = take()
                    dve.tensor_copy(a2("qk", c * T, T), slot(s)).then_inc(slot_free, d.inc(slot_free))
                dve.wait_ge(at_ready, d.next(at_ready))
                tmp = chunk(pre, c % 4)
                dve.tensor_tensor(tmp, a2("xb", c * T, T), a2("xb", c * T, T), ALU.mult).then_inc(vec, d.inc(vec))
                dve.wait_ge(d.last, d.made(d.last))
                dve.scalar_tensor_tensor(a2("r", c * T, T), tmp, 1.0, a2("r", c * T, T), ALU.add, ALU.mult)\
                    .then_inc(m2_ready if c % 2 else vec, d.inc(m2_ready if c % 2 else vec))
            dve.wait_ge(turn_ready, d.next(turn_ready))
            dve.tensor_copy(a2("tab", 0, 4 * HEADS), bank(0, 0, 4 * HEADS)).then_inc(xdt_ready, d.inc(xdt_ready))
            dve.wait_ge(d.last, d.made(d.last))
            for n in range(4):
                dve.wait_ge(xt_ready, d.next(xt_ready))
                for half in range(2):
                    src = bank([1, 2, 3, 0][n]).rearrange("p (c s h f) -> p s c h f", c=2, s=2, h=2)[:, half]
                    out = a2("xdt", half * D + n * T, T).rearrange("p (c h f) -> p c h f", c=2, h=2)
                    dts = a2("tab", half * HEADS + 4 * n, 4).rearrange("p (c h f) -> p c h f", c=2, h=2)
                    dve.tensor_tensor(out, src, dts.to_broadcast([P, 2, 2, HD]), ALU.mult)\
                        .then_inc(xdt_ready if half else vec, d.inc(xdt_ready if half else vec))
            for c in range(RING, CH):
                s = take()
                dve.tensor_copy(a2("qk", c * T, T), slot(s)).then_inc(slot_free, d.inc(slot_free))
            dve.memset(small[:, 58:59], 0.0).then_inc(qk2_ready, d.inc(qk2_ready))
            for q in range(4):
                dve.wait_ge(root_ready, d.next(root_ready))
                dve.tensor_tensor(a2("i", 2 * q * T, 2 * T), a2("i", 2 * q * T, 2 * T), a2("r", 2 * q * T, 2 * T), ALU.mult)\
                    .then_inc(vec, d.inc(vec))
                dve.wait_ge(d.last, d.made(d.last))
                for c in (2 * q, 2 * q + 1):
                    dve.tensor_tensor_scan(a2("r", c * T, T), a2("xb", c * T, T), a2("i", c * T, T), 0.0, ALU.mult, ALU.add)\
                        .then_inc(vec, d.inc(vec))
            dve.wait_ge(consts2_full, d.next(consts2_full))
            for g in range(GROUPS):
                dve.wait_ge(cb_ready, d.next(cb_ready))
                dve.tensor_tensor(a2("cb", g * W15, W15), bank(1 + g, 0, W15), c2("causal", 0, W15), ALU.mult)\
                    .then_inc(cbm_ready, d.inc(cbm_ready))
            for c in range(CH):
                if c % 2 == 0:
                    dve.wait_ge(pm2_ready, d.next(pm2_ready))
                tmp = chunk(pre, c % 4)
                dve.tensor_tensor(a2("qk", c * T, T), a2("qk", c * T, T), c2("cos", 0, T), ALU.mult)\
                    .then_inc(vec, d.inc(vec))
                dve.tensor_tensor(tmp, bank(c // 2, c % 2 * T, T), c2("sin", 0, T), ALU.mult)\
                    .then_inc(vec, d.inc(vec))
                dve.wait_ge(d.last, d.made(d.last))
                dve.tensor_tensor(a2("qk", c * T, T), a2("qk", c * T, T), tmp, ALU.add)\
                    .then_inc(rot_ready, d.inc(rot_ready))

            def times_activation(tile, buf):
                dve.wait_ge(d.last, d.made(d.last))
                with d.loop(CH // RING) as i:
                    for k in range(RING):
                        c = i * RING + k
                        take()
                        dve.wait_ge(act_out, d.next(act_out))
                        out = chunk(mixf, k % 2) if buf is not None else tile(c)
                        dve.tensor_tensor(out, tile(c), chunk(pre, k), ALU.mult)\
                            .then_inc(prod_ready, d.inc(prod_ready))
                        if buf is not None:
                            parts_low(buf, c, out)
                        release()

            def gated_branch(first):
                with d.loop(CH // RING * 2) as i:
                    for k in range(2):
                        c = i * 2 + k
                        take()
                        s = take()
                        dve.wait_ge(act_out, d.next(act_out))
                        if first:
                            dve.tensor_tensor(a2("merged", c * T, T), slot(s), chunk(pre, k), ALU.mult)\
                                .then_inc(slot_free, d.inc(slot_free, 2))
                        else:
                            dve.tensor_tensor(chunk(mixf, k), slot(s), chunk(pre, k), ALU.mult)\
                                .then_inc(slot_free, d.inc(slot_free, 2))
                            dve.wait_ge(d.last, d.made(d.last))
                            dve.tensor_tensor(a2("merged", c * T, T), a2("merged", c * T, T), chunk(mixf, k), ALU.add)\
                                .then_inc(vec, d.inc(vec))

            times_activation(lambda c: a2("r", c * T, T), 0)
            gated_branch(True)
            for h in range(HEADS + 3):
                if h >= 3:
                    dve.wait_ge(yh_ready, d.next(yh_ready))
                    c = (h - 3) // 2
                    if h % 2 == 0:
                        dve.scalar_tensor_tensor(a2("xbc", c * T, T), a2("xbc", c * T, T), p2("ssd_d", c), bank(2 + c % 2, 0, T), ALU.mult, ALU.add)\
                            .then_inc(ys_ready, d.inc(ys_ready))
                if h < HEADS:
                    dve.wait_ge(seg_bc, d.next(seg_bc))
                    for half in range(2):
                        dve.tensor_scalar(a2("seg", h % 3 * W15 + half * T, T - half * P), bank(h % 2, half * P, T - half * P), a2("tab", (2 + half) * HEADS + h, 1), 0.0, ALU.subtract, ALU.min)\
                            .then_inc(seg_ready if half else vec, d.inc(seg_ready if half else vec))
                if 1 <= h <= HEADS:
                    dve.wait_ge(dec_ready, d.next(dec_ready))
                    seg = a2("seg", (h - 1) % 3 * W15, W15)
                    dve.tensor_tensor(seg, seg, a2("cb", (h - 1) // (HEADS // GROUPS) * W15, W15), ALU.mult)\
                        .then_inc(m_ready, d.inc(m_ready))
                if h % 2 and h < HEADS:
                    s = take()
                    v = ar("v", 0, 2 * D).rearrange("p (h c) -> p h c", h=2)[:, :, h // 2 * P:(h // 2 + 1) * P]
                    dve.tensor_copy(v, slot(s).rearrange("p (h c) -> p h c", h=2))\
                        .then_inc(slot_free, d.inc(slot_free))
            times_activation(lambda c: a2("xbc", c * T, T), None)
            for h in range(RET_H):
                dve.wait_ge(rs_ready, d.next(rs_ready))
                dve.tensor_tensor(ar("p", h % 2 * W15, W15), bank(1, 0, W15), c2("decay", h * W15, W15), ALU.mult)\
                    .then_inc(rp_ready, d.inc(rp_ready))
                dve.wait_ge(ry_ready, d.next(ry_ready))
                dve.tensor_copy(ar("y", 2 * h * T, 2 * T), bank(2)).then_inc(ryf_ready, d.inc(ryf_ready))
                if h == 0:
                    dve.wait_ge(sd_ready, d.next(sd_ready))
                    dve.reciprocal(rstd[:, :], rows[:, :]).then_inc(vec, d.inc(vec))
                    dve.wait_ge(d.last, d.made(d.last))
                    for c in range(CH):
                        dve.scalar_tensor_tensor(a2("xbc", c * T, T), a2("xbc", c * T, T), p2("ssd_g", c), rstd[:, :], ALU.mult, ALU.mult)\
                            .then_inc(hf_ready if c % 2 else vec, d.inc(hf_ready if c % 2 else vec))
                if h == 2:
                    for q in range(4):
                        dve.wait_ge(yhi2_ready, d.next(yhi2_ready))
                        dve.tensor_tensor(chunk(y_lo, CH + 2 * q, 2), a2("xbc", 2 * q * T, 2 * T), chunk(y_hi, CH + 2 * q, 2).bitcast(F32), ALU.subtract)\
                            .then_inc(ylo2_ready, d.inc(ylo2_ready))
            dve.wait_ge(rsd_ready, d.next(rsd_ready))
            dve.reciprocal(rstd[0:RET_H, :], rows[0:RET_H, :]).then_inc(rrow_ready, d.inc(rrow_ready))
            gated_branch(False)
            for h in range(RET_H):
                if h % 2 == 0:
                    dve.wait_ge(rbc_ready, d.next(rbc_ready))
                for e in range(2):
                    y = ar("y", (2 * h + e) * T, T)
                    dve.tensor_tensor(y, y, bank(1 + h // 2, h % 2 * T, T), ALU.mult)\
                        .then_inc(rn_ready if e else vec, d.inc(rn_ready if e else vec))
            times_activation(lambda c: ar("y", c * T, T), 0)
            gated_branch(False)
            dve.wait_ge(d.last, d.made(d.last))
            dve.memset(small[:, 58:59], 0.0).then_inc(merged_ready, d.inc(merged_ready))
            for c in range(CH):
                dve.wait_ge(fhi_ready, d.next(fhi_ready))
                dve.tensor_tensor(chunk(f_lo, c % 2), a2("merged", c * T, T), chunk(f_hi, c % 2).bitcast(F32), ALU.subtract)\
                    .then_inc(flo_ready, d.inc(flo_ready))
            d.skip(unit_done, CH - 1)
            residual()
            norm(P2["g_ffn"])

            def ffn2(j, b):
                s = take()
                shifted_taps(chunk(pre, b), s, "ffn", j, 4, 3, cg_ready)
                s = take()
                dve.wait_ge(sil_ready, d.next(sil_ready))
                dve.tensor_tensor(chunk(mixf, b), slot(s), chunk(pre, b), ALU.mult)\
                    .then_inc(mixf_ready, d.inc(mixf_ready))
                release(2)
                feed_low(b)

            for j in range(2):
                ffn2(j, j)
            with d.loop((FF2 - 2) // RING) as i:
                for jj in range(RING):
                    ffn2(i * RING + (2 + jj), jj % 2)
                    d.skip(unit_done)
            for jj in range((FF2 - 2) % RING):
                ffn2(FF2 - (FF2 - 2) % RING + jj, jj % 2)
                d.skip(unit_done)
            d.skip(unit_done)
            residual()
            dve.wait_ge(sd_ready, d.next(sd_ready))
            dve.reciprocal(rstd[:, :], rows[:, :]).then_inc(vec, d.inc(vec))
            dve.wait_ge(d.last, d.made(d.last))
            for c in range(CH):
                dve.scalar_tensor_tensor(chunk(arena, c), chunk(x, c), p2("g_out", c), rstd[:, :], ALU.mult, ALU.mult)\
                    .then_inc(result_ready, d.inc(result_ready))


def constants():
    q = np.arange(T)
    common = np.zeros((P, NK0), np.float32)
    common[:, K0["ident"]:K0["ident"] + P] = np.eye(P)
    common[:, K0["ones"]:K0["ones"] + P] = 1.0 / D
    common[:, K0["ones256"]:K0["ones256"] + P] = 1.0 / 256
    k1 = np.zeros((P, NK1), np.float32)
    part = np.arange(P)
    for j in range(QKT):
        for h in range(2):
            k1[h * HD:(h + 1) * HD, K1["hstat"] + j * 2 * QKT + 2 * j + h] = 1.0 / HD
            k1[2 * j + h, K1["hsel"] + j * P + h * HD:K1["hsel"] + j * P + (h + 1) * HD] = 1.0
    dim = part % HD
    partner = np.where(dim < 8, part + 8, np.where(dim < 16, part - 8, part))
    k1[partner, K1["perm"] + part] = 1.0
    inv = 500000.0 ** (-np.arange(0, 16, 2) / 16.0)
    ang = np.float32(q)[None, :] * np.float32(inv)[:, None]
    cos, sin = np.ones((P, T)), np.zeros((P, T))
    for p in range(P):
        if dim[p] < 16:
            cos[p] = np.cos(ang[dim[p] % 8])
            sin[p] = np.sin(ang[dim[p] % 8]) * (-1 if dim[p] < 8 else 1)
    k1[:, K1["cos"]:K1["cos"] + T] = cos
    k1[:, K1["sin"]:K1["sin"] + T] = sin
    diff = q[:, None] - q[None, :]
    count = sum(((diff % dil == 0) & (np.abs(diff) <= w // 2)).astype(int) for w, dil in ((128, 1), (512, 4), (2048, 16)))
    dil = np.where(count > 0, np.log(np.maximum(count, 1)), NEG)
    swa = np.where(np.abs(diff) <= 128, 0.0, NEG)
    for name, m in (("dil", dil), ("swa", swa)):
        k1[:, K1[name]:K1[name] + 2 * T] = m.reshape(2, P, T).transpose(1, 0, 2).reshape(P, 2 * T)
    return common, k1


def cols(w, order):
    w = w[:, order]
    return w.reshape(CH, P, -1, P).transpose(2, 1, 0, 3).reshape(-1, P, D)


def rows_of(w):
    return w.reshape(-1, P, D)


def per_part(v):
    return v.reshape(-1, P).T


def interleave(*parts):
    return np.stack(parts, 1).reshape(-1, *parts[0].shape[1:])


def lag2(pairs, acc):
    out = []
    for j in range(len(pairs)):
        out += list(pairs[j])
        if j >= 2:
            out.append(acc[j - 2])
    return out + [acc[-2], acc[-1]]


def block1_layout(a):
    units, params, bias = [], [], []
    dc = np.arange(64)
    start = np.clip(dc - 8, 0, 48)
    inside = (dc[None, :] >= start[:, None]) & (dc[None, :] < start[:, None] + 16)
    delta = np.clip(dc[None, :] - dc[:, None] + 15, 0, 30)
    r = np.arange(4)
    dr = r[None, :] - r[:, None] + 7
    swa_heads = np.concatenate([np.arange(64) + 64 * h for h in (0, 2, 1, 3)])
    for l in range(DEPTH):
        w = a["w_in"][l]
        o = np.cumsum([0, 4096, 512, 768, 768, 256, 256])
        gate_order = np.arange(4096).reshape(4, CH, P).transpose(1, 0, 2).ravel()
        na, dil, sq, kv = o[2], o[3], o[4], o[5]
        qk = np.concatenate([na + np.arange(512), dil + np.arange(512), sq + swa_heads, kv + np.arange(128)])
        v = np.concatenate([na + 512 + np.arange(256), dil + 512 + np.arange(256), kv + 128 + np.arange(128)])
        units += [cols(w, o[1] + np.arange(512)), cols(w, qk), cols(w, v), cols(w, gate_order)]
        wb = a["w_branch"][l].copy().reshape(4, 256, D)
        wb[3] = wb[3][swa_heads]
        wb = wb.reshape(4 * 2, P, CH, P).transpose(2, 1, 0, 3).reshape(CH, P, D)
        wo = rows_of(a["w_out"][l])
        units.append(np.stack(lag2([(u,) for u in wb], wo)))
        up = cols(a["w_up"][l], np.arange(2 * 2816))
        down = rows_of(a["w_down"][l])
        units.append(np.stack(lag2([(up[j], up[FF1 + j]) for j in range(FF1)], down)))
        units.append(np.zeros((PAD1, P, D), np.float32))
        p = np.zeros((P, NP1), np.float32)

        def put(name, m):
            p[:, P1[name]:P1[name] + m.shape[1]] = m

        put("g_mix", per_part(a["g_mix"][l]))
        put("g_ffn", per_part(a["g_ffn"][l]))
        put("gate_b", per_part(a["gate_b"][l].reshape(-1)[gate_order]))
        cw = a["a_conv_w"][l]
        put("conv_w", np.concatenate([cw[:, :P].T, cw[:, P:].T], 1))
        put("conv_b", per_part(a["a_conv_b"][l]))
        put("ln_g", per_part(a["a_ln_g"][l]))
        put("ln_b", per_part(a["a_ln_b"][l]))
        gains = ["na_qn"] * 2 + ["na_kn"] * 2 + ["dil_qn"] * 2 + ["dil_kn"] * 2 + ["swa_qn"] * 2 + ["swa_kn"]
        put("qk_g", np.stack([np.tile(a[g][l], 2) for g in gains], 1))
        put("sink", np.broadcast_to(a["swa_sink"][l], (P, 4)))
        fw, fb = a["ffn_conv_w"][l].reshape(3, 2, FF1, P), a["ffn_conv_b"][l].reshape(2, FF1, P)
        ff = np.concatenate([fw, fb[None]], 0)
        put("ffn", ff.transpose(3, 2, 1, 0).reshape(P, FF1 * 8))
        params.append(p)
        b = a["na_rpb"][l][:, dr[:, :, None, None], delta[None, None, :, :]]
        b = np.where(inside[None, None, None], b, np.float32(NEG)).transpose(0, 1, 3, 2, 4).reshape(4, 2, P, T)
        bias.append(b.transpose(2, 0, 1, 3).reshape(P, 4 * 2 * T))
    return units, np.stack(params), np.stack(bias)


def constants2():
    k = np.zeros((P, NK2), np.float32)
    part, q = np.arange(P), np.arange(T)
    k[part ^ 1, K2["perm"] + part] = 1.0
    inv = np.float32(1.0) / (np.float32(10000.0) ** np.linspace(0.0, 1.0, 64, dtype=np.float32))
    ang = q.astype(np.float32)[None, :] * inv[part // 2][:, None]
    k[:, K2["cos"]:K2["cos"] + T] = np.cos(ang)
    k[:, K2["sin"]:K2["sin"] + T] = np.sin(ang) * np.where(part % 2, 1, -1)[:, None]
    back = np.concatenate([q[None, :] - part[:, None], (q[None, P:] - part[:, None] - P)], 1)
    k[:, K2["causal"]:K2["causal"] + W15] = back >= 0
    for h in range(RET_H):
        log_gamma = np.log(1.0 - 2.0 ** (-5.0 - h))
        k[:, K2["decay"] + h * W15:K2["decay"] + (h + 1) * W15] = np.where(back >= 0, np.exp(np.maximum(back, 0) * log_gamma), 0) * P ** -0.5
        k[:, K2["hot"] + h * RET_H + h] = 1.0 / (2 * P)
    for h in range(HEADS):
        k[h, K2["sel"] + h * P:K2["sel"] + (h + 1) * P] = 1.0
    return k


def block2_layout(a):
    w = a["w_in_2"][0]
    o = np.cumsum([0, 1024, 1536, 16, 1024, 1024, 512, 512, 1024, 1024, 3072])
    z, xbc, dt, ly, lx, qk, v, g, gates = (cols(w, np.arange(lo, hi)) for lo, hi in (
        (o[0], o[1]), (o[1], o[2]), (o[2], o[2] + P), (o[3], o[4]), (o[4], o[5]), (o[5], o[7]), (o[7], o[8]), (o[8], o[9]), (o[9], o[10])))
    lru = np.stack([a["lru_w_a_2"][0], a["lru_w_i_2"][0]], 1)
    lru = lru.reshape(4, 2, 2, P, 2, P).transpose(0, 3, 1, 4, 2, 5).reshape(4, P, D)
    wb = [cols(m, np.arange(D)) for m in a["w_branch_2"][0]]
    gb = [interleave(gates[n * CH:(n + 1) * CH], wb[n]) for n in range(3)]
    wo = rows_of(a["w_o_2"][0])
    up = cols(a["ffn_w_in_2"][0], np.arange(2 * 3072))
    down = rows_of(a["ffn_w_out_2"][0])
    ff = np.stack(lag2([(up[j], up[FF2 + j]) for j in range(FF2)], down))
    units = [lx, xbc, dt, lru, qk, ly, gb[1], v, z, gb[0], g, gb[2], wo, ff]
    p = np.zeros((P, NP2), np.float32)

    def put(name, m):
        p[:m.shape[0], P2[name]:P2[name] + m.shape[1]] = m

    def taps(wc, b):
        return np.concatenate([wc, b[None]], 0).reshape(len(wc) + 1, -1, P).transpose(2, 1, 0).reshape(P, -1)

    put("g_mix", per_part(a["norm_mix_2"][0]))
    put("g_ffn", per_part(a["norm_ffn_2"][0]))
    put("g_out", per_part(a["norm_final_2"]))
    put("ssd_conv", taps(a["ssd_conv_w_2"][0], a["ssd_conv_b_2"][0]))
    put("dt_bias", a["ssd_dt_bias_2"][0][:, None])
    put("a_log", a["ssd_a_log_2"][0][:, None])
    put("ssd_d", per_part(np.repeat(a["ssd_d_2"][0], 64)))
    put("ssd_g", per_part(a["ssd_norm_2"][0]))
    put("lru_conv", taps(a["lru_conv_w_2"][0], a["lru_conv_b_2"][0]))
    put("b_a", per_part(a["lru_b_a_2"][0]))
    put("b_i", per_part(a["lru_b_i_2"][0]))
    put("lam", per_part(a["lru_lambda_2"][0]))
    put("ffn", taps(a["ffn_conv_w_2"][0], a["ffn_conv_b_2"][0]))
    return units, p


def kernel(**inputs):
    import concourse.bacc as bacc
    from concourse.bass_utils import run_bass_kernel_spmd as run

    a = {k: np.asarray(v) for k, v in inputs.items()}
    units, params1, bias1 = block1_layout(a)
    units2, params2 = block2_layout(a)
    units += units2
    common, k1 = constants()
    arrays = {"x": np.ascontiguousarray(a["x"][0].T), "units": np.ascontiguousarray(np.concatenate(units)),
              "params1": params1, "bias1": np.ascontiguousarray(bias1), "common": common, "consts1": k1, "params2": params2, "consts2": constants2()}

    def build(per_trip, found):
        nc = bacc.Bacc("TRN2", target_bir_lowering=False, num_devices=1)
        t = {n: nc.dram_tensor(f"in_{n}", v.shape, mybir.dt.from_np(v.dtype), kind="ExternalInput").ap()
             for n, v in arrays.items()}
        t["out"] = nc.dram_tensor("out", (D, T), F32, kind="ExternalOutput").ap()
        program(nc, t, per_trip, found)
        return nc

    per_trip = {}
    build({}, per_trip)
    nc = build(per_trip, {})
    r = run(nc, [{f"in_{n}": v for n, v in arrays.items()}], core_ids=[0])
    return r.results[0]["out"].T[None]
```

```python
from contextlib import ExitStack, contextmanager

import numpy as np
import concourse.bass as bass
from concourse import mybir

F32 = mybir.dt.float32
F32R = mybir.dt.float32r
ALU = mybir.AluOpType
ACT = mybir.ActivationFunctionType
AX = mybir.AxisListType.X

P = 128
T = 256
D = 1024
CH = D // P
DEPTH = 2
EPS = 1e-6
NEG = -1e30
RING = 4

HD = 64
NG1 = 4
QKT = 11
VT = 5
TAPS = 31
FF1 = 2816 // P
EARLY = 12
BESIDE = (4, 4, 3, 3, 3, 3)
SCALE = 0.125
UNITS1 = 4 + QKT + VT + 4 * CH + 2 * CH + 3 * FF1
UNITS_BEFORE = 4 + QKT + VT
PAD1 = -UNITS1 % RING
SWA_TILE = 8
PIECES = [
    (0, 2, 0, 64, 2), (1, 3, 128, 64, 3),
    (4, 6, 256, 64, 4), (5, 7, 384, 64, 5),
    (8, 10, 512, 64, 6), (9, 10, 512, 64, 7)]


def columns(widths):
    at, out = 0, {}
    for name, w in widths:
        out[name] = at
        at += w
    return out, at


P1, NP1 = columns([("g_mix", CH), ("g_ffn", CH), ("gate_b", 4 * CH), ("conv_w", 2 * TAPS), ("conv_b", 2),
                   ("ln_g", 2), ("ln_b", 2), ("qk_g", QKT), ("sink", 4), ("ffn", 8 * FF1)])

SSD_T = 12
HEADS, GROUPS = 16, 2
RET_H = 4
FF2 = 3072 // P
RET_PARTS = [(), (), (0, 1), (2, 3), (4,), (5,), (6,), (7,)]
UNITS2 = CH + SSD_T + 1 + 4 + CH + CH + CH + CH + CH + 3 * 2 * CH + CH + 3 * FF2
W15 = T + T // 2
P2, NP2 = columns([("g_mix", CH), ("g_ffn", CH), ("g_out", CH), ("ssd_conv", 5 * SSD_T), ("dt_bias", 1), ("a_log", 1),
                   ("ssd_d", CH), ("ssd_g", CH), ("lru_conv", 5 * CH), ("b_a", CH), ("b_i", CH), ("lam", CH),
                   ("ffn", 4 * FF2)])
K2, NK2 = columns([("perm", P), ("cos", T), ("sin", T), ("causal", W15), ("decay", RET_H * W15),
                   ("sel", HEADS * P), ("hot", 2 * RET_H * RET_H)])
K0, NK0 = columns([("ident", P), ("ones", P), ("ones256", P)])
K1, NK1 = columns([("hstat", QKT * 2 * QKT), ("hsel", QKT * P), ("perm", P), ("cos", T), ("sin", T),
                   ("dil", 2 * T), ("swa", 2 * T)])


STEP = {}


class Desk:

    def __init__(self, eng, name, per_trip, found):
        self.eng, self.name, self.per_trip, self.found = eng, name, per_trip, found
        self.n, self.loops, self.n_loops, self.last = {}, [], 0, None

    def value(self, sem, role, back=0):
        v = self.n.get((sem.name, role), 0) - back
        for reg, loop in self.loops:
            per = self.per_trip.get((loop, sem.name, role), 0)
            if per:
                v = reg * per + v
        return v

    def skip(self, sem, k=1, role="wait"):
        self.n[(sem.name, role)] = self.n.get((sem.name, role), 0) + k * STEP.get(sem.name, 1)

    def next(self, sem, k=1, role="wait"):
        self.skip(sem, k, role)
        return self.value(sem, role)

    def inc(self, sem, k=1):
        self.skip(sem, k, "made")
        self.last = sem
        return k * STEP.get(sem.name, 1)

    def made(self, sem, back=0):
        return self.value(sem, "made", back)

    @contextmanager
    def loop(self, trips):
        loop = (self.name, self.n_loops)
        self.n_loops += 1
        before = dict(self.n)
        with self.eng.Fori(0, trips) as i:
            self.loops.append((i, loop))
            yield i
            self.loops.pop()
        for key, n in self.n.items():
            per = n - before.get(key, 0)
            self.found[(loop, *key)] = per
            self.n[key] = before.get(key, 0) + trips * per


def program(nc, t, per_trip, found, blocks=3):
    with ExitStack() as ctx:
        def sb(name, n, dt=F32):
            return ctx.enter_context(nc.sbuf_tensor(name, [P, n], dt))

        def signal(name, step=1):
            sem = ctx.enter_context(nc.semaphore(name))
            STEP[sem.name] = step
            return sem

        raw = [sb(f"raw{s}", D) for s in range(RING)]
        w_hi = [sb(f"w_hi{s}", D, F32R) for s in range(RING)]
        w_lo = [sb(f"w_lo{s}", D, F32R) for s in range(RING)]
        h_hi, h_lo = sb("h_hi", CH * T, F32R), sb("h_lo", CH * T, F32R)
        y_hi, y_lo = sb("y_hi", 2 * CH * T, F32R), sb("y_lo", 2 * CH * T, F32R)
        f_hi, f_lo = sb("f_hi", 2 * T, F32R), sb("f_lo", 2 * T, F32R)
        zero = sb("zero", T, F32R)
        x = sb("x", CH * T)
        common = sb("common", NK0)
        A1, NA1 = columns([("gates", 4 * CH * T), ("qk", QKT * T), ("v", 2 * VT * P), ("u", 2 * (T + TAPS - 1)),
                           ("conv", 2 * T), ("sg", 2 * T), ("sc", 4 * 2 * T), ("pts", 2 * 2 * T),
                           ("consts", NK1), ("bias", 4 * 2 * T)])
        A2, NA2 = columns([("xb", CH * T), ("r", CH * T), ("i", CH * T), ("qk", CH * T), ("xbc", SSD_T * T),
                           ("xdt", 2 * D), ("cb", GROUPS * W15), ("seg", 3 * W15), ("dt", 2 * T), ("tab", 4 * HEADS),
                           ("merged", CH * T), ("consts", NK2)])
        A2R, _ = columns([("v", 2 * D), ("y", CH * T), ("p", 2 * W15)])
        arena = sb("arena", max(NA1, NA2))
        rows, rstd = sb("rows", T), sb("rstd", T)
        small = sb("small", 64)
        pre = sb("pre", 4 * T)
        mixf = sb("mixf", 2 * T)
        prm = sb("prm", max(NP1, NP2))
        psum = ctx.enter_context(nc.psum_tensor("psum", [P, 8 * 512], F32))

        def a1(name, lo, n):
            return arena[:, A1[name] + lo:A1[name] + lo + n]

        def a2(name, lo, n, parts=P, table=A2):
            lo = lo + table[name]
            return arena[0:parts, lo:lo + n] if isinstance(lo, int) else arena[0:parts, bass.ds(lo, n)]

        def ar(name, lo, n, parts=P):
            return a2(name, lo, n, parts, A2R)

        def c2(name, lo, n, parts=P):
            return a2("consts", K2[name] + lo, n, parts)

        def p2(name, lo=0, n=1, parts=P):
            lo = lo + P2[name]
            return prm[0:parts, lo:lo + n] if isinstance(lo, int) else prm[0:parts, bass.ds(lo, n)]

        def seg(h):
            return a2("seg", h % 4 * W15, W15) if h % 4 < 3 else pre[:, 0:W15]

        def ck(name, lo, n, parts=P):
            return arena[0:parts, A1["consts"] + K1[name] + lo:A1["consts"] + K1[name] + lo + n]

        def bank(b, lo=0, n=512):
            return psum[:, b * 512 + lo:b * 512 + lo + n]

        def slot(s):
            return bank(4 + s, 0, T)

        def acc(f):
            return psum[:, f * T:(f + 1) * T]

        ident, ones, ones256 = (common[:, K0[n]:K0[n] + P] for n in ("ident", "ones", "ones256"))

        def chunk(buf, c, n=1):
            return buf[:, c * T:(c + n) * T] if isinstance(c, int) else buf[:, bass.ds(c * T, n * T)]

        raw_full = [signal(f"raw_full{s}", 16) for s in range(RING)]
        hi_ready, lo_ready = signal("hi_ready"), signal("lo_ready")
        unit_done = signal("unit_done")
        slot_free = signal("slot_free")
        gate_free = signal("gate_free")
        x_in = [signal(f"x_in{q}", 16) for q in range(4)]
        loaded, consts1_full = signal("loaded", 16), signal("consts1_full", 16)
        params_full = signal("params_full", 16)
        bias_full = signal("bias_full", 16)
        init = signal("init")
        vec, act_own = signal("vec"), signal("act_own")
        gate_done = signal("gate_done")
        acc_done = signal("acc_done")
        x_ready, sq_ready, stat_ready = signal("x_ready"), signal("sq_ready"), signal("stat_ready")
        sd_ready, hf_ready = signal("sd_ready"), signal("hf_ready")
        hhi_ready, hlo_ready = signal("hhi_ready"), signal("hlo_ready")
        sg_ready, qsq_ready, qr_ready = signal("sg_ready"), signal("qsq_ready"), signal("qr_ready")
        bc_ready, qn_ready, pm_ready, rope_ready = (signal(n) for n in ("bc_ready", "qn_ready", "pm_ready", "rope_ready"))
        conv_ready, mean_ready = signal("conv_ready"), signal("mean_ready")
        s_ready, s_free, negm_ready, exp_ready = (signal(n) for n in ("s_ready", "s_free", "negm_ready", "exp_ready"))
        p_ready, pt_ready, pts_ready, o_ready = (signal(n) for n in ("p_ready", "pt_ready", "pts_ready", "o_ready"))
        yhi_ready, ylo_ready = signal("yhi_ready"), signal("ylo_ready")
        gsig_ready, mixf_ready = signal("gsig_ready"), signal("mixf_ready")
        fhi_ready, flo_ready = signal("fhi_ready"), signal("flo_ready")
        pre_ready, cg_ready, sil_ready = signal("pre_ready"), signal("cg_ready"), signal("sil_ready")
        consts2_full = signal("consts2_full", 16)
        soft_in, soft_exp, coef_ready = signal("soft_in"), signal("soft_exp"), signal("coef_ready")
        conv_done, ri_ready, at_ready, m2_ready, root_ready = (
            signal(n) for n in ("conv_done", "ri_ready", "at_ready", "m2_ready", "root_ready"))
        acs_ready, turn_ready, xt_ready, xdt_ready = (signal(n) for n in ("acs_ready", "turn_ready", "xt_ready", "xdt_ready"))
        silu_ready, cb_ready, cbm_ready, ea_ready = (signal(n) for n in ("silu_ready", "cb_ready", "cbm_ready", "ea_ready"))
        seg_bc, seg_ready, dec_ready, m_ready, yh_ready, ys_ready = (
            signal(n) for n in ("seg_bc", "seg_ready", "dec_ready", "m_ready", "yh_ready", "ys_ready"))
        pm2_ready, rot_ready = signal("pm2_ready"), signal("rot_ready")
        act_out, prod_ready, yhi2_ready, ylo2_ready = (signal(n) for n in ("act_out", "prod_ready", "yhi2_ready", "ylo2_ready"))
        v_ready, rs_ready, rp_ready, ry_ready, ryf_ready, rsq_ready = (
            signal(n) for n in ("v_ready", "rs_ready", "rp_ready", "ry_ready", "ryf_ready", "rsq_ready"))
        rstat_ready, rsd_ready, rrow_ready, rbc_ready, rn_ready = (
            signal(n) for n in ("rstat_ready", "rsd_ready", "rrow_ready", "rbc_ready", "rn_ready"))
        merged_ready, result_ready = signal("merged_ready"), signal("result_ready")
        stored = signal("stored", 16)

        total_units = t["units"].shape[0]
        block = ctx.enter_context(nc.Block())

        @block.sync
        def _(sp):
            d = Desk(sp, "sp", per_trip, found)
            sp.dma_start(common[:, :], t["common"]).then_inc(loaded, d.inc(loaded))
            for q in range(4):
                sp.dma_start(chunk(x, 2 * q, 2).rearrange("p (c t) -> p c t", c=2),
                             t["x"].rearrange("(c p) t -> p c t", p=P)[:, 2 * q:2 * q + 2, :]).then_inc(x_in[q], d.inc(x_in[q]))
            for s in range(RING):
                sp.dma_start(raw[s][:, :], t["units"][s]).then_inc(raw_full[s], d.inc(raw_full[s]))

            def load(index, s):
                sp.wait_ge(hi_ready, d.next(hi_ready))
                sp.wait_ge(lo_ready, d.next(lo_ready))
                sp.dma_start(raw[s][:, :], t["units"][bass.ds(index, 1)].rearrange("a p c -> p (a c)"))\
                    .then_inc(raw_full[s], d.inc(raw_full[s]))

            for s in range(RING):
                load(RING + s, s)
            sp.dma_start(arena[:, A1["consts"]:A1["consts"] + NK1], t["consts1"]).then_inc(consts1_full, d.inc(consts1_full))
            with d.loop(total_units // RING - 2) as i:
                for s in range(RING):
                    load(i * RING + (2 * RING + s), s)
            for u in range(total_units - total_units % RING, total_units):
                load(u, u % RING)
            for q in range(4):
                sp.wait_ge(result_ready, d.next(result_ready, 2))
                sp.dma_start(t["out"].rearrange("(c p) t -> p c t", p=P)[:, 2 * q:2 * q + 2, :],
                                    chunk(arena, 2 * q, 2).rearrange("p (c t) -> p c t", c=2))\
                                        .then_inc(stored, d.inc(stored))
            sp.wait_ge(stored, d.made(stored))

        @block.gpsimd
        def _(pool):
            d = Desk(pool, "pool", per_trip, found)

            def low(s):
                pool.wait_ge(raw_full[s], d.next(raw_full[s]))
                pool.wait_ge(hi_ready, d.next(hi_ready))
                pool.wait_ge(unit_done, d.next(unit_done, 1, "slot"))
                pool.tensor_tensor(w_lo[s][:, :], raw[s][:, :], w_hi[s][:, :].bitcast(F32), ALU.subtract)\
                    .then_inc(lo_ready, d.inc(lo_ready))

            with d.loop(total_units // RING) as _:
                for s in range(RING):
                    low(s)
            for s in range(total_units % RING):
                low(s)

        @block.scalar
        def _(act):
            d = Desk(act, "act", per_trip, found)
            units_hi = [0]

            def high(n=1):
                for _ in range(n):
                    if not d.loops and d.n.get((hi_ready.name, "made"), 0) >= total_units:
                        return
                    s = units_hi[0] % RING
                    units_hi[0] += 1
                    act.wait_ge(raw_full[s], d.next(raw_full[s]))
                    act.wait_ge(unit_done, d.next(unit_done, 1, "slot"))
                    act.activation(w_hi[s][:, :], raw[s][:, :], ACT.Copy).then_inc(hi_ready, d.inc(hi_ready))

            def norm(load, ahead=0):
                act.activation(small[:, 57:58], small[:, 60:61], ACT.Sqrt)
                for q in range(4):
                    act.wait_ge(x_ready, d.next(x_ready))
                    act.activation(chunk(arena, 2 * q, 2), chunk(x, 2 * q, 2), ACT.Square)\
                        .then_inc(sq_ready, d.inc(sq_ready))
                load()
                act.wait_ge(stat_ready, d.next(stat_ready))
                act.activation(rows[:, :], bank(0, 0, T), ACT.Sqrt, bias=small[:, 60:61])\
                    .then_inc(sd_ready, d.inc(sd_ready))
                high(ahead)
                for q in range(4):
                    act.wait_ge(hf_ready, d.next(hf_ready))
                    act.activation(chunk(h_hi, 2 * q, 2), chunk(arena, 2 * q, 2), ACT.Copy)\
                        .then_inc(hhi_ready, d.inc(hhi_ready))

            def exps(p):
                q_tile = PIECES[p][0]
                for h in range(2):
                    sc = a1("sc", (2 * (p % 2) + h) * 512, 512)
                    act.wait_ge(negm_ready, d.next(negm_ready))
                    c = 8 * h
                    for r in range(2):
                        last = act.activation(sc[:, r * T:(r + 1) * T], sc[:, r * T:(r + 1) * T], ACT.Exp,
                                              bias=small[:, c + 2 + r:c + 3 + r], accum_out=small[:, c + 4 + r:c + 5 + r])
                        if r == 0:
                            last.then_inc(act_own, d.inc(act_own))
                    if q_tile >= SWA_TILE:
                        last.then_inc(act_own, d.inc(act_own))
                        head = q_tile - SWA_TILE + 2 * h
                        last = act.activation(small[:, c + 6:c + 8], small[:, c + 2:c + 4], ACT.Exp,
                                              bias=prm[:, P1["sink"] + head:P1["sink"] + head + 1])
                    last.then_inc(exp_ready, d.inc(exp_ready))

            def outputs(p):
                for h in range(2):
                    act.wait_ge(pt_ready, d.next(pt_ready))
                    act.activation(a1("pts", h * 512, 512), bank(h), ACT.Copy).then_inc(pts_ready, d.inc(pts_ready))
                act.wait_ge(o_ready, d.next(o_ready))
                act.activation(chunk(y_hi, PIECES[p][4]), bank(0, 0, T), ACT.Copy)\
                    .then_inc(yhi_ready, d.inc(yhi_ready))

            d.skip(unit_done, RING)
            act.wait_ge(init, d.next(init))
            with d.loop(DEPTH) as layer:
                def load_params1():
                    act.dma_start(prm[:, :], t["params1"][bass.ds(layer, 1)].rearrange("a p c -> p (a c)"))\
                        .then_inc(params_full, d.inc(params_full))
                    high()

                norm(load_params1, RING - 2)
                act.dma_start(a1("bias", 0, 4 * 2 * T), t["bias1"][bass.ds(layer, 1)].rearrange("a p c -> p (a c)"))\
                    .then_inc(bias_full, d.inc(bias_full))
                high(2)
                d.skip(unit_done, 2)
                for k in range(2):
                    high()
                    act.wait_ge(unit_done, d.next(unit_done))
                    act.activation(a1("sg", k * T, T), slot(2 + k), ACT.Sigmoid).then_inc(sg_ready, d.inc(sg_ready))
                for k in range(QKT):
                    high()
                    act.wait_ge(unit_done, d.next(unit_done))
                    act.activation(a1("gates", (8 + k) * T, T), slot(k % RING), ACT.Square)\
                        .then_inc(qsq_ready, d.inc(qsq_ready))
                for k in range(VT):
                    high()
                d.skip(unit_done, VT)
                act.wait_ge(stat_ready, d.next(stat_ready))
                act.activation(rows[0:2 * QKT, :], psum[0:2 * QKT, 0:T], ACT.Sqrt,
                                      bias=small[0:2 * QKT, 60:61]).then_inc(sd_ready, d.inc(sd_ready))
                for g in range(EARLY):
                    high()
                    act.wait_ge(unit_done, d.next(unit_done))
                    act.activation(a1("gates", g * T, T), slot((UNITS_BEFORE + g) % RING), ACT.Sigmoid,
                                   bias=prm[:, P1["gate_b"] + g:P1["gate_b"] + g + 1]).then_inc(gate_free, d.inc(gate_free))
                high()
                exps(0)
                act.wait_ge(hf_ready, d.next(hf_ready))
                act.activation(a1("sg", 0, 2 * T), a1("conv", 0, 2 * T), ACT.Square)\
                    .then_inc(sq_ready, d.inc(sq_ready))
                act.activation(small[:, 57:58], small[:, 60:61], ACT.Sqrt)
                high()
                act.wait_ge(stat_ready, d.next(stat_ready))
                act.activation(rows[:, :], bank(1, T, T), ACT.Sqrt, bias=small[:, 60:61])\
                    .then_inc(sd_ready, d.inc(sd_ready))
                act.activation(small[:, 61:62], small[:, 60:61], ACT.Silu)
                high(2)
                for k in range(2):
                    act.wait_ge(hf_ready, d.next(hf_ready))
                    act.activation(a1("sg", k * T, T), a1("conv", k * T, T), ACT.Silu,
                                          bias=prm[:, P1["ln_b"] + k:P1["ln_b"] + k + 1])\
                                              .then_inc(act_own, d.inc(act_own))
                act.wait_ge(d.last, d.made(d.last))
                act.activation(chunk(y_hi, 0, 2), a1("sg", 0, 2 * T), ACT.Copy)\
                    .then_inc(yhi_ready, d.inc(yhi_ready))
                d.skip(unit_done, BESIDE[0])
                outputs(0)

                def gate_sigmoid(c):
                    act.activation(a1("gates", c * 4 * T, 4 * T), a1("gates", c * 4 * T, 4 * T), ACT.Sigmoid)\
                        .then_inc(gsig_ready, d.inc(gsig_ready))

                for p in range(1, len(PIECES)):
                    high()
                    exps(p)
                    high(BESIDE[p] - 1)
                    d.skip(unit_done, BESIDE[p])
                    outputs(p)

                def feed_high(b):
                    act.wait_ge(mixf_ready, d.next(mixf_ready))
                    act.activation(chunk(f_hi, b), chunk(mixf, b), ACT.Copy).then_inc(fhi_ready, d.inc(fhi_ready))

                for c in range(CH):
                    high()
                    d.skip(unit_done)
                    if c >= 2:
                        high()
                        act.wait_ge(unit_done, d.next(unit_done))
                    feed_high(c % 2)
                    if c + EARLY // 4 < CH:
                        gate_sigmoid(c + EARLY // 4)
                high(2)
                d.skip(unit_done, 2)
                norm(lambda: None)

                def ffn_act(j, b):
                    for k in range(2):
                        high()
                        act.wait_ge(unit_done, d.next(unit_done))
                        cols = P1["ffn"] + 4 * k
                        at = (lambda o: prm[:, bass.ds(j * 8 + (cols + o), 1)])
                        act.activation(pre[:, (2 * b + k) * T:(2 * b + k + 1) * T], slot(2 * b + k), ACT.Identity,
                                              scale=at(1), bias=at(3)).then_inc(pre_ready, d.inc(pre_ready))

                def ffn_gate(b):
                    act.wait_ge(cg_ready, d.next(cg_ready))
                    act.activation(pre[:, 2 * b * T:(2 * b + 1) * T], pre[:, 2 * b * T:(2 * b + 1) * T], ACT.Silu)\
                        .then_inc(sil_ready, d.inc(sil_ready))

                for j in range(2):
                    ffn_act(j, j)
                    ffn_gate(j)
                    feed_high(j)
                with d.loop((FF1 - 2) // RING) as i:
                    for jj in range(RING):
                        ffn_act(i * RING + (2 + jj), jj % 2)
                        high()
                        ffn_gate(jj % 2)
                        act.wait_ge(unit_done, d.next(unit_done))
                        feed_high(jj % 2)
                high(2 + PAD1 - (RING - 1))
                d.skip(unit_done, 2 + PAD1)

            slots = [0]

            def next_slot():
                slots[0] += 1
                return (slots[0] - 1) % RING

            def take():
                high()
                act.wait_ge(unit_done, d.next(unit_done))
                return next_slot()

            def middle_tap(dst, tap, bias):
                s = take()
                act.wait_ge(init, 1)
                act.activation(dst, slot(s), ACT.Identity, scale=tap, bias=bias)\
                    .then_inc(pre_ready, d.inc(pre_ready))

            def softplus_exp(n, parts):
                act.wait_ge(soft_in, d.next(soft_in))
                e = small[:, 16:16 + n] if n == CH else rows[0:parts, :]
                act.activation(e, e, ACT.Exp).then_inc(soft_exp, d.inc(soft_exp))

            def parts_high(buf, c, src):
                act.wait_ge(init, 1)
                act.activation(chunk(y_hi, buf * CH + c), src, ACT.Copy).then_inc(yhi2_ready, d.inc(yhi2_ready))

            def load_params2():
                act.dma_start(prm[:, 0:NP2], t["params2"]).then_inc(params_full, d.inc(params_full))
                high()

            norm(load_params2, RING - 2)
            act.dma_start(a2("consts", 0, NK2), t["consts2"]).then_inc(consts2_full, d.inc(consts2_full))
            softplus_exp(CH, P)
            for c in range(CH):
                middle_tap(a2("xb", c * T, T), p2("lru_conv", c * 5 + 3), p2("lru_conv", c * 5 + 4))
                if c:
                    act.wait_ge(conv_done, d.next(conv_done))
                    parts_high(1, c - 1, a2("xb", (c - 1) * T, T))
            high()
            d.skip(unit_done, 1)
            next_slot()
            act.wait_ge(conv_done, d.next(conv_done))
            parts_high(1, CH - 1, a2("xb", (CH - 1) * T, T))
            softplus_exp(T, HEADS)
            act.activation(small[0:HEADS, 58:59], p2("a_log", 0, 1, HEADS), ACT.Exp)\
                .then_inc(ea_ready, d.inc(ea_ready))
            for c in range(SSD_T + 1):
                if c < SSD_T:
                    middle_tap(a2("xbc", c * T, T), p2("ssd_conv", c * 5 + 3), p2("ssd_conv", c * 5 + 4))
                if c:
                    act.wait_ge(conv_done, d.next(conv_done))
                    act.activation(a2("xbc", (c - 1) * T, T), a2("xbc", (c - 1) * T, T), ACT.Silu)\
                        .then_inc(silu_ready, d.inc(silu_ready))
            for b in range(4):
                for k in range(4):
                    if k < 3:
                        act.wait_ge(gate_done, d.next(gate_done))
                    else:
                        act.wait_ge(unit_done, d.next(unit_done))
                    name, bias, c = (("r", "b_a"), ("i", "b_i"))[k // 2] + (2 * b + k % 2,)
                    act.activation(a2(name, c * T, T), slot(next_slot()), ACT.Sigmoid, bias=p2(bias, c))\
                        .then_inc(ri_ready, d.inc(ri_ready))
                high(2)
                d.skip(unit_done)
                next_slot()
            act.wait_ge(coef_ready, d.next(coef_ready))
            for c in range(CH):
                if c < RING:
                    high()
                    d.skip(unit_done)
                    next_slot()
                if c % 2 == 0:
                    act.wait_ge(conv_done, d.next(conv_done))
                act.wait_ge(ri_ready, d.made(ri_ready))
                act.activation(a2("xb", c * T, T), a2("r", c * T, T), ACT.Exp, scale=small[:, 24 + c:25 + c])\
                    .then_inc(act_own, d.inc(act_own))
                act.activation(a2("r", c * T, T), a2("r", c * T, T), ACT.Tanh, scale=small[:, 32 + c:33 + c])\
                    .then_inc(at_ready, d.inc(at_ready))
            act.wait_ge(m2_ready, d.next(m2_ready))
            for q in range(4):
                if q:
                    act.wait_ge(m2_ready, d.next(m2_ready))
                act.activation(a2("r", 2 * q * T, 2 * T), a2("r", 2 * q * T, 2 * T), ACT.Sqrt)\
                    .then_inc(root_ready, d.inc(root_ready))

            def gated_branch():
                with d.loop(CH // RING * 2) as _:
                    for k in range(2):
                        act.activation(chunk(pre, k), slot(take()), ACT.Sigmoid).then_inc(act_out, d.inc(act_out))
                        high()
                        d.skip(unit_done)
                        next_slot()

            for c in range(CH + 2):
                if c < CH:
                    act.activation(chunk(pre, c % RING), slot(take()), ACT.Gelu_apprx_tanh).then_inc(act_out, d.inc(act_out))
                if c >= 2:
                    act.wait_ge(prod_ready, d.next(prod_ready))
                    parts_high(0, c - 2, chunk(mixf, c % 2))
            gated_branch()
            for h in range(HEADS):
                act.wait_ge(seg_ready, d.next(seg_ready))
                act.activation(seg(h), seg(h), ACT.Exp).then_inc(dec_ready, d.inc(dec_ready))
                if h % 2 == 0:
                    high()
                    d.skip(unit_done)
                    next_slot()
            for c in range(CH):
                act.activation(chunk(pre, (c + 2) % RING), slot(take()), ACT.Silu).then_inc(act_out, d.inc(act_out))
                if c:
                    act.wait_ge(prod_ready, d.next(prod_ready))
                    act.activation(a2("seg", (c - 1) % 4 * T, T), a2("xbc", (c - 1) * T, T), ACT.Square)\
                        .then_inc(sq_ready, d.inc(sq_ready))
            act.wait_ge(prod_ready, d.next(prod_ready))
            act.activation(a2("seg", (CH - 1) % 4 * T, T), a2("xbc", (CH - 1) * T, T), ACT.Square)\
                .then_inc(sq_ready, d.inc(sq_ready))

            def head_square(h):
                act.wait_ge(ryf_ready, d.next(ryf_ready))
                act.activation(a2("seg", h % 2 * 2 * T, 2 * T), ar("y", 2 * h * T, 2 * T), ACT.Square)\
                    .then_inc(rsq_ready, d.inc(rsq_ready))

            for h in range(RET_H):
                for c in (2 * h, 2 * h + 1):
                    act.activation(a2("xdt", c * T, T), slot(take()), ACT.Silu).then_inc(act_out, d.inc(act_out))
                if h == 0:
                    act.wait_ge(stat_ready, d.next(stat_ready))
                    act.activation(rows[:, :], bank(0, 0, T), ACT.Sqrt, bias=small[:, 60:61])\
                        .then_inc(sd_ready, d.inc(sd_ready))
                if h >= 2:
                    head_square(h - 2)
                if h in (1, 2):
                    for q in (2 * h - 2, 2 * h - 1):
                        act.wait_ge(hf_ready, d.next(hf_ready))
                        act.activation(chunk(y_hi, CH + 2 * q, 2), a2("xbc", 2 * q * T, 2 * T), ACT.Copy)\
                            .then_inc(yhi2_ready, d.inc(yhi2_ready))
            head_square(RET_H - 2)
            head_square(RET_H - 1)
            for c in range(CH):
                s = take()
                if c == 0:
                    act.wait_ge(rstat_ready, d.next(rstat_ready))
                    act.activation(rows[0:RET_H, :], psum[0:RET_H, 3 * 512:3 * 512 + T], ACT.Sqrt, bias=small[0:RET_H, 60:61])\
                        .then_inc(rsd_ready, d.inc(rsd_ready))
                act.activation(chunk(pre, c % 2), slot(s), ACT.Sigmoid).then_inc(act_out, d.inc(act_out))
                high()
                d.skip(unit_done)
                next_slot()
                for y in RET_PARTS[c]:
                    act.wait_ge(prod_ready, d.next(prod_ready))
                    act.activation(chunk(y_hi, y), ar("y", y * T, T), ACT.Copy).then_inc(yhi2_ready, d.inc(yhi2_ready))

            def merged_high(c):
                act.wait_ge(merged_ready, d.next(merged_ready))
                act.activation(chunk(y_hi, CH + c), a2("merged", c * T, T), ACT.Copy)\
                    .then_inc(yhi2_ready, d.inc(yhi2_ready))

            for c in range(CH):
                act.activation(chunk(pre, c % 2), slot(take()), ACT.Sigmoid).then_inc(act_out, d.inc(act_out))
                high()
                d.skip(unit_done)
                next_slot()
                if c:
                    merged_high(c - 1)
            merged_high(CH - 1)
            high(CH)
            d.skip(unit_done, CH)
            norm(lambda: None)

            def ffn2(j, b):
                s = take()
                act.wait_ge(init, 1)
                act.activation(chunk(pre, b), slot(s), ACT.Identity, scale=p2("ffn", j * 4 + 2), bias=p2("ffn", j * 4 + 3))\
                    .then_inc(pre_ready, d.inc(pre_ready))
                high()
                next_slot()
                act.wait_ge(cg_ready, d.next(cg_ready))
                act.activation(chunk(pre, b), chunk(pre, b), ACT.Gelu_apprx_tanh)\
                    .then_inc(sil_ready, d.inc(sil_ready))

            for j in range(2):
                ffn2(j, j)
                d.skip(unit_done)
                feed_high(j)
            with d.loop((FF2 - 2) // RING) as i:
                for jj in range(RING):
                    ffn2(i * RING + (2 + jj), jj % 2)
                    high()
                    d.skip(unit_done)
                    act.wait_ge(unit_done, d.next(unit_done))
                    feed_high(jj % 2)
            for jj in range((FF2 - 2) % RING):
                ffn2(FF2 - (FF2 - 2) % RING + jj, jj % 2)
                if jj == 0:
                    high()
                d.skip(unit_done)
                act.wait_ge(unit_done, d.next(unit_done))
                feed_high(jj % 2)
            act.activation(small[:, 57:58], small[:, 60:61], ACT.Sqrt)
            for q in range(4):
                act.wait_ge(x_ready, d.next(x_ready))
                act.activation(chunk(arena, 2 * q, 2), chunk(x, 2 * q, 2), ACT.Square)\
                    .then_inc(sq_ready, d.inc(sq_ready))
            act.wait_ge(stat_ready, d.next(stat_ready))
            act.activation(rows[:, :], bank(0, 0, T), ACT.Sqrt, bias=small[:, 60:61])\
                .then_inc(sd_ready, d.inc(sd_ready))

        @block.tensor
        def _(pe):
            d = Desk(pe, "pe", per_trip, found)
            n_units, n_slots = [0], [0]

            def next_slot():
                s = n_slots[0] % RING
                n_slots[0] += 1
                return s

            def mm3(out, hi, lo, r_hi, r_lo, start, stop, **kw):
                pe.matmul(out, hi, r_hi, start=start, stop=False, **kw)
                pe.matmul(out, lo, r_hi, start=False, stop=False, **kw)
                return pe.matmul(out, hi, r_lo, start=False, stop=stop, **kw)

            def blocks_of(w, k):
                return w[:, k * P:(k + 1) * P]

            def unit():
                s = n_units[0] % RING
                n_units[0] += 1
                pe.wait_ge(lo_ready, d.next(lo_ready))
                return s

            def linear_unit(src_hi, src_lo, first=None, free=slot_free):
                s = unit()
                o = slot(next_slot())
                pe.wait_ge(free, d.next(free))
                for c in range(CH):
                    if first is not None and c % 2 == 0:
                        pe.wait_ge(first, d.next(first))
                    last = mm3(o, blocks_of(w_hi[s], c), blocks_of(w_lo[s], c), chunk(src_hi, c), chunk(src_lo, c),
                               c == 0, c == CH - 1)
                last.then_inc(unit_done, d.inc(unit_done))

            pair = []

            def value_part(part):
                s = unit()
                if part == 0:
                    pe.wait_ge(slot_free, d.next(slot_free, 2))
                    pair[:] = [next_slot(), next_slot()]
                for half in range(2):
                    for c in range(CH // 2):
                        lo = (part * (CH // 2) + c) * T + half * P
                        last = mm3(slot(pair[half]), h_hi[:, lo:lo + P], h_lo[:, lo:lo + P],
                                   w_hi[s][:, c * T:(c + 1) * T], w_lo[s][:, c * T:(c + 1) * T],
                                   part == 0 and c == 0, part == 1 and c == CH // 2 - 1)
                last.then_inc(unit_done, d.inc(unit_done))

            def value_unit():
                s = unit()
                o = slot(next_slot())
                pe.wait_ge(slot_free, d.next(slot_free))
                for half in range(2):
                    for c in range(CH):
                        lo = c * T + half * P
                        last = mm3(o[:, half * P:(half + 1) * P], h_hi[:, lo:lo + P], h_lo[:, lo:lo + P],
                                   blocks_of(w_hi[s], c), blocks_of(w_lo[s], c), c == 0, c == CH - 1)
                last.then_inc(unit_done, d.inc(unit_done))

            def zero_acc():
                for b in range(4):
                    for k in range(2):
                        pe.matmul(bank(b, k * T, T), zero[:, 0:P], zero[:, :], start=(k == 0), stop=(k == 1), skip_group_check=True)

            def acc_unit(b, pads=0, final=False):
                s = unit()
                pe.wait_ge(flo_ready, d.next(flo_ready))
                for f in range(CH):
                    last = mm3(acc(f), blocks_of(w_hi[s], f), blocks_of(w_lo[s], f), chunk(f_hi, b), chunk(f_lo, b),
                               False, f == CH - 1, skip_group_check=True)
                    if final and f in (1, 3, 5):
                        last.then_inc(acc_done, d.inc(acc_done))
                d.skip(lo_ready, pads)
                n_units[0] += pads
                last.then_inc(unit_done, d.inc(unit_done, 1 + pads))

            def keep_warm(n):
                with d.loop(n // 8) as _:
                    for _ in range(8):
                        pe.matmul(bank(1, 0, T), zero[:, 0:P], zero[:, :], start=True, stop=True)

            def norm_stats(warm=48):
                for q in range(4):
                    pe.wait_ge(sq_ready, d.next(sq_ready))
                    for c in (2 * q, 2 * q + 1):
                        last = pe.matmul(bank(0, 0, T), ones, chunk(arena, c), start=(c == 0), stop=(c == CH - 1))
                last.then_inc(stat_ready, d.inc(stat_ready))
                if warm:
                    keep_warm(warm)

            def scores(p):
                q_tile, k_tile = PIECES[p][:2]
                if p:
                    pe.wait_ge(s_free, d.next(s_free, 2))
                for h in range(2):
                    lo, hi = h * HD, (h + 1) * HD
                    for r in range(2):
                        at = A1["qk"] + q_tile * T + r * P
                        ak = A1["qk"] + k_tile * T
                        last = pe.matmul(bank(2 + h, r * T, T), arena[lo:hi, at:at + P], arena[lo:hi, ak:ak + T],
                                         start=True, stop=True)
                    last.then_inc(s_ready, d.inc(s_ready))
                if p == len(PIECES) - 1:
                    d.skip(s_free, 2)

            def attend(p):
                v0, step = PIECES[p][2:4]
                pe.wait_ge(yhi_ready, d.next(yhi_ready))
                pe.wait_ge(ylo_ready, d.next(ylo_ready))
                for h in range(2):
                    pe.wait_ge(p_ready, d.next(p_ready))
                    sc = a1("sc", (2 * (p % 2) + h) * 512, 512)
                    for kc in range(2):
                        for r in range(2):
                            last = pe.transpose(bank(h, kc * T + r * P, P), sc[:, r * T + kc * P:r * T + (kc + 1) * P], ident)
                    last.then_inc(pt_ready, d.inc(pt_ready))
                if p < len(PIECES) - 1:
                    scores(p + 1)
                for h in range(2):
                    pe.wait_ge(pts_ready, d.next(pts_ready))
                    for kc in range(2):
                        av = A1["v"] + kc * VT * P + v0 + h * step
                        last = pe.matmul(psum[h * HD:(h + 1) * HD, 0:T], arena[:, av:av + HD],
                                         a1("pts", h * 512 + kc * T, T), start=(kc == 0), stop=(kc == 1))
                last.then_inc(o_ready, d.inc(o_ready))

            pe.wait_ge(init, d.next(init))
            keep_warm(16)
            pe.wait_ge(loaded, d.next(loaded))
            pe.sem_inc(unit_done, RING)
            with d.loop(DEPTH) as _:
                norm_stats()
                linear_unit(h_hi, h_lo, hlo_ready)
                for _ in range(3):
                    linear_unit(h_hi, h_lo)
                with d.loop(2) as _:
                    for _ in range(RING):
                        linear_unit(h_hi, h_lo)
                for _ in range(QKT - 2 * RING):
                    linear_unit(h_hi, h_lo)
                for j in range(VT - 1):
                    value_part(j % 2)
                value_unit()
                pe.wait_ge(consts1_full, 16)
                pe.wait_ge(qsq_ready, d.next(qsq_ready, QKT))
                for j in range(QKT):
                    last = pe.matmul(psum[0:2 * QKT, 0:T], ck("hstat", j * 2 * QKT, 2 * QKT),
                                     a1("gates", (8 + j) * T, T), start=(j == 0), stop=(j == QKT - 1))
                last.then_inc(stat_ready, d.inc(stat_ready))
                for _ in range(RING):
                    linear_unit(h_hi, h_lo)
                def spread(tiles):
                    for b in range(4):
                        for j in tiles[2 * b:2 * b + 2]:
                            last = pe.matmul(bank(b, j % 2 * T, T), ck("hsel", j * P, P, 2 * QKT), rstd[0:2 * QKT, :],
                                             start=True, stop=True)
                            if j % 2 or j == QKT - 1:
                                last.then_inc(bc_ready, d.inc(bc_ready))

                def partners(tiles, b):
                    for j in tiles:
                        last = pe.matmul(bank(b, j % 2 * T, T), ck("perm", 0, P), a1("qk", j * T, T), start=True, stop=True)
                    last.then_inc(pm_ready, d.inc(pm_ready))

                pe.wait_ge(qr_ready, d.next(qr_ready))
                spread(range(8))
                for _ in range(RING):
                    linear_unit(h_hi, h_lo, free=gate_free)
                pe.wait_ge(qn_ready, d.next(qn_ready, 8))
                spread(range(8, QKT))
                partners((4, 5), 2)
                partners((6, 7), 3)
                pe.wait_ge(qn_ready, d.next(qn_ready, QKT - 8))
                partners((8, 9), 0)
                partners((10,), 1)
                for _ in range(RING):
                    linear_unit(h_hi, h_lo, free=gate_free)
                pe.wait_ge(rope_ready, d.next(rope_ready, QKT - 4))
                scores(0)
                pe.wait_ge(conv_ready, d.next(conv_ready))
                for k in range(2):
                    last = pe.matmul(bank(1, 0, T), ones256, a1("conv", k * T, T), start=(k == 0), stop=(k == 1))
                last.then_inc(mean_ready, d.inc(mean_ready))
                for _ in range(2):
                    linear_unit(h_hi, h_lo, free=gate_free)
                pe.wait_ge(sq_ready, d.next(sq_ready))
                for k in range(2):
                    last = pe.matmul(bank(1, T, T), ones256, a1("sg", k * T, T), start=(k == 0), stop=(k == 1))
                last.then_inc(stat_ready, d.inc(stat_ready))
                for _ in range(2):
                    linear_unit(h_hi, h_lo, free=gate_free)
                attend(0)
                for p in range(1, len(PIECES)):
                    for _ in range(BESIDE[p]):
                        linear_unit(h_hi, h_lo)
                    attend(p)
                pe.wait_ge(yhi_ready, d.next(yhi_ready))
                pe.wait_ge(ylo_ready, d.next(ylo_ready))

                def branch_unit():
                    s = unit()
                    pe.wait_ge(slot_free, d.next(slot_free, 2))
                    pair = [next_slot(), next_slot()]
                    for n in range(NG1):
                        o = bank(4 + pair[n // 2], n % 2 * T, T)
                        for c in (2 * n, 2 * n + 1):
                            last = mm3(o, blocks_of(w_hi[s], c), blocks_of(w_lo[s], c), chunk(y_hi, c), chunk(y_lo, c),
                                       c == 2 * n, c == 2 * n + 1)
                    last.then_inc(unit_done, d.inc(unit_done))

                zero_acc()
                branch_unit()
                branch_unit()
                with d.loop((CH - 2) // 2) as _:
                    for b in range(2):
                        branch_unit()
                        acc_unit(b)
                acc_unit(0)
                acc_unit(1, final=True)
                norm_stats()
                linear_unit(h_hi, h_lo, hlo_ready)
                zero_acc()
                for _ in range(3):
                    linear_unit(h_hi, h_lo)
                with d.loop((FF1 - 2) // RING) as _:
                    for jj in range(RING):
                        linear_unit(h_hi, h_lo)
                        linear_unit(h_hi, h_lo)
                        acc_unit(jj % 2)
                acc_unit(0)
                acc_unit(1, PAD1, final=True)

            norm_stats()
            linear_unit(h_hi, h_lo, hlo_ready)
            for _ in range(3):
                linear_unit(h_hi, h_lo)

            def linear_units(n, src_hi=h_hi, src_lo=h_lo):
                with d.loop(n // RING) as _:
                    for _ in range(RING):
                        linear_unit(src_hi, src_lo)

            linear_units(CH - RING)
            linear_unit(h_hi, h_lo)
            linear_units(SSD_T)
            y1_hi, y1_lo = y_hi[:, CH * T:2 * CH * T], y_lo[:, CH * T:2 * CH * T]
            pe.wait_ge(acs_ready, d.next(acs_ready))
            for n in range(2):
                for half in range(2):
                    last = pe.transpose(bank(0, (2 * n + half) * HEADS, HEADS), a2("dt", n * T + half * P, P, HEADS), ident[0:HEADS, 0:HEADS])
            last.then_inc(turn_ready, d.inc(turn_ready))
            pe.wait_ge(ylo2_ready, d.next(ylo2_ready, CH))
            for b in range(4):
                s = unit()
                for k in range(4):
                    o = slot(next_slot())
                    pe.wait_ge(slot_free, d.next(slot_free))
                    for c in range(2):
                        last = mm3(o, blocks_of(w_hi[s], 2 * k + c), blocks_of(w_lo[s], 2 * k + c),
                                   chunk(y1_hi, 2 * b + c), chunk(y1_lo, 2 * b + c), c == 0, c == 1)
                    if k < 3:
                        last.then_inc(gate_done, d.inc(gate_done))
                last.then_inc(unit_done, d.inc(unit_done))
                linear_unit(h_hi, h_lo)
            for _ in range(RING):
                linear_unit(h_hi, h_lo)
            pe.wait_ge(silu_ready, d.next(silu_ready, SSD_T))
            for c in range(CH):
                if c == 6:
                    pe.wait_ge(xdt_ready, d.next(xdt_ready, 1))
                for half in range(2):
                    last = pe.transpose(bank([1, 2, 3, 0][c // 2], (c % 2 * 2 + half) * P, P), a2("xbc", c * T + half * P, P), ident)
                if c % 2:
                    last.then_inc(xt_ready, d.inc(xt_ready))
            for _ in range(2):
                linear_unit(h_hi, h_lo)
            pe.wait_ge(xdt_ready, d.next(xdt_ready, 4))
            for g in range(GROUPS):
                bt, ct = CH + g, CH + GROUPS + g
                pe.matmul(bank(1 + g, 0, T), a2("xbc", bt * T, P), a2("xbc", ct * T, T), start=True, stop=True)
                last = pe.matmul(bank(1 + g, T, P), a2("xbc", bt * T + P, P), a2("xbc", ct * T + P, P), start=True, stop=True)
                last.then_inc(cb_ready, d.inc(cb_ready))

            def gated_branch():
                linear_unit(h_hi, h_lo)
                pe.wait_ge(ylo2_ready, d.next(ylo2_ready, CH))
                linear_unit(y_hi, y_lo)
                linear_unit(h_hi, h_lo)
                linear_unit(y_hi, y_lo)
                with d.loop((CH - 2) // 2) as _:
                    for _ in range(2):
                        linear_unit(h_hi, h_lo)
                        linear_unit(y_hi, y_lo)

            for _ in range(2):
                linear_unit(h_hi, h_lo)
            linear_units(CH - RING)
            gated_branch()
            pe.wait_ge(cbm_ready, d.next(cbm_ready, GROUPS))
            pe.wait_ge(consts2_full, d.next(consts2_full))

            def segments(k):
                for e in range(2):
                    last = pe.matmul(bank(k % 2, e * T, T), c2("sel", (2 * k + e) * P, P, HEADS), a2("dt", T, T, HEADS),
                                     start=True, stop=True)
                last.then_inc(seg_bc, d.inc(seg_bc))

            def ssd_heads(k):
                b = 2 + k % 2
                if k >= 2:
                    pe.wait_ge(ys_ready, d.next(ys_ready))
                for h in (2 * k, 2 * k + 1):
                    lo = h % 2 * HD
                    pe.wait_ge(m_ready, d.next(m_ready))
                    pe.matmul(psum[lo:lo + HD, b * 512:b * 512 + T], a2("xdt", h * HD, HD), seg(h)[:, 0:T], start=True, stop=False)
                    last = pe.matmul(psum[lo:lo + HD, b * 512 + P:b * 512 + T], a2("xdt", D + h * HD, HD), seg(h)[:, T:W15], start=False, stop=True)
                last.then_inc(yh_ready, d.inc(yh_ready))

            segments(0)
            for k in range(CH + 1):
                if k < CH:
                    value_part(k % 2)
                if k + 1 < CH:
                    if k:
                        pe.wait_ge(seg_ready, d.next(seg_ready, 2))
                    segments(k + 1)
                if k == CH:
                    linear_unit(h_hi, h_lo)
                if k:
                    ssd_heads(k - 1)
            pe.wait_ge(seg_ready, d.next(seg_ready, 4))
            pe.wait_ge(ys_ready, d.next(ys_ready, 2))

            def ssd_stat(c):
                pe.wait_ge(sq_ready, d.next(sq_ready))
                return pe.matmul(bank(0, 0, T), ones, a2("seg", c % 4 * T, T), start=(c == 0), stop=(c == CH - 1))

            for c in range(CH):
                if c:
                    linear_unit(h_hi, h_lo)
                if c >= 2:
                    ssd_stat(c - 2)
                if c >= 3:
                    pe.wait_ge(rot_ready, d.next(rot_ready))
                pe.matmul(bank(1 + c % 3, 0, T), c2("perm", 0, P), a2("qk", c * T, T), start=True, stop=True)\
                    .then_inc(pm2_ready, d.inc(pm2_ready))

            def ret_scores(h):
                kt, qt = RET_H + h, h
                pe.matmul(bank(1, 0, T), a2("qk", kt * T, P), a2("qk", qt * T, T), start=True, stop=True)
                pe.matmul(bank(1, T, P), a2("qk", kt * T + P, P), a2("qk", qt * T + P, P), start=True, stop=True)\
                    .then_inc(rs_ready, d.inc(rs_ready))

            def ret_outputs(h):
                pe.wait_ge(rp_ready, d.next(rp_ready))
                pr = ar("p", h % 2 * W15, W15)
                for e in range(2):
                    cv = h * 2 * P + e * P
                    pe.matmul(bank(2, e * T, T), ar("v", cv, P), pr[:, 0:T], start=True, stop=False)
                    last = pe.matmul(bank(2, e * T + P, P), ar("v", D + cv, P), pr[:, T:W15], start=False, stop=True)
                last.then_inc(ry_ready, d.inc(ry_ready))

            def ret_stat(h):
                pe.wait_ge(rsq_ready, d.next(rsq_ready))
                for e in range(2):
                    last = pe.matmul(psum[0:RET_H, 3 * 512:3 * 512 + T], c2("hot", h * RET_H, RET_H),
                                     a2("seg", (h % 2 * 2 + e) * T, T), start=(h == 0 and e == 0), stop=(h == RET_H - 1 and e == 1))
                return last

            for h in range(RET_H):
                linear_unit(h_hi, h_lo)
                if h == 0:
                    ssd_stat(CH - 2)
                    ssd_stat(CH - 1).then_inc(stat_ready, d.inc(stat_ready))
                linear_unit(h_hi, h_lo)
                if h >= 2:
                    ret_stat(h - 2)
                if h:
                    ret_outputs(h - 1)
                else:
                    pe.wait_ge(rot_ready, d.next(rot_ready, 3))
                ret_scores(h)
            ret_stat(RET_H - 2)
            ret_outputs(RET_H - 1)
            linear_unit(h_hi, h_lo)
            ret_stat(RET_H - 1).then_inc(rstat_ready, d.inc(rstat_ready))
            pe.wait_ge(ylo2_ready, d.next(ylo2_ready, 4))
            linear_unit(y1_hi, y1_lo)
            linear_unit(h_hi, h_lo)
            linear_unit(y1_hi, y1_lo)
            pe.wait_ge(rrow_ready, d.next(rrow_ready))
            for h in range(RET_H):
                last = pe.matmul(bank(1 + h // 2, h % 2 * T, T), c2("sel", h * P, P, RET_H), rstd[0:RET_H, :], start=True, stop=True)
                if h % 2:
                    last.then_inc(rbc_ready, d.inc(rbc_ready))
            with d.loop(3) as _:
                for _ in range(2):
                    linear_unit(h_hi, h_lo)
                    linear_unit(y1_hi, y1_lo)
            gated_branch()
            pe.wait_ge(rn_ready, d.next(rn_ready, RET_H))
            zero_acc()
            for c in range(CH):
                s = unit()
                pe.wait_ge(ylo2_ready, d.next(ylo2_ready))
                for f in range(CH):
                    last = mm3(acc(f), blocks_of(w_hi[s], f), blocks_of(w_lo[s], f), chunk(y1_hi, c), chunk(y1_lo, c),
                               False, f == CH - 1, skip_group_check=True)
                    if c == CH - 1 and f in (1, 3, 5):
                        last.then_inc(acc_done, d.inc(acc_done))
                last.then_inc(unit_done, d.inc(unit_done))
            norm_stats()
            linear_unit(h_hi, h_lo, hlo_ready)
            zero_acc()
            for _ in range(3):
                linear_unit(h_hi, h_lo)
            with d.loop((FF2 - 2) // RING) as _:
                for jj in range(RING):
                    linear_unit(h_hi, h_lo)
                    linear_unit(h_hi, h_lo)
                    acc_unit(jj % 2)
            for jj in range((FF2 - 2) % RING):
                linear_unit(h_hi, h_lo)
                linear_unit(h_hi, h_lo)
                acc_unit(jj % 2)
            acc_unit(0)
            acc_unit(1, final=True)
            norm_stats(0)

        @block.vector
        def _(dve):
            d = Desk(dve, "dve", per_trip, found)

            def norm(gain, new_params=False):
                dve.wait_ge(sd_ready, d.next(sd_ready))
                dve.reciprocal(rstd[:, :], rows[:, :]).then_inc(vec, d.inc(vec))
                if new_params:
                    dve.wait_ge(params_full, d.next(params_full))
                dve.wait_ge(d.last, d.made(d.last))
                for q in range(6):
                    if q < 4:
                        for c in (2 * q, 2 * q + 1):
                            dve.scalar_tensor_tensor(chunk(arena, c), chunk(x, c), prm[:, gain + c:gain + c + 1], rstd[:, :], ALU.mult, ALU.mult)\
                                .then_inc(hf_ready if c % 2 else vec, d.inc(hf_ready if c % 2 else vec))
                    if q >= 2:
                        dve.wait_ge(hhi_ready, d.next(hhi_ready))
                        dve.tensor_tensor(chunk(h_lo, 2 * q - 4, 2), chunk(arena, 2 * q - 4, 2), chunk(h_hi, 2 * q - 4, 2).bitcast(F32), ALU.subtract)\
                            .then_inc(hlo_ready, d.inc(hlo_ready))

            def residual():
                for q in range(4):
                    if q < 3:
                        dve.wait_ge(acc_done, d.next(acc_done))
                    else:
                        dve.wait_ge(unit_done, d.next(unit_done))
                    dve.tensor_tensor(chunk(x, 2 * q, 2), chunk(x, 2 * q, 2), bank(q), ALU.add)\
                        .then_inc(x_ready, d.inc(x_ready))

            def feed_low(b):
                dve.wait_ge(fhi_ready, d.next(fhi_ready))
                dve.tensor_tensor(chunk(f_lo, b), chunk(mixf, b), chunk(f_hi, b).bitcast(F32), ALU.subtract)\
                    .then_inc(flo_ready, d.inc(flo_ready))

            def conv_taps(first, n):
                with d.loop(n) as i:
                    for k in range(2):
                        dve.wait_ge(vec, d.made(vec, 1))
                        dve.scalar_tensor_tensor(a1("conv", k * T, T), arena[:, bass.ds(i + (A1["u"] + k * (T + TAPS - 1) + first), T)], prm[:, bass.ds(i + (P1["conv_w"] + k * TAPS + first), 1)], a1("conv", k * T, T), ALU.mult, ALU.add)\
                            .then_inc(vec, d.inc(vec))

            def tap(i):
                for k in range(2):
                    dve.wait_ge(vec, d.made(vec, 1))
                    u = k * (T + TAPS - 1) + i
                    w = P1["conv_w"] + k * TAPS + i
                    dve.scalar_tensor_tensor(a1("conv", k * T, T), a1("u", u, T), prm[:, w:w + 1], a1("conv", k * T, T), ALU.mult, ALU.add)\
                        .then_inc(vec, d.inc(vec))

            gate_tiles = [0]

            def gates(n):
                for _ in range(n):
                    g = gate_tiles[0]
                    gate_tiles[0] += 1
                    dve.wait_ge(unit_done, d.next(unit_done))
                    dve.tensor_scalar(a1("gates", g * T, T), slot((UNITS_BEFORE + g) % RING), prm[:, P1["gate_b"] + g:P1["gate_b"] + g + 1], None, ALU.add)\
                        .then_inc(slot_free, d.inc(slot_free))

            def softmax_scores(p):
                q_tile = PIECES[p][0]
                for h in range(2):
                    sc = a1("sc", (2 * (p % 2) + h) * 512, 512)
                    c = 8 * h
                    if p < 2:
                        bias = a1("bias", (2 * p + h) * 512, 512)
                    else:
                        bias = ck("dil" if p < 4 else "swa", 0, 512)
                    dve.wait_ge(s_ready, d.next(s_ready))
                    dve.scalar_tensor_tensor(sc, bank(2 + h), SCALE, bias, ALU.mult, ALU.add)\
                        .then_inc(s_free, d.inc(s_free))
                    dve.wait_ge(d.last, d.made(d.last))
                    dve.reduce_max(small[:, c:c + 2], sc.rearrange("p (r k) -> p r k", r=2), AX)\
                        .then_inc(vec, d.inc(vec))
                    dve.wait_ge(d.last, d.made(d.last))
                    if q_tile >= SWA_TILE:
                        head = q_tile - SWA_TILE + 2 * h
                        dve.tensor_scalar(small[:, c + 2:c + 4], small[:, c:c + 2], prm[:, P1["sink"] + head:P1["sink"] + head + 1], -1.0, ALU.max, ALU.mult)\
                            .then_inc(negm_ready, d.inc(negm_ready))
                    else:
                        dve.tensor_scalar(small[:, c + 2:c + 4], small[:, c:c + 2], -1.0, None, ALU.mult)\
                            .then_inc(negm_ready, d.inc(negm_ready))

            def softmax_norm(p):
                q_tile = PIECES[p][0]
                for h in range(2):
                    sc = a1("sc", (2 * (p % 2) + h) * 512, 512)
                    c = 8 * h
                    dve.wait_ge(exp_ready, d.next(exp_ready))
                    if q_tile >= SWA_TILE:
                        dve.tensor_tensor(small[:, c + 4:c + 6], small[:, c + 4:c + 6], small[:, c + 6:c + 8], ALU.add)\
                            .then_inc(vec, d.inc(vec))
                        dve.wait_ge(d.last, d.made(d.last))
                    dve.reciprocal(small[:, c + 4:c + 6], small[:, c + 4:c + 6]).then_inc(vec, d.inc(vec))
                    dve.wait_ge(d.last, d.made(d.last))
                    for r in range(2):
                        dve.tensor_scalar(sc[:, r * T:(r + 1) * T], sc[:, r * T:(r + 1) * T], small[:, c + 4 + r:c + 5 + r], None, ALU.mult)\
                            .then_inc(p_ready if r else vec, d.inc(p_ready if r else vec))

            def y_low(p):
                dve.wait_ge(yhi_ready, d.next(yhi_ready))
                cy = PIECES[p][4]
                dve.tensor_tensor(chunk(y_lo, cy), bank(0, 0, T), chunk(y_hi, cy).bitcast(F32), ALU.subtract)\
                    .then_inc(ylo_ready, d.inc(ylo_ready))

            dve.memset(zero[:, :].bitcast(F32), 0.0).then_inc(vec, d.inc(vec))
            dve.memset(a1("u", 0, 2 * (T + TAPS - 1)), 0.0).then_inc(vec, d.inc(vec))
            dve.memset(small[:, 60:61], EPS).then_inc(init, d.inc(init))
            dve.sem_inc(slot_free, RING)
            for q in range(4):
                dve.wait_ge(x_in[q], d.next(x_in[q]))
                dve.sem_inc(x_ready, 1)
            d.skip(x_ready, 4, "made")
            d.skip(slot_free, RING, "made")
            d.skip(unit_done, RING)
            with d.loop(DEPTH) as _:
                gate_tiles[0] = EARLY
                norm(P1["g_mix"], new_params=True)
                for k in range(2):
                    dve.wait_ge(sg_ready, d.next(sg_ready))
                    lo = k * (T + TAPS - 1) + TAPS // 2
                    dve.tensor_tensor(a1("u", lo, T), slot(k), a1("sg", k * T, T), ALU.mult)\
                        .then_inc(slot_free if k else vec, d.inc(slot_free if k else vec, RING if k else 1))
                dve.wait_ge(slot_free, d.made(slot_free))
                for k in range(2):
                    dve.tensor_scalar(a1("conv", k * T, T), a1("u", k * (T + TAPS - 1), T), prm[:, P1["conv_w"] + k * TAPS:P1["conv_w"] + k * TAPS + 1], prm[:, P1["conv_b"] + k:P1["conv_b"] + k + 1], ALU.mult, ALU.add)\
                        .then_inc(vec, d.inc(vec))
                d.skip(unit_done, RING)
                for j in range(QKT):
                    dve.wait_ge(unit_done, d.next(unit_done))
                    dve.wait_ge(qsq_ready, d.next(qsq_ready))
                    dve.tensor_copy(a1("qk", j * T, T), slot(j % RING)).then_inc(slot_free, d.inc(slot_free))
                    tap(1 + j)
                for j in range(0, VT - 1, 2):
                    dve.wait_ge(unit_done, d.next(unit_done, 2))
                    for half in range(2):
                        dve.tensor_copy(a1("v", (half * VT + j) * P, 2 * P), slot((QKT + j + half) % RING))\
                            .then_inc(slot_free, d.inc(slot_free))
                    tap(1 + QKT + j)
                    tap(2 + QKT + j)
                dve.wait_ge(unit_done, d.next(unit_done))
                v = a1("v", 0, 2 * VT * P).rearrange("p (h c) -> p h c", h=2)[:, :, (VT - 1) * P:VT * P]
                dve.tensor_copy(v, slot((QKT + VT - 1) % RING).rearrange("p (h c) -> p h c", h=2))\
                    .then_inc(slot_free, d.inc(slot_free))
                d.skip(unit_done, EARLY)
                dve.wait_ge(sd_ready, d.next(sd_ready))
                dve.reciprocal(rstd[0:2 * QKT, :], rows[0:2 * QKT, :]).then_inc(qr_ready, d.inc(qr_ready))
                conv_taps(QKT + VT, 6)

                def normalise(j):
                    if j % 2 == 0:
                        dve.wait_ge(bc_ready, d.next(bc_ready))
                    dve.scalar_tensor_tensor(a1("qk", j * T, T), a1("qk", j * T, T), prm[:, P1["qk_g"] + j:P1["qk_g"] + j + 1], bank(j % 8 // 2, j % 2 * T, T), ALU.mult, ALU.mult)\
                        .then_inc(qn_ready, d.inc(qn_ready))

                for j in range(8):
                    normalise(j)
                conv_taps(QKT + VT + 6, 4)
                for j in range(8, QKT):
                    normalise(j)
                dve.wait_ge(consts1_full, 16)
                for n, j in enumerate(range(4, QKT)):
                    if j % 2 == 0:
                        dve.wait_ge(pm_ready, d.next(pm_ready))
                    tmp = a1("pts", n % 2 * T, T)
                    dve.tensor_tensor(a1("qk", j * T, T), a1("qk", j * T, T), ck("cos", 0, T), ALU.mult)\
                        .then_inc(vec, d.inc(vec))
                    dve.tensor_tensor(tmp, bank([2, 3, 0, 1][n // 2], j % 2 * T, T), ck("sin", 0, T), ALU.mult)\
                        .then_inc(vec, d.inc(vec))
                    dve.wait_ge(d.last, d.made(d.last))
                    dve.tensor_tensor(a1("qk", j * T, T), a1("qk", j * T, T), tmp, ALU.add)\
                        .then_inc(rope_ready, d.inc(rope_ready))
                conv_taps(QKT + VT + 10, TAPS - 1 - (QKT + VT + 10))
                dve.wait_ge(vec, d.made(vec, 1))
                for k in range(2):
                    dve.scalar_tensor_tensor(a1("conv", k * T, T), a1("u", k * (T + TAPS - 1) + TAPS - 1, T), prm[:, P1["conv_w"] + (k + 1) * TAPS - 1:P1["conv_w"] + (k + 1) * TAPS], a1("conv", k * T, T), ALU.mult, ALU.add)\
                        .then_inc(conv_ready if k else vec, d.inc(conv_ready if k else vec))
                    if k == 0:
                        dve.wait_ge(vec, d.made(vec, 1))
                dve.wait_ge(bias_full, d.next(bias_full))
                softmax_scores(0)
                dve.wait_ge(mean_ready, d.next(mean_ready))
                for k in range(2):
                    dve.tensor_tensor(a1("conv", k * T, T), a1("conv", k * T, T), bank(1, 0, T), ALU.subtract)\
                        .then_inc(hf_ready if k else vec, d.inc(hf_ready if k else vec))
                softmax_norm(0)
                gates(2)
                dve.wait_ge(sd_ready, d.next(sd_ready))
                dve.reciprocal(rstd[:, :], rows[:, :]).then_inc(vec, d.inc(vec))
                dve.wait_ge(d.last, d.made(d.last))
                for k in range(2):
                    dve.scalar_tensor_tensor(a1("conv", k * T, T), a1("conv", k * T, T), prm[:, P1["ln_g"] + k:P1["ln_g"] + k + 1], rstd[:, :], ALU.mult, ALU.mult)\
                        .then_inc(hf_ready, d.inc(hf_ready))
                gates(BESIDE[0] - 2)
                dve.wait_ge(yhi_ready, d.next(yhi_ready))
                dve.tensor_tensor(chunk(y_lo, 0, 2), a1("sg", 0, 2 * T), chunk(y_hi, 0, 2).bitcast(F32), ALU.subtract)\
                    .then_inc(ylo_ready, d.inc(ylo_ready))
                softmax_scores(1)
                y_low(0)
                for p in range(1, len(PIECES)):
                    more = p < len(PIECES) - 1
                    gates(2)
                    softmax_norm(p)
                    gates(BESIDE[p] - 2)
                    if more:
                        softmax_scores(p + 1)
                    y_low(p)
                dve.wait_ge(gate_free, d.next(gate_free, EARLY))

                def mix(c, b):
                    dve.wait_ge(unit_done, d.next(unit_done))
                    if c >= EARLY // 4:
                        dve.wait_ge(gsig_ready, d.next(gsig_ready))
                    prod = a1("sc", 0, 4 * T)
                    gat = a1("gates", c * 4 * T, 4 * T)
                    dve.tensor_tensor(prod, psum[:, (4 + 2 * b) * 512:(4 + 2 * b) * 512 + 4 * T], gat, ALU.mult)\
                        .then_inc(slot_free, d.inc(slot_free, 2))
                    dve.wait_ge(d.last, d.made(d.last))
                    half = a1("sc", 4 * T, 2 * T)
                    dve.tensor_tensor(half, prod[:, 0:2 * T], prod[:, 2 * T:4 * T], ALU.add)\
                        .then_inc(vec, d.inc(vec))
                    dve.wait_ge(d.last, d.made(d.last))
                    dve.tensor_tensor(chunk(mixf, b), half[:, 0:T], half[:, T:2 * T], ALU.add)\
                        .then_inc(mixf_ready, d.inc(mixf_ready))
                    feed_low(b)

                for c in range(CH):
                    mix(c, c % 2)
                    if c >= 2:
                        d.skip(unit_done, 1)
                d.skip(unit_done, 1)
                residual()
                norm(P1["g_ffn"])

                def ffn(j, b):
                    at = (lambda k, o: prm[:, bass.ds(j * 8 + (P1["ffn"] + 4 * k + o), 1)])
                    buf = [pre[:, (2 * b + k) * T:(2 * b + k + 1) * T] for k in range(2)]
                    for k in range(2):
                        dve.wait_ge(pre_ready, d.next(pre_ready))
                        dve.scalar_tensor_tensor(buf[k][:, 1:T], slot(2 * b + k)[:, 0:T - 1], at(k, 0), buf[k][:, 1:T], ALU.mult, ALU.add)\
                            .then_inc(vec, d.inc(vec))
                    for k in range(2):
                        dve.wait_ge(vec, d.made(vec, 1 - k))
                        dve.scalar_tensor_tensor(buf[k][:, 0:T - 1], slot(2 * b + k)[:, 1:T], at(k, 2), buf[k][:, 0:T - 1], ALU.mult, ALU.add)\
                            .then_inc(slot_free if k else cg_ready, d.inc(slot_free if k else cg_ready, 2 if k else 1))
                    dve.wait_ge(d.last, d.made(d.last))
                    dve.wait_ge(sil_ready, d.next(sil_ready))
                    dve.tensor_tensor(chunk(mixf, b), buf[0], buf[1], ALU.mult)\
                        .then_inc(mixf_ready, d.inc(mixf_ready))
                    feed_low(b)

                for j in range(2):
                    ffn(j, j)
                d.skip(unit_done, 4)
                with d.loop((FF1 - 2) // RING) as i:
                    for jj in range(RING):
                        ffn(i * RING + (2 + jj), jj % 2)
                        d.skip(unit_done, 3)
                d.skip(unit_done, 1)
                residual()
                d.skip(unit_done, PAD1)

            slots = [0]

            def next_slot():
                slots[0] += 1
                return (slots[0] - 1) % RING

            def take():
                dve.wait_ge(unit_done, d.next(unit_done))
                return next_slot()

            def shifted_taps(dst, s, name, c, per, taps, final):
                dve.wait_ge(pre_ready, d.next(pre_ready))
                for k in range(1, taps):
                    if k > 1:
                        dve.wait_ge(d.last, d.made(d.last))
                    dve.scalar_tensor_tensor(dst[:, k:T], slot(s)[:, 0:T - k], p2(name, c * per + (taps - 1 - k)), dst[:, k:T], ALU.mult, ALU.add)\
                        .then_inc(final if k == taps - 1 else vec, d.inc(final if k == taps - 1 else vec))

            def release(k=1):
                dve.wait_ge(slot_free, d.made(slot_free))
                dve.memset(small[:, 59:60], 0.0).then_inc(slot_free, d.inc(slot_free, k))

            def softplus_start(src, work):
                e, s, q = work
                dve.scalar_tensor_tensor(e, src, -1.0, src, ALU.mult, ALU.min).then_inc(soft_in, d.inc(soft_in))
                dve.tensor_scalar(src, src, 0.0, None, ALU.max).then_inc(vec, d.inc(vec))
                dve.wait_ge(soft_exp, d.next(soft_exp))
                dve.tensor_scalar(s, e, 2.0, None, ALU.add).then_inc(vec, d.inc(vec))
                dve.wait_ge(d.last, d.made(d.last))
                dve.reciprocal(s, s).then_inc(vec, d.inc(vec))
                dve.wait_ge(d.last, d.made(d.last))
                dve.tensor_tensor(s, s, e, ALU.mult).then_inc(vec, d.inc(vec))
                dve.wait_ge(d.last, d.made(d.last))
                dve.tensor_tensor(q, s, s, ALU.mult).then_inc(vec, d.inc(vec))

            def softplus_end(dst, src, work):
                e, s, q = work
                dve.wait_ge(vec, d.made(vec))
                dve.tensor_scalar(e, q, 1.0 / 17, None, ALU.mult).then_inc(vec, d.inc(vec))
                for k in range(15, 1, -2):
                    dve.wait_ge(d.last, d.made(d.last))
                    dve.scalar_tensor_tensor(e, e, 1.0 / k, q, ALU.add, ALU.mult).then_inc(vec, d.inc(vec))
                dve.wait_ge(d.last, d.made(d.last))
                dve.scalar_tensor_tensor(e, e, 1.0, s, ALU.add, ALU.mult).then_inc(vec, d.inc(vec))
                dve.wait_ge(d.last, d.made(d.last))
                dve.scalar_tensor_tensor(dst, e, 2.0, src, ALU.mult, ALU.add).then_inc(vec, d.inc(vec))

            def parts_low(buf, c, src):
                dve.wait_ge(yhi2_ready, d.next(yhi2_ready))
                dve.tensor_tensor(chunk(y_lo, buf * CH + c), src, chunk(y_hi, buf * CH + c).bitcast(F32), ALU.subtract)\
                    .then_inc(ylo2_ready, d.inc(ylo2_ready))

            norm(P2["g_mix"], new_params=True)
            dve.tensor_scalar(small[:, 40:48], p2("lam", 0, CH), -1.0, None, ALU.mult).then_inc(vec, d.inc(vec))
            dve.wait_ge(d.last, d.made(d.last))
            work = (small[:, 16:24], small[:, 32:40], small[:, 48:56])
            softplus_start(small[:, 40:48], work)
            softplus_end(small[:, 24:32], small[:, 40:48], work)
            dve.wait_ge(d.last, d.made(d.last))
            dve.tensor_scalar(small[:, 32:40], small[:, 24:32], 8.0, None, ALU.mult).then_inc(vec, d.inc(vec))
            dve.tensor_scalar(small[:, 24:32], small[:, 24:32], -8.0, None, ALU.mult)\
                .then_inc(coef_ready, d.inc(coef_ready))
            for c in range(CH):
                s = take()
                shifted_taps(a2("xb", c * T, T), s, "lru_conv", c, 5, 4, conv_done)
                release()
                if c:
                    parts_low(1, c - 1, a2("xb", (c - 1) * T, T))
            parts_low(1, CH - 1, a2("xb", (CH - 1) * T, T))
            s = take()
            row = [a2("dt", 0, T, HEADS), rows[0:HEADS, :], rstd[0:HEADS, :], a2("dt", T, T, HEADS)]
            dve.tensor_scalar(row[0], slot(s)[0:HEADS, :], p2("dt_bias", 0, 1, HEADS), None, ALU.add)\
                .then_inc(slot_free, d.inc(slot_free))
            dve.wait_ge(d.last, d.made(d.last))
            softplus_start(row[0], row[1:])
            for c in range(SSD_T):
                s = take()
                shifted_taps(a2("xbc", c * T, T), s, "ssd_conv", c, 5, 4, conv_done)
                release()
                if c == 4:
                    softplus_end(row[0], row[0], row[1:])
                    dve.wait_ge(d.last, d.made(d.last))
                    dve.memset(row[1], 1.0).then_inc(vec, d.inc(vec))
                    dve.wait_ge(d.last, d.made(d.last))
                    dve.wait_ge(ea_ready, d.next(ea_ready))
                    dve.tensor_scalar(row[2], row[0], small[0:HEADS, 58:59], -1.0, ALU.mult, ALU.mult)\
                        .then_inc(vec, d.inc(vec))
                    dve.wait_ge(d.last, d.made(d.last))
                    dve.tensor_tensor_scan(row[3], row[1], row[2], 0.0, ALU.mult, ALU.add)\
                        .then_inc(acs_ready, d.inc(acs_ready))
            dve.wait_ge(turn_ready, d.next(turn_ready))
            dve.tensor_copy(a2("tab", 0, 4 * HEADS), bank(0, 0, 4 * HEADS)).then_inc(xdt_ready, d.inc(xdt_ready))
            for b in range(4):
                for _ in range(4):
                    dve.wait_ge(ri_ready, d.next(ri_ready))
                    release()
                    next_slot()
                d.skip(unit_done)
                dve.tensor_tensor(a2("i", 2 * b * T, 2 * T), a2("i", 2 * b * T, 2 * T), a2("xb", 2 * b * T, 2 * T), ALU.mult)\
                    .then_inc(conv_done, d.inc(conv_done))
                s = take()
                dve.tensor_copy(a2("qk", b * T, T), slot(s)).then_inc(slot_free, d.inc(slot_free))
            for c in range(CH):
                if c < RING:
                    s = take()
                    dve.tensor_copy(a2("qk", (RING + c) * T, T), slot(s)).then_inc(slot_free, d.inc(slot_free))
                dve.wait_ge(at_ready, d.next(at_ready))
                tmp = chunk(pre, c % 4)
                dve.tensor_tensor(tmp, a2("xb", c * T, T), a2("xb", c * T, T), ALU.mult).then_inc(vec, d.inc(vec))
                dve.wait_ge(d.last, d.made(d.last))
                dve.scalar_tensor_tensor(a2("r", c * T, T), tmp, 1.0, a2("r", c * T, T), ALU.add, ALU.mult)\
                    .then_inc(m2_ready if c % 2 else vec, d.inc(m2_ready if c % 2 else vec))
            dve.wait_ge(d.last, d.made(d.last))
            for n in range(4):
                dve.wait_ge(xt_ready, d.next(xt_ready))
                for half in range(2):
                    src = bank([1, 2, 3, 0][n]).rearrange("p (c s h f) -> p s c h f", c=2, s=2, h=2)[:, half]
                    out = a2("xdt", half * D + n * T, T).rearrange("p (c h f) -> p c h f", c=2, h=2)
                    dts = a2("tab", half * HEADS + 4 * n, 4).rearrange("p (c h f) -> p c h f", c=2, h=2)
                    dve.tensor_tensor(out, src, dts.to_broadcast([P, 2, 2, HD]), ALU.mult)\
                        .then_inc(xdt_ready if half else vec, d.inc(xdt_ready if half else vec))
            for q in range(4):
                dve.wait_ge(root_ready, d.next(root_ready))
                dve.tensor_tensor(a2("i", 2 * q * T, 2 * T), a2("i", 2 * q * T, 2 * T), a2("r", 2 * q * T, 2 * T), ALU.mult)\
                    .then_inc(vec, d.inc(vec))
                dve.wait_ge(d.last, d.made(d.last))
                for c in (2 * q, 2 * q + 1):
                    dve.tensor_tensor_scan(a2("r", c * T, T), a2("xb", c * T, T), a2("i", c * T, T), 0.0, ALU.mult, ALU.add)\
                        .then_inc(vec, d.inc(vec))
            dve.wait_ge(consts2_full, d.next(consts2_full))
            for g in range(GROUPS):
                dve.wait_ge(cb_ready, d.next(cb_ready))
                dve.tensor_tensor(a2("cb", g * W15, W15), bank(1 + g, 0, W15), c2("causal", 0, W15), ALU.mult)\
                    .then_inc(cbm_ready, d.inc(cbm_ready))
            dve.wait_ge(d.last, d.made(d.last))
            for c in range(CH):
                take()
                dve.wait_ge(act_out, d.next(act_out))
                if c >= 2:
                    dve.wait_ge(ylo2_ready, d.made(ylo2_ready))
                dve.tensor_tensor(chunk(mixf, c % 2), a2("r", c * T, T), chunk(pre, c % RING), ALU.mult)\
                    .then_inc(prod_ready, d.inc(prod_ready))
                release()
                if c:
                    parts_low(0, c - 1, chunk(mixf, (c - 1) % 2))
            parts_low(0, CH - 1, chunk(mixf, (CH - 1) % 2))
            with d.loop(CH // 2) as i:
                for k in range(2):
                    c = i * 2 + k
                    take()
                    s = take()
                    dve.wait_ge(act_out, d.next(act_out))
                    dve.tensor_tensor(a2("merged", c * T, T), slot(s), chunk(pre, k), ALU.mult)\
                        .then_inc(slot_free, d.inc(slot_free, 2))
            dve.wait_ge(slot_free, d.made(slot_free))
            for k in range(CH + 2):
                if k >= 2:
                    dve.wait_ge(yh_ready, d.next(yh_ready))
                    c = k - 2
                    dve.scalar_tensor_tensor(a2("xbc", c * T, T), a2("xbc", c * T, T), p2("ssd_d", c), bank(2 + c % 2, 0, T), ALU.mult, ALU.add)\
                        .then_inc(ys_ready, d.inc(ys_ready))
                if k < CH:
                    dve.wait_ge(seg_bc, d.next(seg_bc))
                    for e in range(2):
                        h = 2 * k + e
                        for half in range(2):
                            dve.tensor_scalar(seg(h)[:, half * T:half * T + T - half * P], bank(k % 2, e * T + half * P, T - half * P), a2("tab", (2 + half) * HEADS + h, 1), 0.0, ALU.subtract, ALU.min)\
                                .then_inc(seg_ready if half else vec, d.inc(seg_ready if half else vec))
                if 1 <= k <= CH:
                    for h in (2 * k - 2, 2 * k - 1):
                        dve.wait_ge(dec_ready, d.next(dec_ready))
                        dve.tensor_tensor(seg(h), seg(h), a2("cb", h // (HEADS // GROUPS) * W15, W15), ALU.mult)\
                            .then_inc(m_ready, d.inc(m_ready))
                if k % 2 and k < CH:
                    dve.wait_ge(unit_done, d.next(unit_done, 2))
                    for half in range(2):
                        dve.tensor_copy(ar("v", half * D + (k - 1) * P, 2 * P), slot(next_slot()))\
                            .then_inc(slot_free, d.inc(slot_free))
            dve.wait_ge(ys_ready, d.made(ys_ready))
            for c in range(CH):
                take()
                dve.wait_ge(act_out, d.next(act_out))
                dve.tensor_tensor(a2("xbc", c * T, T), a2("xbc", c * T, T), chunk(pre, (c + 2) % RING), ALU.mult)\
                    .then_inc(prod_ready, d.inc(prod_ready))
                release()
                dve.wait_ge(pm2_ready, d.next(pm2_ready))
                tmp = chunk(mixf, c % 2)
                dve.tensor_tensor(a2("qk", c * T, T), a2("qk", c * T, T), c2("cos", 0, T), ALU.mult)\
                    .then_inc(vec, d.inc(vec))
                dve.tensor_tensor(tmp, bank(1 + c % 3, 0, T), c2("sin", 0, T), ALU.mult)\
                    .then_inc(vec, d.inc(vec))
                dve.wait_ge(d.last, d.made(d.last))
                dve.tensor_tensor(a2("qk", c * T, T), a2("qk", c * T, T), tmp, ALU.add)\
                    .then_inc(rot_ready, d.inc(rot_ready))

            def ret_copy(h):
                dve.wait_ge(ry_ready, d.next(ry_ready))
                dve.tensor_copy(ar("y", 2 * h * T, 2 * T), bank(2)).then_inc(ryf_ready, d.inc(ryf_ready))

            for h in range(RET_H):
                for _ in range(2):
                    take()
                    dve.wait_ge(act_out, d.next(act_out))
                    release()
                if h:
                    ret_copy(h - 1)
                dve.wait_ge(rs_ready, d.next(rs_ready))
                dve.tensor_tensor(ar("p", h % 2 * W15, W15), bank(1, 0, W15), c2("decay", h * W15, W15), ALU.mult)\
                    .then_inc(rp_ready, d.inc(rp_ready))
                if h == 0:
                    dve.wait_ge(sd_ready, d.next(sd_ready))
                    dve.reciprocal(rstd[:, :], rows[:, :]).then_inc(vec, d.inc(vec))
                    dve.wait_ge(d.last, d.made(d.last))
                    for c in range(CH):
                        dve.scalar_tensor_tensor(a2("xbc", c * T, T), a2("xbc", c * T, T), p2("ssd_g", c), rstd[:, :], ALU.mult, ALU.mult)\
                            .then_inc(hf_ready if c % 2 else vec, d.inc(hf_ready if c % 2 else vec))
                if h in (1, 2):
                    for q in (2 * h - 2, 2 * h - 1):
                        dve.wait_ge(yhi2_ready, d.next(yhi2_ready))
                        dve.tensor_tensor(chunk(y_lo, CH + 2 * q, 2), a2("xbc", 2 * q * T, 2 * T), chunk(y_hi, CH + 2 * q, 2).bitcast(F32), ALU.subtract)\
                            .then_inc(ylo2_ready, d.inc(ylo2_ready))
            ret_copy(RET_H - 1)
            dve.wait_ge(rsd_ready, d.next(rsd_ready))
            dve.reciprocal(rstd[0:RET_H, :], rows[0:RET_H, :]).then_inc(rrow_ready, d.inc(rrow_ready))

            def gated_pair(c, final):
                take()
                s = take()
                dve.wait_ge(act_out, d.next(act_out))
                dve.tensor_tensor(chunk(mixf, c % 2), slot(s), chunk(pre, c % 2), ALU.mult)\
                    .then_inc(slot_free, d.inc(slot_free, 2))
                dve.wait_ge(d.last, d.made(d.last))
                dve.tensor_tensor(a2("merged", c * T, T), a2("merged", c * T, T), chunk(mixf, c % 2), ALU.add)\
                    .then_inc(merged_ready if final else vec, d.inc(merged_ready if final else vec))

            for c in range(CH):
                for y in RET_PARTS[c]:
                    h = y // 2
                    if y % 4 == 0:
                        dve.wait_ge(rbc_ready, d.next(rbc_ready))
                    dve.tensor_tensor(ar("y", y * T, T), ar("y", y * T, T), bank(1 + h // 2, h % 2 * T, T), ALU.mult)\
                        .then_inc(rn_ready if y % 2 else vec, d.inc(rn_ready if y % 2 else vec))
                    dve.wait_ge(d.last, d.made(d.last))
                    dve.tensor_tensor(ar("y", y * T, T), ar("y", y * T, T), a2("xdt", y * T, T), ALU.mult)\
                        .then_inc(prod_ready, d.inc(prod_ready))
                gated_pair(c, False)
                for y in RET_PARTS[c]:
                    parts_low(0, y, ar("y", y * T, T))
            for c in range(CH):
                gated_pair(c, True)
                if c:
                    parts_low(1, c - 1, a2("merged", (c - 1) * T, T))
            parts_low(1, CH - 1, a2("merged", (CH - 1) * T, T))
            d.skip(unit_done, CH - 1)
            residual()
            norm(P2["g_ffn"])

            def ffn2(j, b):
                s = take()
                shifted_taps(chunk(pre, b), s, "ffn", j, 4, 3, cg_ready)
                s = take()
                dve.wait_ge(sil_ready, d.next(sil_ready))
                dve.tensor_tensor(chunk(mixf, b), slot(s), chunk(pre, b), ALU.mult)\
                    .then_inc(mixf_ready, d.inc(mixf_ready))
                release(2)
                feed_low(b)

            for j in range(2):
                ffn2(j, j)
            with d.loop((FF2 - 2) // RING) as i:
                for jj in range(RING):
                    ffn2(i * RING + (2 + jj), jj % 2)
                    d.skip(unit_done)
            for jj in range((FF2 - 2) % RING):
                ffn2(FF2 - (FF2 - 2) % RING + jj, jj % 2)
                d.skip(unit_done)
            d.skip(unit_done)
            residual()
            dve.wait_ge(sd_ready, d.next(sd_ready))
            dve.reciprocal(rstd[:, :], rows[:, :]).then_inc(vec, d.inc(vec))
            dve.wait_ge(d.last, d.made(d.last))
            for c in range(CH):
                dve.scalar_tensor_tensor(chunk(arena, c), chunk(x, c), p2("g_out", c), rstd[:, :], ALU.mult, ALU.mult)\
                    .then_inc(result_ready, d.inc(result_ready))


def constants():
    q = np.arange(T)
    common = np.zeros((P, NK0), np.float32)
    common[:, K0["ident"]:K0["ident"] + P] = np.eye(P)
    common[:, K0["ones"]:K0["ones"] + P] = 1.0 / D
    common[:, K0["ones256"]:K0["ones256"] + P] = 1.0 / 256
    k1 = np.zeros((P, NK1), np.float32)
    part = np.arange(P)
    for j in range(QKT):
        for h in range(2):
            k1[h * HD:(h + 1) * HD, K1["hstat"] + j * 2 * QKT + 2 * j + h] = 1.0 / HD
            k1[2 * j + h, K1["hsel"] + j * P + h * HD:K1["hsel"] + j * P + (h + 1) * HD] = 1.0
    dim = part % HD
    partner = np.where(dim < 8, part + 8, np.where(dim < 16, part - 8, part))
    k1[partner, K1["perm"] + part] = 1.0
    inv = 500000.0 ** (-np.arange(0, 16, 2) / 16.0)
    ang = np.float32(q)[None, :] * np.float32(inv)[:, None]
    cos, sin = np.ones((P, T)), np.zeros((P, T))
    for p in range(P):
        if dim[p] < 16:
            cos[p] = np.cos(ang[dim[p] % 8])
            sin[p] = np.sin(ang[dim[p] % 8]) * (-1 if dim[p] < 8 else 1)
    k1[:, K1["cos"]:K1["cos"] + T] = cos
    k1[:, K1["sin"]:K1["sin"] + T] = sin
    diff = q[:, None] - q[None, :]
    count = sum(((diff % dil == 0) & (np.abs(diff) <= w // 2)).astype(int) for w, dil in ((128, 1), (512, 4), (2048, 16)))
    dil = np.where(count > 0, np.log(np.maximum(count, 1)), NEG)
    swa = np.where(np.abs(diff) <= 128, 0.0, NEG)
    for name, m in (("dil", dil), ("swa", swa)):
        k1[:, K1[name]:K1[name] + 2 * T] = m.reshape(2, P, T).transpose(1, 0, 2).reshape(P, 2 * T)
    return common, k1


def cols(w, order):
    w = w[:, order]
    return w.reshape(CH, P, -1, P).transpose(2, 1, 0, 3).reshape(-1, P, D)


def cols_by_two(w, order):
    w = w[:, order]
    return w.reshape(2, CH // 2, P, -1, 2 * P).transpose(3, 0, 2, 1, 4).reshape(-1, P, D)


def rows_of(w):
    return w.reshape(-1, P, D)


def per_part(v):
    return v.reshape(-1, P).T


def interleave(*parts):
    return np.stack(parts, 1).reshape(-1, *parts[0].shape[1:])


def lag2(pairs, acc):
    out = []
    for j in range(len(pairs)):
        out += list(pairs[j])
        if j >= 2:
            out.append(acc[j - 2])
    return out + [acc[-2], acc[-1]]


def block1_layout(a):
    units, params, bias = [], [], []
    dc = np.arange(64)
    start = np.clip(dc - 8, 0, 48)
    inside = (dc[None, :] >= start[:, None]) & (dc[None, :] < start[:, None] + 16)
    delta = np.clip(dc[None, :] - dc[:, None] + 15, 0, 30)
    r = np.arange(4)
    dr = r[None, :] - r[:, None] + 7
    swa_heads = np.concatenate([np.arange(64) + 64 * h for h in (0, 2, 1, 3)])
    for l in range(DEPTH):
        w = a["w_in"][l]
        o = np.cumsum([0, 4096, 512, 768, 768, 256, 256])
        gate_order = np.arange(4096).reshape(4, CH, P).transpose(1, 0, 2).ravel()
        na, dil, sq, kv = o[2], o[3], o[4], o[5]
        qk = np.concatenate([na + np.arange(512), dil + np.arange(512), sq + swa_heads, kv + np.arange(128)])
        v = np.concatenate([na + 512 + np.arange(256), dil + 512 + np.arange(256), kv + 128 + np.arange(128)])
        units += [cols(w, o[1] + np.arange(512)), cols(w, qk), cols_by_two(w, v[:-P]), cols(w, v[-P:]), cols(w, gate_order)]
        wb = a["w_branch"][l].copy().reshape(4, 256, D)
        wb[3] = wb[3][swa_heads]
        wb = wb.reshape(4 * 2, P, CH, P).transpose(2, 1, 0, 3).reshape(CH, P, D)
        wo = rows_of(a["w_out"][l])
        units.append(np.stack(lag2([(u,) for u in wb], wo)))
        up = cols(a["w_up"][l], np.arange(2 * 2816))
        down = rows_of(a["w_down"][l])
        units.append(np.stack(lag2([(up[j], up[FF1 + j]) for j in range(FF1)], down)))
        units.append(np.zeros((PAD1, P, D), np.float32))
        p = np.zeros((P, NP1), np.float32)

        def put(name, m):
            p[:, P1[name]:P1[name] + m.shape[1]] = m

        put("g_mix", per_part(a["g_mix"][l]))
        put("g_ffn", per_part(a["g_ffn"][l]))
        put("gate_b", per_part(a["gate_b"][l].reshape(-1)[gate_order]))
        cw = a["a_conv_w"][l]
        put("conv_w", np.concatenate([cw[:, :P].T, cw[:, P:].T], 1))
        put("conv_b", per_part(a["a_conv_b"][l]))
        put("ln_g", per_part(a["a_ln_g"][l]))
        put("ln_b", per_part(a["a_ln_b"][l]))
        gains = ["na_qn"] * 2 + ["na_kn"] * 2 + ["dil_qn"] * 2 + ["dil_kn"] * 2 + ["swa_qn"] * 2 + ["swa_kn"]
        put("qk_g", np.stack([np.tile(a[g][l], 2) for g in gains], 1))
        put("sink", np.broadcast_to(a["swa_sink"][l], (P, 4)))
        fw, fb = a["ffn_conv_w"][l].reshape(3, 2, FF1, P), a["ffn_conv_b"][l].reshape(2, FF1, P)
        ff = np.concatenate([fw, fb[None]], 0)
        put("ffn", ff.transpose(3, 2, 1, 0).reshape(P, FF1 * 8))
        params.append(p)
        b = a["na_rpb"][l][:, dr[:, :, None, None], delta[None, None, :, :]]
        b = np.where(inside[None, None, None], b, np.float32(NEG)).transpose(0, 1, 3, 2, 4).reshape(4, 2, P, T)
        bias.append(b.transpose(2, 0, 1, 3).reshape(P, 4 * 2 * T))
    return units, np.stack(params), np.stack(bias)


def constants2():
    k = np.zeros((P, NK2), np.float32)
    part, q = np.arange(P), np.arange(T)
    k[part ^ 1, K2["perm"] + part] = 1.0
    inv = np.float32(1.0) / (np.float32(10000.0) ** np.linspace(0.0, 1.0, 64, dtype=np.float32))
    ang = q.astype(np.float32)[None, :] * inv[part // 2][:, None]
    k[:, K2["cos"]:K2["cos"] + T] = np.cos(ang)
    k[:, K2["sin"]:K2["sin"] + T] = np.sin(ang) * np.where(part % 2, 1, -1)[:, None]
    back = np.concatenate([q[None, :] - part[:, None], (q[None, P:] - part[:, None] - P)], 1)
    k[:, K2["causal"]:K2["causal"] + W15] = back >= 0
    for h in range(RET_H):
        log_gamma = np.log(1.0 - 2.0 ** (-5.0 - h))
        k[:, K2["decay"] + h * W15:K2["decay"] + (h + 1) * W15] = np.where(back >= 0, np.exp(np.maximum(back, 0) * log_gamma), 0) * P ** -0.5
        k[:, K2["hot"] + h * RET_H + h] = 1.0 / (2 * P)
    for h in range(HEADS):
        k[h, K2["sel"] + h * P:K2["sel"] + (h + 1) * P] = 1.0
    return k


def block2_layout(a):
    w = a["w_in_2"][0]
    o = np.cumsum([0, 1024, 1536, 16, 1024, 1024, 512, 512, 1024, 1024, 3072])
    z, xbc, dt, ly, lx, qk, v, g, gates = (cols(w, np.arange(lo, hi)) for lo, hi in (
        (o[0], o[1]), (o[1], o[2]), (o[2], o[2] + P), (o[3], o[4]), (o[4], o[5]), (o[5], o[7]), (o[7], o[8]), (o[8], o[9]), (o[9], o[10])))
    lru = np.stack([a["lru_w_a_2"][0], a["lru_w_i_2"][0]], 1)
    lru = lru.reshape(4, 2, 2, P, 2, P).transpose(0, 3, 1, 4, 2, 5).reshape(4, P, D)
    v = cols_by_two(w, np.arange(o[7], o[8]))
    wb = [cols(m, np.arange(D)) for m in a["w_branch_2"][0]]
    gb = [interleave(gates[n * CH:(n + 1) * CH], wb[n]) for n in range(3)]
    wo = rows_of(a["w_o_2"][0])
    up = cols(a["ffn_w_in_2"][0], np.arange(2 * 3072))
    down = rows_of(a["ffn_w_out_2"][0])
    ff = np.stack(lag2([(up[j], up[FF2 + j]) for j in range(FF2)], down))
    units = [lx, dt, xbc, interleave(lru, qk[:4]), qk[4:], ly, gb[1], v, z, g, gb[0], gb[2], wo, ff]
    p = np.zeros((P, NP2), np.float32)

    def put(name, m):
        p[:m.shape[0], P2[name]:P2[name] + m.shape[1]] = m

    def taps(wc, b):
        return np.concatenate([wc, b[None]], 0).reshape(len(wc) + 1, -1, P).transpose(2, 1, 0).reshape(P, -1)

    put("g_mix", per_part(a["norm_mix_2"][0]))
    put("g_ffn", per_part(a["norm_ffn_2"][0]))
    put("g_out", per_part(a["norm_final_2"]))
    put("ssd_conv", taps(a["ssd_conv_w_2"][0], a["ssd_conv_b_2"][0]))
    put("dt_bias", a["ssd_dt_bias_2"][0][:, None])
    put("a_log", a["ssd_a_log_2"][0][:, None])
    put("ssd_d", per_part(np.repeat(a["ssd_d_2"][0], 64)))
    put("ssd_g", per_part(a["ssd_norm_2"][0]))
    put("lru_conv", taps(a["lru_conv_w_2"][0], a["lru_conv_b_2"][0]))
    put("b_a", per_part(a["lru_b_a_2"][0]))
    put("b_i", per_part(a["lru_b_i_2"][0]))
    put("lam", per_part(a["lru_lambda_2"][0]))
    put("ffn", taps(a["ffn_conv_w_2"][0], a["ffn_conv_b_2"][0]))
    return units, p


def kernel(**inputs):
    import concourse.bacc as bacc
    from concourse.bass_utils import run_bass_kernel_spmd as run

    a = {k: np.asarray(v) for k, v in inputs.items()}
    units, params1, bias1 = block1_layout(a)
    units2, params2 = block2_layout(a)
    units += units2
    common, k1 = constants()
    arrays = {"x": np.ascontiguousarray(a["x"][0].T), "units": np.ascontiguousarray(np.concatenate(units)),
              "params1": params1, "bias1": np.ascontiguousarray(bias1), "common": common, "consts1": k1, "params2": params2, "consts2": constants2()}

    def build(per_trip, found):
        nc = bacc.Bacc("TRN2", target_bir_lowering=False, num_devices=1)
        t = {n: nc.dram_tensor(f"in_{n}", v.shape, mybir.dt.from_np(v.dtype), kind="ExternalInput").ap()
             for n, v in arrays.items()}
        t["out"] = nc.dram_tensor("out", (D, T), F32, kind="ExternalOutput").ap()
        program(nc, t, per_trip, found)
        return nc

    per_trip = {}
    build({}, per_trip)
    nc = build(per_trip, {})
    r = run(nc, [{f"in_{n}": v for n, v in arrays.items()}], core_ids=[0])
    return r.results[0]["out"].T[None]
```
